# Optimizing a Trainium2 kernel written in Bass

```python
import math
import jax
import jax.numpy as jnp
from jax import lax
import numpy as np

D_MODEL = 1024
BATCH = 1
SEQ = 256
DEPTH = 2

CTX_LEN = 256
GRID_W = 64
EPS = 1e-6
CONV_CH = 512
CONV_GROUPS = 8
CONV_WIDTH = 31
FOURIER_CH = 512
FOURIER_GROUPS = 4
MIX_IN = 2 * CONV_CH + FOURIER_CH
MIX_OUT = CONV_CH + FOURIER_CH
DA_HEADS = 8
DA_QK_DIM = 64
DA_V_DIM = 2 * DA_QK_DIM
QK_W = DA_HEADS * 2 * DA_QK_DIM
V_W = DA_HEADS * DA_V_DIM
ROPE_BASE = 10000.0
Q_BLOCK = 128
N_EXPERTS = 64
TOP_K = 6
N_GROUPS = 8
TOPK_GROUPS = 4
EXPERT_FF = 256
SHARED_FF = 256
ROUTED_SCALE = 2.5
MOE_BLOCK = 128
N_EVEN = (DEPTH + 1) // 2
N_ODD = DEPTH // 2

kernel_name = 'hybrid_conv_fourier_diffattn_moe_dit'

def rms_norm(x, g):
    xf = x.astype(jnp.float32)
    y = xf * lax.rsqrt(jnp.mean(xf * xf, axis=-1, keepdims=True) + EPS)
    return (y * g.astype(jnp.float32)).astype(x.dtype)

def swiglu(x, w_gate, w_up, w_down):
    return (jax.nn.silu(x @ w_gate) * (x @ w_up)) @ w_down

def conv_fourier_mix(h, w_in, conv_w, conv_b, ln_g, ln_b, w_out):
    bn, seq_len, _ = h.shape
    u = h @ w_in
    a_val, a_gate, f = jnp.split(u, [CONV_CH, 2 * CONV_CH], axis=-1)
    a = a_val * jax.nn.sigmoid(a_gate)
    a = lax.conv_general_dilated(a, conv_w.astype(a.dtype), window_strides=(1,),
                                 padding=[(CONV_WIDTH // 2, CONV_WIDTH // 2)],
                                 dimension_numbers=('NWC', 'WIO', 'NWC'),
                                 feature_group_count=CONV_CH) + conv_b
    ag = a.reshape(bn, seq_len, CONV_GROUPS, -1).astype(jnp.float32)
    mu = jnp.mean(ag, axis=-1, keepdims=True)
    var = jnp.mean(jnp.square(ag - mu), axis=-1, keepdims=True)
    an = ((ag - mu) * lax.rsqrt(var + EPS)).reshape(bn, seq_len, CONV_CH)
    a = jax.nn.silu(an * ln_g.astype(jnp.float32) + ln_b.astype(jnp.float32)).astype(h.dtype)
    fg = f.reshape(bn, seq_len, FOURIER_GROUPS, -1).astype(jnp.float32)
    fr = jnp.fft.fft2(fg, axes=(1, 3), norm='ortho').real.reshape(bn, seq_len, FOURIER_CH).astype(h.dtype)
    return jnp.concatenate([a, fr], axis=-1) @ w_out

def axial_rope_tables(n_tokens):
    rows = n_tokens // GRID_W
    row = jnp.repeat(jnp.arange(rows), GRID_W).astype(jnp.float32)
    col = jnp.tile(jnp.arange(GRID_W), rows).astype(jnp.float32)
    n_freq = DA_QK_DIM // 4
    inv = jnp.power(ROPE_BASE, -jnp.arange(n_freq, dtype=jnp.float32) / n_freq)
    ang = jnp.concatenate([row[:, None] * inv, col[:, None] * inv], axis=-1)
    ang = jnp.concatenate([ang, ang], axis=-1)
    return jnp.cos(ang), jnp.sin(ang)

def apply_rope(x, cos, sin):
    half = DA_QK_DIM // 2
    xf = x.astype(jnp.float32)
    rot = jnp.concatenate([-xf[..., half:], xf[..., :half]], axis=-1)
    c = cos[:, None, None, :]
    s = sin[:, None, None, :]
    return (xf * c + rot * s).astype(x.dtype)

def da_queries(h, w_qkv):
    return (h @ w_qkv[:, :QK_W]).reshape(h.shape[0], h.shape[1], DA_HEADS, 2, DA_QK_DIM)

def da_keys_values(h, w_qkv):
    k, v = jnp.split(h @ w_qkv[:, QK_W:], [QK_W], axis=-1)
    return (k.reshape(h.shape[0], h.shape[1], DA_HEADS, 2, DA_QK_DIM),
            v.reshape(h.shape[0], h.shape[1], DA_HEADS, DA_V_DIM))

def diff_attention_core(q, k, v, lam):
    bn, lq = q.shape[0], q.shape[1]
    nb = lq // Q_BLOCK
    qb = jnp.moveaxis(q.reshape(bn, nb, Q_BLOCK, DA_HEADS, 2, DA_QK_DIM), 1, 0)
    scale = DA_QK_DIM ** -0.5

    def block(qi):
        s = jnp.einsum('bqhcd,bkhcd->bchqk', qi, k, preferred_element_type=jnp.float32) * scale
        p = jax.nn.softmax(s, axis=-1)
        pd = p[:, 0] - lam * p[:, 1]
        return jnp.einsum('bhqk,bkhe->bqhe', pd.astype(v.dtype), v,
                          preferred_element_type=jnp.float32).astype(v.dtype)

    o = lax.map(block, qb)
    return jnp.moveaxis(o, 0, 1).reshape(bn, lq, DA_HEADS, DA_V_DIM)

def diff_attn_out(o, subln_g, lam_init, w_out):
    o = rms_norm(o, subln_g) * (1.0 - lam_init)
    return o.reshape(o.shape[0], o.shape[1], V_W) @ w_out

def moe_ffn(h, router_w, router_b, w_gate, w_up, w_down, sh_gate, sh_up, sh_down):
    n_tok, dm = h.shape
    scores = jax.nn.sigmoid(jnp.matmul(h, router_w, preferred_element_type=jnp.float32))
    biased = scores + router_b.astype(jnp.float32)
    grouped = biased.reshape(n_tok, N_GROUPS, N_EXPERTS // N_GROUPS)
    group_score = jnp.sum(lax.top_k(grouped, 2)[0], axis=-1)
    top_groups = lax.top_k(group_score, TOPK_GROUPS)[1]
    group_mask = jnp.sum(jax.nn.one_hot(top_groups, N_GROUPS, dtype=jnp.float32), axis=1) > 0
    expert_mask = jnp.repeat(group_mask, N_EXPERTS // N_GROUPS, axis=1)
    top_e = lax.top_k(jnp.where(expert_mask, biased, -jnp.inf), TOP_K)[1]
    gates = jnp.take_along_axis(scores, top_e, axis=1)
    gates = gates / jnp.sum(gates, axis=-1, keepdims=True) * ROUTED_SCALE
    n_assign = n_tok * TOP_K
    flat_e = top_e.reshape(-1)
    flat_tok = jnp.repeat(jnp.arange(n_tok, dtype=jnp.int32), TOP_K)
    flat_g = gates.reshape(-1)
    order = jnp.argsort(flat_e)
    sorted_e = flat_e[order]
    counts = jnp.bincount(flat_e, length=N_EXPERTS)
    starts = jnp.cumsum(counts) - counts
    padded = (counts + MOE_BLOCK - 1) // MOE_BLOCK * MOE_BLOCK
    pad_ends = jnp.cumsum(padded)
    pad_starts = pad_ends - padded
    dest = pad_starts[sorted_e] + jnp.arange(n_assign) - starts[sorted_e]
    n_blocks = -(-(n_assign + N_EXPERTS * (MOE_BLOCK - 1)) // MOE_BLOCK)
    n_rows = n_blocks * MOE_BLOCK
    row_tok = jnp.zeros((n_rows,), jnp.int32).at[dest].set(flat_tok[order])
    row_gate = jnp.zeros((n_rows,), jnp.float32).at[dest].set(flat_g[order])
    block_e = jnp.minimum(jnp.searchsorted(pad_ends, jnp.arange(n_blocks) * MOE_BLOCK, side='right'),
                          N_EXPERTS - 1)
    xb = h[row_tok].reshape(n_blocks, MOE_BLOCK, dm)
    yb = lax.map(lambda a: swiglu(a[0], w_gate[a[1]], w_up[a[1]], w_down[a[1]]), (xb, block_e))
    routed = jnp.zeros((n_tok, dm), jnp.float32).at[row_tok].add(
        yb.reshape(n_rows, dm).astype(jnp.float32) * row_gate[:, None])
    shared = swiglu(h, sh_gate, sh_up, sh_down).astype(jnp.float32)
    return (routed + shared).astype(h.dtype)

def setup_inputs(seed: int = 0) -> dict:
    key = jax.random.key(seed)
    ks = jax.random.split(key, 32)
    d = D_MODEL

    def nrm(k, shape, s):
        return jax.random.normal(k, shape, jnp.float32) * s

    return {
        'x': nrm(ks[0], (BATCH, SEQ, d), 1.0),
        'c': nrm(ks[1], (BATCH, d), 1.0),
        'ctx': nrm(ks[2], (BATCH, CTX_LEN, d), 1.0),
        'c_ctx': nrm(ks[3], (d,), 1.0),
        'ada_w': nrm(ks[4], (DEPTH, d, 6 * d), 0.5 * d ** -0.5),
        'ada_b': nrm(ks[5], (DEPTH, 6 * d), 0.02),
        'norm_g': 1.0 + nrm(ks[6], (DEPTH, 4, d), 0.02),
        'cf_w_in': nrm(ks[7], (N_EVEN, d, MIX_IN), d ** -0.5),
        'cf_conv_w': nrm(ks[8], (N_EVEN, CONV_WIDTH, 1, CONV_CH), CONV_WIDTH ** -0.5),
        'cf_conv_b': nrm(ks[9], (N_EVEN, CONV_CH), 0.02),
        'cf_ln_g': 1.0 + nrm(ks[10], (N_EVEN, CONV_CH), 0.02),
        'cf_ln_b': nrm(ks[11], (N_EVEN, CONV_CH), 0.02),
        'cf_w_out': nrm(ks[12], (N_EVEN, MIX_OUT, d), MIX_OUT ** -0.5),
        'da_w_qkv': nrm(ks[13], (N_ODD, d, 2 * QK_W + V_W), d ** -0.5),
        'da_lambda': nrm(ks[14], (N_ODD, 4, DA_QK_DIM), 0.1),
        'da_subln_g': 1.0 + nrm(ks[15], (N_ODD, DA_V_DIM), 0.02),
        'da_w_out': nrm(ks[16], (N_ODD, V_W, d), V_W ** -0.5),
        'moe_router_w': nrm(ks[17], (DEPTH, d, N_EXPERTS), d ** -0.5),
        'moe_router_b': nrm(ks[18], (DEPTH, N_EXPERTS), 0.01),
        'moe_w_gate': nrm(ks[19], (DEPTH, N_EXPERTS, d, EXPERT_FF), d ** -0.5),
        'moe_w_up': nrm(ks[20], (DEPTH, N_EXPERTS, d, EXPERT_FF), d ** -0.5),
        'moe_w_down': nrm(ks[21], (DEPTH, N_EXPERTS, EXPERT_FF, d), EXPERT_FF ** -0.5),
        'moe_sh_gate': nrm(ks[22], (DEPTH, d, SHARED_FF), d ** -0.5),
        'moe_sh_up': nrm(ks[23], (DEPTH, d, SHARED_FF), d ** -0.5),
        'moe_sh_down': nrm(ks[24], (DEPTH, SHARED_FF, d), SHARED_FF ** -0.5),
    }

def reference(x, c, ctx, c_ctx, ada_w, ada_b, norm_g, cf_w_in, cf_conv_w, cf_conv_b, cf_ln_g, cf_ln_b,
              cf_w_out, da_w_qkv, da_lambda, da_subln_g, da_w_out, moe_router_w, moe_router_b,
              moe_w_gate, moe_w_up, moe_w_down, moe_sh_gate, moe_sh_up, moe_sh_down):
    bn, n_lat, dm = x.shape
    n_ctx = ctx.shape[1]
    cos, sin = axial_rope_tables(n_lat)
    c_lat = jax.nn.silu(c)[:, None, :]
    c_con = jax.nn.silu(c_ctx)[None, None, :]
    for i in range(DEPTH):
        last = i == DEPTH - 1
        odd = i % 2 == 1
        j = i // 2
        m_lat = jnp.split(c_lat @ ada_w[i] + ada_b[i], 6, axis=-1)
        m_ctx = jnp.split(c_con @ ada_w[i] + ada_b[i], 6, axis=-1)
        hx = rms_norm(x, norm_g[i, 0]) * (1.0 + m_lat[1]) + m_lat[0]
        if odd:
            hc = rms_norm(ctx, norm_g[i, 0]) * (1.0 + m_ctx[1]) + m_ctx[0]
            lam_init = 0.8 - 0.6 * math.exp(-0.3 * i)
            lp = da_lambda[j].astype(jnp.float32)
            lam = jnp.exp(jnp.sum(lp[0] * lp[1])) - jnp.exp(jnp.sum(lp[2] * lp[3])) + lam_init
            qx = apply_rope(da_queries(hx, da_w_qkv[j]), cos, sin)
            kx, vx = da_keys_values(hx, da_w_qkv[j])
            kx = apply_rope(kx, cos, sin)
            kc, vc = da_keys_values(hc, da_w_qkv[j])
            k_all = jnp.concatenate([kc, kx], axis=1)
            v_all = jnp.concatenate([vc, vx], axis=1)
            yx = diff_attn_out(diff_attention_core(qx, k_all, v_all, lam), da_subln_g[j], lam_init, da_w_out[j])
            if not last:
                qc = da_queries(hc, da_w_qkv[j])
                yc = diff_attn_out(diff_attention_core(qc, kc, vc, lam), da_subln_g[j], lam_init, da_w_out[j])
        else:
            yx = conv_fourier_mix(hx, cf_w_in[j], cf_conv_w[j], cf_conv_b[j], cf_ln_g[j], cf_ln_b[j], cf_w_out[j])
            if not last:
                hc = rms_norm(ctx, norm_g[i, 0]) * (1.0 + m_ctx[1]) + m_ctx[0]
                yc = conv_fourier_mix(hc, cf_w_in[j], cf_conv_w[j], cf_conv_b[j], cf_ln_g[j], cf_ln_b[j],
                                      cf_w_out[j])
        x = x + m_lat[2] * rms_norm(yx, norm_g[i, 1])
        if not last:
            ctx = ctx + m_ctx[2] * rms_norm(yc, norm_g[i, 1])
        tok = (rms_norm(x, norm_g[i, 2]) * (1.0 + m_lat[4]) + m_lat[3]).reshape(-1, dm)
        if not last:
            tok_c = (rms_norm(ctx, norm_g[i, 2]) * (1.0 + m_ctx[4]) + m_ctx[3]).reshape(-1, dm)
            tok = jnp.concatenate([tok, tok_c], axis=0)
        y = moe_ffn(tok, moe_router_w[i], moe_router_b[i], moe_w_gate[i], moe_w_up[i], moe_w_down[i],
                    moe_sh_gate[i], moe_sh_up[i], moe_sh_down[i])
        x = x + m_lat[5] * rms_norm(y[:bn * n_lat].reshape(bn, n_lat, dm), norm_g[i, 3])
        if not last:
            ctx = ctx + m_ctx[5] * rms_norm(y[bn * n_lat:].reshape(bn, n_ctx, dm), norm_g[i, 3])
    return x


_drawn_inputs = setup_inputs


def setup_inputs(seed=0):
    import zlib

    import numpy as np

    out = dict(_drawn_inputs(seed))
    spreads = {}
    factors = {}
    for name, (base, spread) in spreads.items():
        noise = np.random.default_rng([zlib.crc32(name.encode()), seed]).standard_normal(out[name].shape)
        drawn = base * np.exp(spread * noise) if base else spread * noise
        out[name] = jnp.asarray(drawn.astype(out[name].dtype))
    for name, factor in factors.items():
        out[name] = (out[name] * factor).astype(out[name].dtype)
    return out
```

```python
import math
from contextlib import ExitStack

import concourse.bass as bass
import numpy as np
from concourse import mybir

F32 = mybir.dt.float32
BF16 = mybir.dt.bfloat16
I32 = mybir.dt.int32
ALU = mybir.AluOpType
ACT = mybir.ActivationFunctionType
AX = mybir.AxisListType

P = 128
D = 1024
KC = D // P
SEQ = 256
TT = 2 * SEQ // P
EPS = 1e-6
CONV_CH, CONV_W, CONV_GROUP = 512, 31, 64
PAD = CONV_W // 2
CJ = CONV_CH // P
MIX_IN = 1536
HEADS, QK = 8, 64
NE, GROUPS, TOPG, TOPK, FF = 64, 8, 4, 6, 256
RSCALE = 2.5
ROWS = 2 * SEQ
EMPTY = 4096
BIG = 1e30
UNROLL = 4


class Memory:
    pass


def start(nc, ctx, m):

    def sb(name, shape, dt=F32):
        return ctx.enter_context(nc.sbuf_tensor(name, shape, dt))

    m.X = sb("X", [P, TT, D])
    m.hT = sb("hT", [P, KC, 2 * SEQ])
    m.W = sb("W", [P, UNROLL, 3 * 2048])
    m.ident = sb("ident", [P, P])
    m.eps = sb("eps", [P, 1])
    m.ps = ctx.enter_context(nc.psum_tensor("ps", [P, 8, 512], F32))
    m.used = []

    def sem(name):
        m.used.append(nc.alloc_semaphore(name))
        return m.used[-1]

    m.sem = sem
    m.MOD = nc.dram_tensor("mod_scratch", [2, 6, 2, D], F32).ap()
    m.H2 = nc.dram_tensor("h2_scratch", [ROWS, D], F32).ap()
    m.Y6 = nc.dram_tensor("y6_scratch", [TOPK * ROWS, D], F32).ap()


def bank2(m, b):
    return m.ps[:, b:b + 2, :].rearrange("p a n -> p (a n)")


def conditioning(nc, m, io):
    with ExitStack() as ctx:
        def sb(name, shape, dt=F32):
            return ctx.enter_context(nc.sbuf_tensor(name, shape, dt))

        SLOTS = 3
        cT = sb("cT", [P, 2, KC])
        cS = sb("cS", [P, 2, KC])
        brow = sb("brow", [2, SLOTS, 512])
        grow = sb("grow", [2, SLOTS, 512])
        mrow = sb("mrow", [2, 2, 512])
        orow = sb("orow", [2, 2, 512])
        ring = m.W[:, 0:2, :].rearrange("p a b -> p (a b)").rearrange("p (s k n) -> p s k n", s=SLOTS, k=KC)
        c_in = m.sem("ada_c_in")
        chunk_in = [m.sem(f"ada_chunk_in{s}") for s in range(SLOTS)]
        chunk_free = m.sem("ada_chunk_free")
        row_free = m.sem("ada_row_free")
        silu_done = m.sem("ada_silu_done")
        sums_done = m.sem("ada_sums_done")
        bank_free = m.sem("ada_bank_free")
        biased = m.sem("ada_biased")
        row_done = m.sem("ada_row_done")
        stored = [m.sem(f"ada_stored{i}") for i in range(2)]
        m.x_in = m.sem("x_in")
        eps_done = m.sem("eps_done")
        m.w_in_in = m.sem("w_in_in")
        adaw = io["ada_w"].rearrange("l (p k) n -> l p k n", p=P)
        CH = 6 * D // 512

        with nc.Block() as block:
            @block.sync
            def _(sp):
                sp.dma_start(cT[:, 0, :], io["c"].rearrange("o (p k) -> p (o k)", p=P)).then_inc(c_in, 16)
                sp.dma_start(cT[:, 1, :], io["c_ctx"].rearrange("(p k) -> p k", p=P)).then_inc(c_in, 16)
                sp.sem_inc(chunk_free, SLOTS)
                sp.sem_inc(row_free, SLOTS)
                with sp.Fori(0, 2) as l:
                    for j in range(CH):
                        s, v = j % SLOTS, j // 2
                        g = {0: 0, 1: 0, 2: 1, 3: 2, 4: 2, 5: 3}[v]
                        sp.wait_ge(chunk_free, l * CH + j + 1)
                        sp.wait_ge(row_free, l * CH + j + 1)
                        sp.dma_start(ring[:, s], adaw[l, :, :, j * 512:j * 512 + 512]).then_inc(chunk_in[s], 16)
                        sp.dma_start(brow[:, s, :], io["ada_b"][l, j * 512:j * 512 + 512].partition_broadcast(2)).then_inc(chunk_in[s], 16)
                        sp.dma_start(grow[:, s, :], io["norm_g"][l, g, (j % 2) * 512:(j % 2) * 512 + 512].partition_broadcast(2)).then_inc(chunk_in[s], 16)
                sp.dma_start(m.X[:, 0:2, :], io["x"].rearrange("b (t p) d -> p (b t) d", p=P)).then_inc(m.x_in, 16)
                sp.dma_start(m.X[:, 2:4, :], io["ctx"].rearrange("b (t p) d -> p (b t) d", p=P)).then_inc(m.x_in, 16)
                sp.dma_start(m.ident[:], io["k_ident"]).then_inc(m.x_in, 16)
                w_in = m.W[:, 2:4, :].rearrange("p a b -> p (a b)").rearrange("p (k n) -> p k n", k=KC)
                sp.dma_start(w_in, io["cf_w_in"][0].rearrange("(p k) n -> p k n", p=P)).then_inc(m.w_in_in, 16)
                sp.wait_ge(m.x_in, 48)
                for i in range(2):
                    sp.wait_ge(stored[i], 16 * (CH + 1))

            @block.gpsimd
            def _(pool):
                pool.memset(m.eps[:], EPS).then_inc(eps_done, 1)
                pool.wait_ge(eps_done, 1)

            @block.scalar
            def _(act):
                act.wait_ge(c_in, 32)
                act.activation(cS[:], cT[:], ACT.Silu).then_inc(silu_done, 1)
                act.sem_inc(stored[0], 16)
                act.sem_inc(stored[1], 16)
                with act.Fori(0, 2) as l:
                    for j in range(CH):
                        v = j // 2
                        act.wait_ge(row_done, l * CH + j + 1)
                        act.dma_start(m.MOD[l, v, :, (j % 2) * 512:(j % 2) * 512 + 512], orow[:, j % 2, :]).then_inc(stored[j % 2], 16)

            @block.tensor
            def _(pe):
                pe.wait_ge(silu_done, 1)
                pe.sem_inc(bank_free, 2)
                with pe.Fori(0, 2) as l:
                    for j in range(CH):
                        s = j % SLOTS
                        pe.wait_ge(chunk_in[s], (l * (CH // SLOTS) + j // SLOTS + 1) * 48)
                        pe.wait_ge(bank_free, l * CH + j + 1)
                        for k in range(KC):
                            mm = pe.matmul(m.ps[0:2, j % 2, :], cS[:, :, k], ring[:, s, k, :], start=(k == 0), stop=(k == KC - 1))
                        mm.then_inc(sums_done, 1)

            @block.vector
            def _(dve):
                with dve.Fori(0, 2) as l:
                    for j in range(CH):
                        s, v = j % SLOTS, j // 2
                        n = l * CH + j + 1
                        dve.wait_ge(sums_done, n)
                        one = 1.0 if v in (1, 4) else 0.0
                        dve.wait_ge(stored[j % 2], (l * (CH // 2) + j // 2 + 1) * 16)
                        last = dve.scalar_tensor_tensor(mrow[:, j % 2, :], m.ps[0:2, j % 2, :], one, brow[:, s, :], ALU.add, ALU.add)
                        last.then_inc(biased, 1)
                        dve.wait_ge(biased, n)
                        if v in (0, 3):
                            last = dve.tensor_copy(orow[:, j % 2, :], mrow[:, j % 2, :])
                        else:
                            last = dve.tensor_tensor(orow[:, j % 2, :], mrow[:, j % 2, :], grow[:, s, :], ALU.mult)
                        last.then_inc(row_done, 1)
                        dve.wait_ge(row_done, n)
                        dve.sem_inc(bank_free, 1)
                        dve.sem_inc(chunk_free, 1)
                        dve.sem_inc(row_free, 1)


def modulate(nc, m, io, tag, layer, half, tiles, store):
    nt = len(tiles)
    with ExitStack() as ctx:
        def sb(name, shape, dt=F32):
            return ctx.enter_context(nc.sbuf_tensor(f"{tag}_{name}", shape, dt))

        A = sb("A", [P, 2, D])
        B = sb("B", [P, 2, D])
        junk = sb("junk", [P, D])
        h = sb("h", [P, 2, D])
        hp = sb("hp", [P, 2, D])
        ssq = sb("ssq", [P, TT])
        std = sb("std", [P, TT])
        rstd = sb("rstd", [P, TT])
        rows_in = m.sem(f"{tag}_rows_in")
        squared = m.sem(f"{tag}_squared")
        std_done = m.sem(f"{tag}_std_done")
        rstd_done = m.sem(f"{tag}_rstd_done")
        scaled = m.sem(f"{tag}_scaled")
        h_done = m.sem(f"{tag}_h_done")
        turned = m.sem(f"{tag}_turned")
        hT_done = m.sem(f"{tag}_hT_done")
        h_stored = [m.sem(f"{tag}_h_stored{i}") for i in range(2)]
        streams = 2 if nt > 2 else 1

        with nc.Block() as block:
            @block.sync
            def _(sp):
                for s in range(streams):
                    sp.dma_start(A[:, s, :], m.MOD[layer, 3 * half + 1, s, :].partition_broadcast(P)).then_inc(rows_in, 16)
                    sp.dma_start(B[:, s, :], m.MOD[layer, 3 * half, s, :].partition_broadcast(P)).then_inc(rows_in, 16)
                if store:
                    for i, t in enumerate(tiles):
                        sp.wait_ge(h_done, i + 1)
                        sp.dma_start(m.H2[t * P:(t + 1) * P, :], hp[:, i % 2, :]).then_inc(h_stored[i % 2], 16)
                    for i in range(2):
                        sp.wait_ge(h_stored[i], 16 * (nt // 2))

            @block.scalar
            def _(act):
                for i, t in enumerate(tiles):
                    if i:
                        act.wait_ge(squared, i)
                    act.activation(junk[:], m.X[:, t, :], ACT.Square, accum_out=ssq[:, i:i + 1]).then_inc(squared, 1)
                act.wait_ge(squared, nt)
                act.activation(std[:, 0:nt], ssq[:, 0:nt], ACT.Sqrt, bias=m.eps[:], scale=1.0 / D).then_inc(std_done, 1)
                for i, t in enumerate(tiles):
                    act.wait_ge(turned, i + 1)
                    act.activation(m.hT[:, :, t * P:(t + 1) * P], bank2(m, 2 * (i % 2)).rearrange("p (k t) -> p k t", k=KC), ACT.Copy).then_inc(hT_done, 1)

            @block.vector
            def _(dve):
                dve.wait_ge(std_done, 1)
                dve.reciprocal(rstd[:, 0:nt], std[:, 0:nt]).then_inc(rstd_done, 1)
                dve.wait_ge(rstd_done, 1)
                dve.wait_ge(rows_in, 32 * streams)
                for i, t in enumerate(tiles):
                    s = t // 2
                    dve.scalar_tensor_tensor(h[:, i % 2, :], m.X[:, t, :], rstd[:, i:i + 1], A[:, s, :], ALU.mult, ALU.mult).then_inc(scaled, 1)
                    dve.wait_ge(scaled, i + 1)
                    if i >= 2:
                        dve.wait_ge(turned, i - 1)
                        if store:
                            dve.wait_ge(h_stored[i % 2], 16 * (i // 2))
                    dve.tensor_tensor(hp[:, i % 2, :].rearrange("t (k p) -> t p k", k=KC), h[:, i % 2, :].rearrange("t (p k) -> t p k", k=KC),
                                      B[:, s, :].rearrange("t (p k) -> t p k", k=KC), ALU.add).then_inc(h_done, 1)

            @block.tensor
            def _(pe):
                for i in range(nt):
                    pe.wait_ge(h_done, i + 1)
                    if i >= 2:
                        pe.wait_ge(hT_done, i - 1)
                    for k in range(KC):
                        mm = pe.transpose(m.ps[:, 2 * (i % 2) + k // 4, (k % 4) * P:(k % 4 + 1) * P], hp[:, i % 2, k * P:(k + 1) * P], m.ident[:])
                    mm.then_inc(turned, 1)


def mixer(nc, m, io):
    with ExitStack() as ctx:
        def sb(name, shape, dt=F32):
            return ctx.enter_context(nc.sbuf_tensor(f"mix_{name}", shape, dt))

        w_in = m.W[:, 2:4, :].rearrange("p a b -> p (a b)").rearrange("p (k n) -> p k n", k=KC)
        w_out = m.W[:, 0:2, :].rearrange("p a b -> p (a b)")[:, 0:KC * D].rearrange("p (k n) -> p k n", k=KC)
        apad = sb("apad", [P, CJ, 2, SEQ + 2 * PAD])
        sg = sb("sg", [P, 2, 512])
        fT = sb("fT", [P, 4, 512])
        P1 = sb("P1", [P, TT, 4, 256])
        mixT = sb("mixT", [P, KC, 512])
        fch = sb("fch", [P, 256])
        fseq = sb("fseq", [P, 2, 512])
        gmean = sb("gmean", [P, P])
        prow = sb("prow", [CONV_W + 3, 512])
        pcol = sb("pcol", [P, CJ, 64])
        G = sb("G", [P, 2, D])
        tmp = sb("tmp", [P, D])
        ssq = sb("ssq", [P, TT])
        std4 = sb("std4", [P, TT])
        rstd4 = sb("rstd4", [P, TT])
        sq = P1[:].rearrange("p a b c -> p (a b c)")[:, 0:2048].rearrange("p (j n) -> p j n", j=4)
        junk = P1[:].rearrange("p a b c -> p (a b c)")[:, 2048:3072]

        s = m.sem
        consts_in, w_out_in = s("mix_consts_in"), s("mix_w_out_in")
        params_turned, params_done = s("mix_params_turned"), s("mix_params_done")
        padded = s("mix_padded")
        u_done, gate_done, val_done, f_done = s("mix_u_done"), s("mix_gate_done"), s("mix_val_done"), s("mix_f_done")
        ch_done, ch_out, seq_done, seq_out = s("mix_ch_done"), s("mix_ch_out"), s("mix_seq_done"), s("mix_seq_out")
        tap, conv_done = s("mix_tap"), s("mix_conv_done")
        mean_done, centred, squared = s("mix_mean_done"), s("mix_centred"), s("mix_squared")
        var_done, std_done, rec_done, normed, a_done = s("mix_var_done"), s("mix_std_done"), s("mix_rec_done"), s("mix_normed"), s("mix_a_done")
        y_done, y_sq, y_std, y_rec, y_scaled, x_done = s("mix_y_done"), s("mix_y_sq"), s("mix_y_std"), s("mix_y_rec"), s("mix_y_scaled"), s("mix_x_done")

        with nc.Block() as block:
            @block.sync
            def _(sp):
                sp.dma_start(prow[0:CONV_W, :], io["cf_conv_w"][0].rearrange("w o c -> w (o c)")).then_inc(consts_in, 16)
                for i, n in enumerate(("cf_conv_b", "cf_ln_g", "cf_ln_b")):
                    sp.dma_start(prow[CONV_W + i:CONV_W + i + 1, :], io[n]).then_inc(consts_in, 16)
                sp.dma_start(fch[:], io["k_fch"]).then_inc(consts_in, 16)
                sp.dma_start(fseq[:], io["k_fseq"]).then_inc(consts_in, 16)
                sp.dma_start(gmean[:], io["k_gmean"]).then_inc(consts_in, 16)
                for i in range(2):
                    sp.dma_start(G[:, i, :], m.MOD[0, 2, i, :].partition_broadcast(P)).then_inc(consts_in, 16)
                sp.dma_start(w_out, io["cf_w_out"][0].rearrange("(k p) n -> p k n", p=P)).then_inc(w_out_in, 16)

            @block.gpsimd
            def _(pool):
                pool.memset(apad[:], 0.0).then_inc(padded, 1)

            @block.tensor
            def _(pe):
                pe.wait_ge(consts_in, 16 * 9)
                for j in range(CJ):
                    mm = pe.transpose(m.ps[:, 7, j * 64:j * 64 + CONV_W + 3], prow[:, j * P:(j + 1) * P], m.ident[0:CONV_W + 3, 0:CONV_W + 3])
                mm.then_inc(params_turned, 1)
                pe.wait_ge(m.w_in_in, 16)
                order = [x for j in range(CJ) for x in (CJ + j, j)] + [2 * CJ + g for g in range(4)]
                for n, mt in enumerate(order):
                    if n >= 4:
                        q = n - 4
                        if q < 8:
                            pe.wait_ge((gate_done, val_done)[q % 2], q // 2 + 1)
                        else:
                            pe.wait_ge(f_done, q - 7)
                    for k in range(KC):
                        mm = pe.matmul(m.ps[:, n % 4, :], w_in[:, k, mt * P:(mt + 1) * P], m.hT[:, k, :], start=(k == 0), stop=(k == KC - 1))
                    mm.then_inc(u_done, 1)
                pe.wait_ge(f_done, 4)
                for n in range(2 * TT):
                    t, gp = n // 2, n % 2
                    if n >= 2:
                        pe.wait_ge(ch_out, n - 1)
                    for g in (2 * gp, 2 * gp + 1):
                        mm = pe.matmul(m.ps[:, 4 + n % 2, (g % 2) * 256:(g % 2) * 256 + 256], fT[:, g, t * P:(t + 1) * P], fch[:], start=True, stop=True)
                    mm.then_inc(ch_done, 1)
                pe.wait_ge(ch_out, 2 * TT)
                pe.wait_ge(params_done, 1)
                for g in range(4):
                    if g >= 2:
                        pe.wait_ge(seq_out, g - 1)
                    for st in range(2):
                        for n in range(4):
                            kt, cs = n // 2, n % 2
                            mm = pe.matmul(m.ps[:, 6 + g % 2, st * 256:st * 256 + 256], P1[:, 2 * st + kt, g, cs * P:(cs + 1) * P],
                                           fseq[:, kt, cs * 256:cs * 256 + 256], start=(n == 0), stop=(n == 3))
                    mm.then_inc(seq_done, 1)
                for j in range(CJ):
                    pe.wait_ge(conv_done, j + 1)
                    pe.matmul(m.ps[:, j, :], gmean[:], mixT[:, j, :], start=True, stop=True).then_inc(mean_done, 1)
                pe.wait_ge(seq_out, 4)
                for j in range(CJ):
                    pe.wait_ge(squared, j + 1)
                    pe.matmul(m.ps[:, 4 + j, :], gmean[:], sq[:, j, :], start=True, stop=True).then_inc(var_done, 1)
                pe.wait_ge(w_out_in, 16)
                pe.wait_ge(a_done, CJ)
                for t in range(TT):
                    if t >= 2:
                        pe.wait_ge(y_scaled, t - 1)
                    for n in range(2):
                        for k in range(KC):
                            mm = pe.matmul(m.ps[:, 2 * (t % 2) + n, :], mixT[:, k, t * P:(t + 1) * P], w_out[:, k, n * 512:n * 512 + 512],
                                           start=(k == 0), stop=(k == KC - 1))
                    mm.then_inc(y_done, 1)

            @block.scalar
            def _(act):
                for j in range(CJ):
                    act.wait_ge(u_done, 2 * j + 1)
                    if j >= 2:
                        act.wait_ge(val_done, j - 1)
                    act.activation(sg[:, j % 2, :], m.ps[:, (2 * j) % 4, :], ACT.Sigmoid).then_inc(gate_done, 1)
                for g in range(4):
                    act.wait_ge(u_done, 9 + g)
                    act.activation(fT[:, g, :], m.ps[:, g % 4, :], ACT.Copy).then_inc(f_done, 1)
                for n in range(2 * TT):
                    act.wait_ge(ch_done, n + 1)
                    act.activation(P1[:, n // 2, 2 * (n % 2):2 * (n % 2) + 2, :], m.ps[:, 4 + n % 2, :].rearrange("p (g c) -> p g c", g=2), ACT.Copy).then_inc(ch_out, 1)
                for g in range(4):
                    act.wait_ge(seq_done, g + 1)
                    act.activation(mixT[:, 4 + g, :], m.ps[:, 6 + g % 2, :], ACT.Copy).then_inc(seq_out, 1)
                for j in range(CJ):
                    act.wait_ge(centred, j + 1)
                    act.activation(sq[:, j, :], mixT[:, j, :], ACT.Square).then_inc(squared, 1)
                for j in range(CJ):
                    act.wait_ge(var_done, j + 1)
                    act.activation(fT[:, j, :], m.ps[:, 4 + j, :], ACT.Sqrt, bias=m.eps[:]).then_inc(std_done, 1)
                for j in range(CJ):
                    act.wait_ge(normed, j + 1)
                    act.activation(mixT[:, j, :], mixT[:, j, :], ACT.Silu, bias=pcol[:, j, CONV_W + 2:CONV_W + 3], scale=pcol[:, j, CONV_W + 1:CONV_W + 2]).then_inc(a_done, 1)
                for t in range(TT):
                    act.wait_ge(y_done, t + 1)
                    if t:
                        act.wait_ge(y_sq, t)
                    act.activation(junk, bank2(m, 2 * (t % 2)), ACT.Square, accum_out=ssq[:, t:t + 1]).then_inc(y_sq, 1)
                    act.wait_ge(y_sq, t + 1)
                    act.activation(std4[:, t:t + 1], ssq[:, t:t + 1], ACT.Sqrt, bias=m.eps[:], scale=1.0 / D).then_inc(y_std, 1)

            @block.vector
            def _(dve):
                dve.wait_ge(params_turned, 1)
                dve.tensor_copy(pcol[:, :, 0:CONV_W + 3], m.ps[:, 7, 0:256].rearrange("p (j w) -> p j w", j=CJ)[:, :, 0:CONV_W + 3]).then_inc(params_done, 1)
                dve.wait_ge(padded, 1)
                for j in range(CJ):
                    dve.wait_ge(gate_done, j + 1)
                    dve.wait_ge(u_done, 2 * j + 2)
                    dve.tensor_tensor(apad[:, j, :, PAD:PAD + SEQ], m.ps[:, (2 * j + 1) % 4, :].rearrange("p (s n) -> p s n", s=2),
                                      sg[:, j % 2, :].rearrange("p (s n) -> p s n", s=2), ALU.mult).then_inc(val_done, 1)
                dve.wait_ge(params_done, 1)
                taps = 0
                for j in range(CJ):
                    dve.wait_ge(val_done, j + 1)
                    acc = mixT[:, j, :].rearrange("p (s n) -> p s n", s=2)
                    dve.tensor_scalar(acc, apad[:, j, :, 0:SEQ], pcol[:, j, 0:1], pcol[:, j, CONV_W:CONV_W + 1], ALU.mult, ALU.add).then_inc(tap, 1)
                    taps += 1
                    for w in range(1, CONV_W):
                        dve.wait_ge(tap, taps)
                        last = dve.scalar_tensor_tensor(acc, apad[:, j, :, w:w + SEQ], pcol[:, j, w:w + 1], acc, ALU.mult, ALU.add)
                        if w < CONV_W - 1:
                            last.then_inc(tap, 1)
                            taps += 1
                        else:
                            last.then_inc(conv_done, 1)
                for j in range(CJ):
                    dve.wait_ge(mean_done, j + 1)
                    dve.tensor_tensor(mixT[:, j, :], mixT[:, j, :], m.ps[:, j, :], ALU.subtract).then_inc(centred, 1)
                for j in range(CJ):
                    dve.wait_ge(std_done, j + 1)
                    dve.reciprocal(fT[:, j, :], fT[:, j, :]).then_inc(rec_done, 1)
                    dve.wait_ge(rec_done, j + 1)
                    dve.wait_ge(squared, j + 1)
                    dve.tensor_tensor(mixT[:, j, :], mixT[:, j, :], fT[:, j, :], ALU.mult).then_inc(normed, 1)
                dve.wait_ge(consts_in, 16 * 9)
                for t in range(TT):
                    dve.wait_ge(y_std, t + 1)
                    dve.reciprocal(rstd4[:, t:t + 1], std4[:, t:t + 1]).then_inc(y_rec, 1)
                    dve.wait_ge(y_rec, t + 1)
                    if t:
                        dve.wait_ge(x_done, t)
                    dve.scalar_tensor_tensor(tmp[:], bank2(m, 2 * (t % 2)), rstd4[:, t:t + 1], G[:, t // 2, :], ALU.mult, ALU.mult).then_inc(y_scaled, 1)
                    dve.wait_ge(y_scaled, t + 1)
                    dve.tensor_tensor(m.X[:, t, :], m.X[:, t, :], tmp[:], ALU.add).then_inc(x_done, 1)


def attention(nc, m, io):
    lam_init = 0.8 - 0.6 * math.exp(-0.3)
    scale = QK ** -0.5
    with ExitStack() as ctx:
        def sb(name, shape, dt=F32):
            return ctx.enter_context(nc.sbuf_tensor(f"att_{name}", shape, dt))

        wc = m.W[:].rearrange("p a b -> p (a b)").rearrange("p (c k n) -> p c k n", c=6, k=KC)
        qT = sb("qT", [P, HEADS, SEQ])
        kT = sb("kT", [P, HEADS, 2 * SEQ])
        v = sb("v", [P, TT, D])
        cosT, sinT = sb("cosT", [P, SEQ]), sb("sinT", [P, SEQ])
        rot = sb("rot", [P, P])
        t1, t2 = sb("t1", [P, SEQ]), sb("t2", [P, SEQ])
        lp = sb("lp", [P, 4 * QK])
        lj = sb("lj", [P, 2 * QK])
        ls, le, nlam = sb("ls", [P, 2]), sb("le", [P, 2]), sb("nlam", [P, 1])
        mx, nm, sm, rs = (sb(n, [P, 2 * HEADS, 2]) for n in ("mx", "nm", "sm", "rs"))
        cf = sb("cf", [P, 2 * HEADS])
        p0, p1 = sb("p0", [P, 2, 512]), sb("p1", [P, 2, 512])
        pdT = sb("pdT", [P, 2, 512])
        o = sb("o", [P, 2, D])
        ss8, st8, r8 = (sb(n, [P, 2, HEADS]) for n in ("ss8", "st8", "r8"))
        sub = sb("sub", [P, 1])
        subs = sb("subs", [P, 1])
        G = sb("G", [P, D])
        tmp = sb("tmp", [P, D])
        ssq, std, rstd = (sb(n, [P, 2]) for n in ("ssq", "std", "rstd"))
        oT = m.hT[:, :, 0:SEQ]

        s = m.sem
        w_in = [s(f"att_w_in{c}") for c in range(6)]
        consts_in, w_out_in = s("att_consts_in"), s("att_w_out_in")
        lam_step, lam_sum, lam_exp = s("att_lam_step"), s("att_lam_sum"), s("att_lam_exp")
        raw_done, raw_out, turned, t1_done, t2_done, roped = (s(f"att_{n}") for n in ("raw_done", "raw_out", "turned", "t1_done", "t2_done", "roped"))
        v_done, v_out = s("att_v_done"), s("att_v_out")
        s_done, max_done, neg_done, exp_done, rec_done, cf_done, p1_done, pd_done = (
            s(f"att_{n}") for n in ("s_done", "max_done", "neg_done", "exp_done", "rec_done", "cf_done", "p1_done", "pd_done"))
        pT_done, pT_out, o_done, o_out = (s(f"att_{n}") for n in ("pT_done", "pT_out", "o_done", "o_out"))
        o_sq, o_sum, o_std, o_rec, o_norm, oT_done, oT_out = (s(f"att_{n}") for n in ("o_sq", "o_sum", "o_std", "o_rec", "o_norm", "oT_done", "oT_out"))
        y_done, y_sq, y_std, y_rec, y_scaled, x_done = (s(f"att_y{n}") for n in ("_done", "_sq", "_std", "_rec", "_scaled", "_x"))
        UNITS = 2 * HEADS
        CONSTS = 16 * 6

        with nc.Block() as block:
            @block.sync
            def _(sp):
                wq = io["da_w_qkv"][0].rearrange("(p k) n -> p k n", p=P)
                for c in (0, 2, 1, 3, 4, 5):
                    sp.dma_start(wc[:, c], wq[:, :, c * 512:c * 512 + 512]).then_inc(w_in[c], 16)
                    if c == 0:
                        sp.dma_start(cosT[:], io["k_cos"]).then_inc(consts_in, 16)
                        sp.dma_start(sinT[:], io["k_sin"]).then_inc(consts_in, 16)
                        sp.dma_start(rot[:], io["k_rot"]).then_inc(consts_in, 16)
                        sp.dma_start(lp[:], io["da_lambda"][0].rearrange("a b -> (a b)").partition_broadcast(P)).then_inc(consts_in, 16)
                        sp.dma_start(G[:], m.MOD[1, 2, 0, :].partition_broadcast(P)).then_inc(consts_in, 16)
                        sp.dma_start(sub[:], io["da_subln_g"].rearrange("a p -> p a")).then_inc(consts_in, 16)
                sp.wait_ge(raw_done, UNITS)
                for n in range(2):
                    sp.dma_start(wc[:, n], io["da_w_out"][0].rearrange("(k p) n -> p k n", p=P)[:, :, n * 512:n * 512 + 512]).then_inc(w_out_in, 16)

            @block.tensor
            def _(pe):
                def rotate(u):
                    hd, is_k = u // 2, u % 2
                    pe.wait_ge(raw_out, u + 1)
                    if u >= 2:
                        pe.wait_ge(t2_done, u - 1)
                    src = kT[:, hd, 0:SEQ] if is_k else qT[:, hd, :]
                    pe.matmul(m.ps[:, 2 + u % 2, 0:SEQ], rot[:], src, start=True, stop=True).then_inc(turned, 1)

                for u in range(UNITS):
                    hd, is_k = u // 2, u % 2
                    c, n = 2 * is_k + hd // 4, SEQ * (1 + is_k)
                    pe.wait_ge(w_in[c], 16)
                    if u >= 2:
                        pe.wait_ge(raw_out, u - 1)
                    for k in range(KC):
                        mm = pe.matmul(m.ps[:, u % 2, 0:n], wc[:, c, k, (hd % 4) * P:(hd % 4 + 1) * P], m.hT[:, k, 0:n], start=(k == 0), stop=(k == KC - 1))
                    mm.then_inc(raw_done, 1)
                    if u == 0:
                        pe.wait_ge(consts_in, CONSTS)
                    else:
                        rotate(u - 1)
                for i in range(2 * TT):
                    t, n = i // 2, i % 2
                    pe.wait_ge(w_in[4 + n], 16)
                    if i >= 2:
                        pe.wait_ge(v_out, i - 1)
                    for k in range(KC):
                        mm = pe.matmul(m.ps[:, 4 + i % 2, :], m.hT[:, k, t * P:(t + 1) * P], wc[:, 4 + n, k, :], start=(k == 0), stop=(k == KC - 1))
                    mm.then_inc(v_done, 1)
                    if i == 0:
                        rotate(UNITS - 1)
                pe.wait_ge(v_out, 2 * TT)
                pe.wait_ge(roped, UNITS)

                def scores(a):
                    hd, qt = a // 2, a % 2
                    if a >= 2:
                        pe.wait_ge(exp_done, 2 * (a - 1))
                    for c in range(2):
                        mm = pe.matmul(m.ps[:, 2 * (a % 2) + c, :], qT[c * QK:(c + 1) * QK, hd, qt * P:(qt + 1) * P], kT[c * QK:(c + 1) * QK, hd, :], start=True, stop=True)
                        mm.then_inc(s_done, 1)

                def values(a):
                    hd = a // 2
                    pe.wait_ge(pd_done, a + 1)
                    if a >= 2:
                        pe.wait_ge(pT_out, a - 1)
                        pe.wait_ge(o_out, a - 1)
                    for t in range(TT):
                        mm = pe.transpose(m.ps[:, 4 + a % 2, t * P:(t + 1) * P], p0[:, a % 2, t * P:(t + 1) * P], m.ident[:])
                    mm.then_inc(pT_done, 1)
                    pe.wait_ge(pT_out, a + 1)
                    for t in range(TT):
                        mm = pe.matmul(m.ps[:, 6 + a % 2, 0:P], pdT[:, a % 2, t * P:(t + 1) * P], v[:, t, hd * P:(hd + 1) * P], start=(t == 0), stop=(t == TT - 1))
                    mm.then_inc(o_done, 1)

                for a in range(2 * HEADS):
                    scores(a)
                    if a:
                        values(a - 1)
                values(2 * HEADS - 1)
                for qt in range(2):
                    pe.wait_ge(o_norm, qt + 1)
                    for k in range(KC):
                        mm = pe.transpose(m.ps[:, 2 * qt + k // 4, (k % 4) * P:(k % 4 + 1) * P], o[:, qt, k * P:(k + 1) * P], m.ident[:])
                    mm.then_inc(oT_done, 1)
                pe.wait_ge(w_out_in, 32)
                pe.wait_ge(o_out, 2 * HEADS)
                for qt in range(2):
                    pe.wait_ge(oT_out, qt + 1)
                    for n in range(2):
                        for k in range(KC):
                            mm = pe.matmul(m.ps[:, 4 + 2 * qt + n, :], oT[:, k, qt * P:(qt + 1) * P], wc[:, n, k, :], start=(k == 0), stop=(k == KC - 1))
                    mm.then_inc(y_done, 1)

            @block.scalar
            def _(act):
                for u in range(UNITS):
                    hd, is_k = u // 2, u % 2
                    act.wait_ge(raw_done, u + 1)
                    dst = kT[:, hd, :] if is_k else qT[:, hd, :]
                    act.activation(dst, m.ps[:, u % 2, 0:SEQ * (1 + is_k)], ACT.Copy).then_inc(raw_out, 1)
                for i in range(2 * TT):
                    act.wait_ge(v_done, i + 1)
                    act.activation(v[:, i // 2, (i % 2) * 512:(i % 2) * 512 + 512], m.ps[:, 4 + i % 2, :], ACT.Copy).then_inc(v_out, 1)
                act.wait_ge(lam_sum, 2)
                act.activation(le[:], ls[:], ACT.Exp).then_inc(lam_exp, 1)

                def output(a):
                    act.wait_ge(pT_done, a + 1)
                    if a >= 2:
                        act.wait_ge(o_done, a - 1)
                    act.activation(pdT[:, a % 2, :], m.ps[:, 4 + a % 2, :], ACT.Copy).then_inc(pT_out, 1)
                    act.wait_ge(o_done, a + 1)
                    act.activation(o[:, a % 2, (a // 2) * P:(a // 2 + 1) * P], m.ps[:, 6 + a % 2, 0:P], ACT.Copy).then_inc(o_out, 1)

                for a in range(2 * HEADS):
                    act.wait_ge(neg_done, a + 1)
                    if a >= 2:
                        act.wait_ge(pT_done, a - 1)
                    for c, pc in enumerate((p0, p1)):
                        act.activation(pc[:, a % 2, :], m.ps[:, 2 * (a % 2) + c, :], ACT.Exp, bias=nm[:, a, c:c + 1], scale=scale,
                                       accum_out=sm[:, a, c:c + 1]).then_inc(exp_done, 1)
                    if a:
                        output(a - 1)
                output(2 * HEADS - 1)
                for qt in range(2):
                    act.wait_ge(o_sum, qt + 1)
                    act.activation(st8[:, qt, :], ss8[:, qt, :], ACT.Sqrt, bias=m.eps[:], scale=1.0 / P).then_inc(o_std, 1)
                for qt in range(2):
                    act.wait_ge(oT_done, qt + 1)
                    act.wait_ge(lam_step, 3)
                    act.activation(oT[:, :, qt * P:(qt + 1) * P], bank2(m, 2 * qt).rearrange("p (k t) -> p k t", k=KC), ACT.Copy, scale=subs[:]).then_inc(oT_out, 1)
                for qt in range(2):
                    act.wait_ge(y_done, qt + 1)
                    act.activation(v[:, qt, :], bank2(m, 4 + 2 * qt), ACT.Square, accum_out=ssq[:, qt:qt + 1]).then_inc(y_sq, 1)
                    act.wait_ge(y_sq, qt + 1)
                    act.activation(std[:, qt:qt + 1], ssq[:, qt:qt + 1], ACT.Sqrt, bias=m.eps[:], scale=1.0 / D).then_inc(y_std, 1)

            @block.vector
            def _(dve):
                dve.wait_ge(consts_in, CONSTS)
                dve.tensor_scalar(subs[:], sub[:], 1.0 - lam_init, None, ALU.mult).then_inc(lam_step, 1)
                for i in range(2):
                    dve.tensor_tensor(lj[:, i * QK:(i + 1) * QK], lp[:, 2 * i * QK:(2 * i + 1) * QK], lp[:, (2 * i + 1) * QK:(2 * i + 2) * QK], ALU.mult).then_inc(lam_step, 1)
                dve.wait_ge(lam_step, 3)
                for i in range(2):
                    dve.tensor_reduce(ls[:, i:i + 1], lj[:, i * QK:(i + 1) * QK], AX.X, ALU.add).then_inc(lam_sum, 1)
                for u in range(UNITS):
                    hd, is_k = u // 2, u % 2
                    dst = kT[:, hd, 0:SEQ] if is_k else qT[:, hd, :]
                    dve.wait_ge(turned, u + 1)
                    if u:
                        dve.wait_ge(roped, u)
                    dve.tensor_tensor(t1[:], dst, cosT[:], ALU.mult).then_inc(t1_done, 1)
                    dve.tensor_tensor(t2[:], m.ps[:, 2 + u % 2, 0:SEQ], sinT[:], ALU.mult).then_inc(t2_done, 1)
                    dve.wait_ge(t1_done, u + 1)
                    dve.wait_ge(t2_done, u + 1)
                    dve.tensor_tensor(dst, t1[:], t2[:], ALU.add).then_inc(roped, 1)
                dve.wait_ge(lam_exp, 1)
                dve.tensor_tensor(nlam[:], le[:, 1:2], le[:, 0:1], ALU.subtract).then_inc(lam_step, 1)
                dve.wait_ge(lam_step, 4)
                dve.tensor_scalar(nlam[:], nlam[:], -lam_init, None, ALU.add).then_inc(lam_step, 1)
                dve.wait_ge(lam_step, 5)

                def weights(a):
                    dve.wait_ge(exp_done, 2 * a + 2)
                    dve.reciprocal(rs[:, a, :], sm[:, a, :]).then_inc(rec_done, 1)
                    dve.wait_ge(rec_done, a + 1)
                    dve.tensor_tensor(cf[:, a:a + 1], rs[:, a, 1:2], nlam[:], ALU.mult).then_inc(cf_done, 1)
                    dve.wait_ge(cf_done, a + 1)
                    dve.tensor_scalar(p1[:, a % 2, :], p1[:, a % 2, :], cf[:, a:a + 1], None, ALU.mult).then_inc(p1_done, 1)
                    dve.wait_ge(p1_done, a + 1)
                    dve.scalar_tensor_tensor(p0[:, a % 2, :], p0[:, a % 2, :], rs[:, a, 0:1], p1[:, a % 2, :], ALU.mult, ALU.add).then_inc(pd_done, 1)

                for a in range(2 * HEADS):
                    dve.wait_ge(s_done, 2 * a + 2)
                    dve.tensor_reduce(mx[:, a, :], m.ps[:, 2 * (a % 2):2 * (a % 2) + 2, :], AX.X, ALU.max).then_inc(max_done, 1)
                    dve.wait_ge(max_done, a + 1)
                    dve.tensor_scalar(nm[:, a, :], mx[:, a, :], -scale, None, ALU.mult).then_inc(neg_done, 1)
                    if a:
                        weights(a - 1)
                weights(2 * HEADS - 1)
                dve.wait_ge(o_out, 2 * HEADS)
                for qt in range(2):
                    dve.tensor_tensor(v[:, qt, :], o[:, qt, :], o[:, qt, :], ALU.mult).then_inc(o_sq, 1)
                    dve.wait_ge(o_sq, qt + 1)
                    dve.tensor_reduce(ss8[:, qt, :], v[:, qt, :].rearrange("p (h d) -> p h d", h=HEADS), AX.X, ALU.add).then_inc(o_sum, 1)
                for qt in range(2):
                    dve.wait_ge(o_std, qt + 1)
                    dve.reciprocal(r8[:, qt, :], st8[:, qt, :]).then_inc(o_rec, 1)
                    dve.wait_ge(o_rec, qt + 1)
                    oh = o[:, qt, :].rearrange("p (h d) -> p h d", h=HEADS)
                    dve.tensor_tensor(oh, oh, r8[:, qt, :].unsqueeze(2).broadcast_to([P, HEADS, P]), ALU.mult).then_inc(o_norm, 1)
                for t in range(2):
                    dve.wait_ge(y_std, t + 1)
                    dve.reciprocal(rstd[:, t:t + 1], std[:, t:t + 1]).then_inc(y_rec, 1)
                    dve.wait_ge(y_rec, t + 1)
                    if t:
                        dve.wait_ge(x_done, t)
                    dve.scalar_tensor_tensor(tmp[:], bank2(m, 4 + 2 * t), rstd[:, t:t + 1], G[:], ALU.mult, ALU.mult).then_inc(y_scaled, 1)
                    dve.wait_ge(y_scaled, t + 1)
                    dve.tensor_tensor(m.X[:, t, :], m.X[:, t, :], tmp[:], ALU.add).then_inc(x_done, 1)


def moe(nc, m, io, layer, nt):
    L = f"moe{layer}"
    with ExitStack() as ctx:
        def sb(name, shape, dt=F32):
            return ctx.enter_context(nc.sbuf_tensor(f"{L}_{name}", shape, dt))

        r = Memory()
        r.L, r.layer, r.nt = L, layer, nt
        r.gk = sb("gk", [P, nt, 8])
        r.posb = sb("posb", [P, nt, NE])
        r.V = sb("V", [P, nt, NE, 3], BF16)
        r.passes = sb("passes", [1, 4], I32)
        r.counts = sb("counts", [1, NE], I32)
        r.hf_done, r.y_done, r.gu_done = m.sem(f"{L}_hf_done"), m.sem(f"{L}_y_done"), m.sem(f"{L}_gu_done")
        r.xt_out, r.y_out = ([m.sem(f"{L}_{n}_out_{e}") for e in ("act", "dve")] for n in ("xt", "y"))
        r.s_free = m.sem(f"{L}_s_free")
        r.pass_done = m.sem(f"{L}_pass_done")
        route(nc, m, io, r)
        experts(nc, m, io, r)
        combine(nc, m, io, r)


def route(nc, m, io, r):
    nt, L = r.nt, r.L
    with ExitStack() as ctx:
        def sb(name, shape, dt=F32):
            return ctx.enter_context(nc.sbuf_tensor(f"{L}r_{name}", shape, dt))

        rw = sb("rw", [P, KC, NE])
        rb = sb("rb", [P, NE])
        tri = sb("tri", [P, P], BF16)
        ones = sb("ones", [P, P], BF16)
        trif = sb("trif", [P, P])
        low = sb("low", [P, GROUPS, GROUPS])
        pid = sb("pid", [P, 1])
        sc, bi, sel, G, t1, t2 = (sb(n, [P, nt, NE]) for n in ("sc", "bi", "sel", "G", "t1", "t2"))
        selb = sb("selb", [P, nt, NE], BF16)
        m8 = sb("m8", [P, nt, GROUPS, 8])
        gs = sb("gs", [P, nt, GROUPS])
        cmp1, cmp2 = sb("cmp1", [P, nt, GROUPS, GROUPS]), sb("cmp2", [P, nt, GROUPS, GROUPS])
        beat, gm, neg = (sb(n, [P, nt, GROUPS]) for n in ("beat", "gm", "neg"))
        top = sb("top", [P, nt, 8])
        v6 = sb("v6", [P, nt])
        need = sb("need", [P, nt])
        HALF = NE // 2
        sa, sbuf = sb("sa", [P, nt, HALF + NE]), sb("sb", [P, nt, HALF + NE])
        cnt = sb("cnt", [1, NE])
        mxc = sb("mxc", [1, 1])
        ge = sb("ge", [1, 4])
        npf = sb("npf", [1, 1])

        s = m.sem
        consts_in, ones_done, logits_done, scored = (s(f"{L}_{n}") for n in ("rconsts", "rones", "logits", "scored"))
        chain, sel_done, pos_done, route_done = (s(f"{L}_{n}") for n in ("rchain", "sel", "pos", "routed"))
        m.sh_in = s(f"{L}_sh_in")

        with nc.Block() as block:
            @block.sync
            def _(sp):
                sp.dma_start(rw[:], io["moe_router_w"][r.layer].rearrange("(p k) n -> p k n", p=P)).then_inc(consts_in, 16)
                sp.dma_start(rb[:], io["moe_router_b"][r.layer].partition_broadcast(P)).then_inc(consts_in, 16)
                sp.dma_start(trif[:], io["k_tri"]).then_inc(consts_in, 16)
                sp.dma_start(low[:], io["k_low"].partition_broadcast(P)).then_inc(consts_in, 16)
                sp.dma_start(pid[:], io["k_pid"]).then_inc(consts_in, 16)

            @block.gpsimd
            def _(pool):
                pool.sem_inc(r.hf_done, 2)
                pool.sem_inc(r.y_done, 2)
                pool.sem_inc(r.gu_done, 2)
                for i in range(2):
                    pool.sem_inc(r.xt_out[i], 1)
                    pool.sem_inc(r.y_out[i], 2)
                pool.sem_inc(r.s_free, UNROLL)
                pool.sem_inc(r.pass_done, 1)
                pool.memset(ones[:], 1.0).then_inc(ones_done, 1)
                pool.memset(sa[:], 0.0).then_inc(ones_done, 1)
                pool.memset(sbuf[:], 0.0).then_inc(ones_done, 1)

            @block.scalar
            def _(act):
                act.wait_ge(logits_done, 1)
                act.activation(sc[:], m.ps[:, 0, 0:nt * NE].rearrange("p (t e) -> p t e", t=nt), ACT.Sigmoid).then_inc(scored, 1)

            @block.tensor
            def _(pe):
                pe.wait_ge(consts_in, 80)
                for t in range(nt):
                    for k in range(KC):
                        mm = pe.matmul(m.ps[:, 0, t * NE:(t + 1) * NE], m.hT[:, k, t * P:(t + 1) * P], rw[:, k, :], start=(k == 0), stop=(k == KC - 1))
                mm.then_inc(logits_done, 1)
                pe.wait_ge(sel_done, 1)
                pe.wait_ge(ones_done, 3)
                for t in range(nt):
                    for q in range(t):
                        pe.matmul(m.ps[:, 1, t * NE:(t + 1) * NE], ones[:], selb[:, q, :], start=(q == 0), stop=False)
                    pe.matmul(m.ps[:, 1, t * NE:(t + 1) * NE], tri[:], selb[:, t, :], start=(t == 0), stop=True)
                for t in range(nt):
                    mm = pe.matmul(m.ps[:, 2, 0:NE], ones[:], selb[:, t, :], start=(t == 0), stop=(t == nt - 1))
                mm.then_inc(pos_done, 1)

            @block.vector
            def _(dve):
                done = [0]

                def link(ins):
                    done[0] += 1
                    ins.then_inc(chain, 1)
                    dve.wait_ge(chain, done[0])

                def scan(src, out):
                    link(dve.tensor_copy(sa[:, :, HALF:], src))
                    a, b, d = sa, sbuf, 1
                    while d <= HALF:
                        link(dve.tensor_tensor(b[:, :, HALF:] if d < HALF else out, a[:, :, HALF:], a[:, :, HALF - d:HALF + NE - d], ALU.add))
                        a, b, d = b, a, 2 * d

                dve.wait_ge(consts_in, 80)
                dve.wait_ge(ones_done, 3)
                link(dve.tensor_copy(tri[:], trif[:]))
                dve.wait_ge(scored, 1)
                for t in range(nt):
                    last = dve.tensor_tensor(bi[:, t, :], sc[:, t, :], rb[:], ALU.add)
                link(last)
                for t in range(nt):
                    for g in range(GROUPS):
                        last = dve.max(m8[:, t, g, :], bi[:, t, g * 8:(g + 1) * 8])
                link(last)
                link(dve.tensor_tensor(gs[:], m8[:, :, :, 0], m8[:, :, :, 1], ALU.add))
                for t in range(nt):
                    other = gs[:, t, :].unsqueeze(1).broadcast_to([P, GROUPS, GROUPS])
                    own = gs[:, t, :].unsqueeze(2).broadcast_to([P, GROUPS, GROUPS])
                    dve.tensor_tensor(cmp1[:, t], other, own, ALU.is_gt)
                    link(dve.tensor_tensor(cmp2[:, t], other, own, ALU.is_equal))
                    link(dve.tensor_tensor(cmp2[:, t], cmp2[:, t], low[:], ALU.mult))
                link(dve.tensor_tensor(cmp1[:], cmp1[:], cmp2[:], ALU.add))
                link(dve.tensor_reduce(beat[:], cmp1[:], AX.X, ALU.add))
                link(dve.tensor_scalar(gm[:], beat[:], float(TOPG), None, ALU.is_lt))
                link(dve.tensor_scalar(neg[:], gm[:], -1.0, BIG, ALU.add, ALU.mult))
                for t in range(nt):
                    bit = bi[:, t, :].rearrange("p (g e) -> p g e", g=GROUPS)
                    link(dve.tensor_tensor(bit, bit, gm[:, t, :].unsqueeze(2).broadcast_to([P, GROUPS, 8]), ALU.mult))
                    link(dve.tensor_tensor(bit, bit, neg[:, t, :].unsqueeze(2).broadcast_to([P, GROUPS, 8]), ALU.add))
                for t in range(nt):
                    last = dve.max(top[:, t, :], bi[:, t, :])
                link(last)
                for t in range(nt):
                    dve.tensor_scalar(t1[:, t, :], bi[:, t, :], top[:, t, TOPK - 1:TOPK], None, ALU.is_gt)
                    link(dve.tensor_scalar(t2[:, t, :], bi[:, t, :], top[:, t, TOPK - 1:TOPK], None, ALU.is_equal))
                link(dve.tensor_reduce(need[:], t1[:], AX.X, ALU.add))
                link(dve.tensor_scalar(need[:], need[:], -1.0, float(TOPK), ALU.mult, ALU.add))
                scan(t2[:], G[:])
                for t in range(nt):
                    link(dve.tensor_scalar(G[:, t, :], G[:, t, :], need[:, t:t + 1], None, ALU.is_le))
                link(dve.tensor_tensor(t2[:], t2[:], G[:], ALU.mult))
                link(dve.tensor_tensor(sel[:], t1[:], t2[:], ALU.add))
                dve.tensor_copy(selb[:], sel[:]).then_inc(sel_done, 1)
                link(dve.tensor_tensor(G[:], sc[:], sel[:], ALU.mult))
                link(dve.tensor_reduce(v6[:], G[:], AX.X, ALU.add))
                link(dve.reciprocal(need[:], v6[:]))
                for t in range(nt):
                    link(dve.tensor_scalar(G[:, t, :], G[:, t, :], need[:, t:t + 1], RSCALE, ALU.mult, ALU.mult))
                scan(sel[:], t1[:])
                link(dve.tensor_tensor(t1[:], t1[:], sel[:], ALU.mult))
                link(dve.tensor_scalar(t1[:], t1[:], -1.0, None, ALU.add))
                for k in range(TOPK):
                    link(dve.scalar_tensor_tensor(t2[:], t1[:], float(k), G[:], ALU.is_equal, ALU.mult))
                    link(dve.tensor_reduce(r.gk[:, :, k:k + 1].rearrange("p t o -> p (t o)"), t2[:], AX.X, ALU.add))
                dve.tensor_copy(r.V[:, :, :, 2], t1[:])
                for t in range(nt):
                    dve.tensor_scalar(r.V[:, t, :, 1], sel[:, t, :], 0.0, float(t - EMPTY // P), ALU.mult, ALU.add)
                    link(dve.tensor_scalar(r.V[:, t, :, 0], sel[:, t, :], 0.0, pid[:], ALU.mult, ALU.add))
                dve.wait_ge(pos_done, 1)
                for t in range(nt):
                    link(dve.scalar_tensor_tensor(r.posb[:, t, :], m.ps[:, 1, t * NE:(t + 1) * NE], float(P + 1), sel[:, t, :], ALU.add, ALU.mult))
                link(dve.tensor_scalar(r.posb[:], r.posb[:], -1.0, None, ALU.add))
                link(dve.tensor_copy(cnt[:], m.ps[0:1, 2, 0:NE]))
                link(dve.tensor_copy(r.counts[:], cnt[:]))
                link(dve.tensor_reduce(mxc[:], cnt[:], AX.X, ALU.max))
                for i in range(4):
                    link(dve.tensor_scalar(ge[:, i:i + 1], mxc[:], float(P * i) if i else -1.0, None, ALU.is_gt))
                link(dve.tensor_reduce(npf[:], ge[:], AX.X, ALU.add))
                dve.tensor_copy(r.passes[:, 0:1], npf[:]).then_inc(route_done, 1)
                dve.wait_ge(route_done, 1)


def experts(nc, m, io, r):
    nt, L, layer = r.nt, r.L, r.layer
    with ExitStack() as ctx:
        def sb(name, shape, dt=F32):
            return ctx.enter_context(nc.sbuf_tensor(f"{L}e_{name}", shape, dt))

        iota = sb("iota", [P, P])
        iob = sb("iob", [P, P], BF16)
        S = sb("S", [P, UNROLL, nt, P], BF16)
        idf = sb("idf", [P, 3, NE])
        idg, ids = sb("idg", [P, NE], I32), sb("ids", [P, NE], I32)
        ig, isc = sb("ig", [P, UNROLL], I32), sb("isc", [P, UNROLL], I32)
        xg = sb("xg", [P, UNROLL, D])
        xT = sb("xT", [P, 2, KC, P])
        sl = sb("sl", [P, 2, 2 * P])
        hf = sb("hf", [P, 2, 2 * P])
        y = sb("y", [P, 2, D])
        shs = sb("shs", [P, 512])
        shh = sb("shh", [P, 2, 512])

        def wg(s):
            return m.W[:, s, 0:2048].rearrange("p (k n) -> p k n", k=KC)

        def wu(s):
            return m.W[:, s, 2048:4096].rearrange("p (k n) -> p k n", k=KC)

        def wd(s):
            return m.W[:, s, 4096:6144].rearrange("p (k n) -> p k n", k=2)

        q = m.sem
        consts_in, sh_in, iob_done = q(f"{L}e_consts"), q(f"{L}e_sh_in"), q(f"{L}e_iob")
        sh_g, sh_u, sh_s, sh_h, sh_y, sh_out = (q(f"{L}e_{n}") for n in ("sh_g", "sh_u", "sh_s", "sh_h", "sh_y", "sh_out"))
        w_in = [q(f"{L}e_w_in{s}") for s in range(UNROLL)]
        sh_free = q(f"{L}e_sh_free")
        shifted, picked, id_done, id_step, id_ready = (q(f"{L}e_{n}") for n in ("shifted", "picked", "id_done", "id_step", "id_ready"))
        hf_done, y_done, gu_done, xt_out, y_out, s_free, pass_done = r.hf_done, r.y_done, r.gu_done, r.xt_out, r.y_out, r.s_free, r.pass_done
        scattered = [q(f"{L}e_scattered{i}") for i in range(2)]
        pool_steps = q(f"{L}e_pool_steps")
        cleared, ig_done, is_done = (q(f"{L}e_{n}") for n in ("cleared", "ig_done", "is_done"))
        gathered = [q(f"{L}e_gathered{s}") for s in range(UNROLL)]
        xt_done, sl_done = q(f"{L}e_xt_done"), q(f"{L}e_sl_done")

        GI = NE // UNROLL
        HT = nt * P

        def g_is_first(g):
            return isinstance(g, int) and g == 0

        def load(sp, e, s, layer=layer):
            sp.dma_start(wg(s), io["moe_w_gate"][layer, e].rearrange("(p k) n -> p k n", p=P)).then_inc(w_in[s], 16)
            sp.dma_start(wu(s), io["moe_w_up"][layer, e].rearrange("(p k) n -> p k n", p=P)).then_inc(w_in[s], 16)
            sp.dma_start(wd(s), io["moe_w_down"][layer, e].rearrange("(k p) n -> p k n", p=P)).then_inc(w_in[s], 16)

        with nc.Block() as block:
            @block.sync
            def _(sp):
                sp.dma_start(wg(0), io["moe_sh_gate"][layer].rearrange("(p k) n -> p k n", p=P)).then_inc(sh_in, 16)
                sp.dma_start(wu(0), io["moe_sh_up"][layer].rearrange("(p k) n -> p k n", p=P)).then_inc(sh_in, 16)
                sp.dma_start(wd(0), io["moe_sh_down"][layer].rearrange("(k p) n -> p k n", p=P)).then_inc(sh_in, 16)
                sp.dma_start(iota[:], io["k_iota"].partition_broadcast(P)).then_inc(consts_in, 16)
                for s in (1, 2, 3, 0):
                    if s == 0:
                        sp.wait_ge(sh_free, 1)
                    load(sp, s, s)
                npass = sp.value_load(r.passes[0:1, 0:1], min_val=1, max_val=4)
                with sp.Fori(1, npass * GI) as g:
                    for s in range(UNROLL):
                        sp.wait_ge(y_done, g * UNROLL + s - 1)
                        load(sp, (g % GI) * UNROLL + s, s)

            @block.tensor
            def _(pe):
                pe.wait_ge(sh_in, 48)
                for f in range(2):
                    for w, b in ((wg(0), 0), (wu(0), 1)):
                        if f:
                            pe.wait_ge(sh_h, 1)
                        for k in range(KC):
                            mm = pe.matmul(m.ps[:, b, 0:HT], w[:, k, f * P:(f + 1) * P], m.hT[:, k, 0:HT], start=(k == 0), stop=(k == KC - 1))
                        mm.then_inc(sh_g if b == 0 else sh_u, 1)
                pe.wait_ge(sh_h, 2)
                for t in range(nt):
                    if t >= 2:
                        pe.wait_ge(sh_out, t - 1)
                    for n in range(2):
                        for f in range(2):
                            mm = pe.matmul(m.ps[:, 2 + 2 * (t % 2) + n, :], shh[:, f, t * P:(t + 1) * P], wd(0)[:, f, n * 512:n * 512 + 512], start=(f == 0), stop=(f == 1))
                    mm.then_inc(sh_y, 1)
                pe.wait_ge(sh_y, nt)
                pe.sem_inc(sh_free, 1)
                pe.wait_ge(sh_out, nt)

                npass = pe.value_load(r.passes[0:1, 0:1], min_val=1, max_val=4)
                with pe.Fori(0, npass) as b:
                    with pe.Fori(0, GI) as i:
                        for s in range(UNROLL):
                            pe.wait_ge(picked, (b * NE + i * UNROLL + s + 1))
                            for t in range(nt):
                                mm = pe.matmul(m.ps[:, 0, bass.ds((i * UNROLL + s) * 3, 3)], S[:, s, t, :], r.V[:, t, bass.ds(i * UNROLL + s, 1), :],
                                               start=(t == 0), stop=(t == nt - 1))
                            mm.then_inc(id_done, 1)

                    def turn(n, s):
                        pe.wait_ge(gathered[s], (b * GI + n // UNROLL + 1) * 16 if isinstance(n, int) else (b * GI + n[0] + 1) * 16)
                        for half in xt_out:
                            pe.wait_ge(half, b * NE + at(n) + 1)
                        for k in range(KC):
                            mm = pe.transpose(m.ps[:, k // 4, (k % 4) * P:(k % 4 + 1) * P], xg[:, s, k * P:(k + 1) * P], m.ident[:])
                        mm.then_inc(xt_done, 1)

                    def at(n):
                        return n if isinstance(n, int) else n[0] * UNROLL + n[1]

                    def up(n, s):
                        g = n // UNROLL if isinstance(n, int) else n[0]
                        pe.wait_ge(w_in[s], (b * GI + g + 1) * 48)
                        for half in xt_out:
                            pe.wait_ge(half, b * NE + at(n) + 2)
                        pe.wait_ge(hf_done, b * NE + at(n) + 1)
                        for c in range(4):
                            w = wg(s) if c < 2 else wu(s)
                            for k in range(KC):
                                mm = pe.matmul(m.ps[:, 2 + s % 2, c * P:(c + 1) * P], w[:, k, (c % 2) * P:(c % 2 + 1) * P], xT[:, s % 2, k, :],
                                               start=(k == 0), stop=(k == KC - 1))
                        mm.then_inc(gu_done, 1)

                    def down(n, s):
                        pe.wait_ge(hf_done, b * NE + at(n) + 3)
                        for half in y_out:
                            pe.wait_ge(half, b * NE + at(n) + 1)
                        for c in range(2):
                            for k in range(2):
                                mm = pe.matmul(m.ps[:, 4 + 2 * (s % 2) + c, :], hf[:, s % 2, k * P:(k + 1) * P], wd(s)[:, k, c * 512:c * 512 + 512], start=(k == 0), stop=(k == 1))
                        mm.then_inc(y_done, 1)

                    turn(0, 0)
                    up(0, 0)
                    turn(1, 1)
                    with pe.Fori(0, GI - 1) as i:
                        for s in range(UNROLL):
                            up((i + (s + 1) // UNROLL, (s + 1) % UNROLL), (s + 1) % UNROLL)
                            turn((i + (s + 2) // UNROLL, (s + 2) % UNROLL), (s + 2) % UNROLL)
                            down((i, s), s)
                    for n in range(NE - UNROLL, NE):
                        if n + 1 < NE:
                            up(n + 1, (n + 1) % UNROLL)
                        if n + 2 < NE:
                            turn(n + 2, (n + 2) % UNROLL)
                        down(n, n % UNROLL)

            @block.vector
            def _(dve):
                for f in range(2):
                    dve.wait_ge(sh_s, f + 1)
                    dve.wait_ge(sh_u, f + 1)
                    dve.tensor_tensor(shh[:, f, 0:HT], shs[:, 0:HT], m.ps[:, 1, 0:HT], ALU.mult).then_inc(sh_h, 1)
                dve.wait_ge(consts_in, 16)
                dve.tensor_copy(iob[:], iota[:]).then_inc(iob_done, 1)
                for t in range(nt):
                    dve.wait_ge(sh_y, t + 1)
                    dve.tensor_copy(m.hT[:].rearrange("p a b -> p (a b)")[:, t * D:(t + 1) * D], bank2(m, 2 + 2 * (t % 2))).then_inc(sh_out, 1)
                dve.wait_ge(iob_done, 1)
                npass = dve.value_load(r.passes[0:1, 0:1], min_val=1, max_val=4)
                with dve.Fori(0, npass) as b:
                    dve.tensor_scalar(r.posb[:], r.posb[:], -float(P), None, ALU.add).then_inc(shifted, 1)
                    with dve.Fori(0, GI) as i:
                        dve.wait_ge(shifted, b + 1)
                        for s in range(UNROLL):
                            dve.wait_ge(s_free, b * NE + i * UNROLL + s + 1)
                            for t in range(nt):
                                last = dve.tensor_scalar(S[:, s, t, :], iob[:], r.posb[:, t, bass.ds(i * UNROLL + s, 1)], None, ALU.is_equal)
                            last.then_inc(picked, 1)
                            if s == UNROLL - 1:
                                dve.wait_ge(id_done, b * NE + i * UNROLL + UNROLL)
                                dve.sem_inc(s_free, UNROLL)
                    tab = m.ps[:, 0, 0:3 * NE].rearrange("p (e c) -> p c e", c=3)
                    dve.tensor_scalar(idf[:, 0, :], tab[:, 1, :], float(P), float(EMPTY), ALU.mult, ALU.add).then_inc(id_step, 1)
                    dve.wait_ge(id_step, b * 3 + 1)
                    dve.tensor_tensor(idf[:, 1, :], idf[:, 0, :], tab[:, 0, :], ALU.add).then_inc(id_step, 1)
                    dve.wait_ge(id_step, b * 3 + 2)
                    dve.scalar_tensor_tensor(idf[:, 2, :], tab[:, 2, :], float(ROWS), idf[:, 1, :], ALU.mult, ALU.add).then_inc(id_step, 1)
                    dve.wait_ge(id_step, b * 3 + 3)
                    dve.tensor_copy(idg[:], idf[:, 1, :]).then_inc(id_ready, 1)
                    dve.tensor_copy(ids[:], idf[:, 2, :]).then_inc(id_ready, 1)
                    dve.wait_ge(id_ready, b * 2 + 2)

                    def xt_copy(g, s):
                        dve.wait_ge(xt_done, b * NE + g * UNROLL + s + 1)
                        dve.wait_ge(gu_done, b * NE + g * UNROLL + s + 1)
                        dve.tensor_copy(xT[:, s % 2, 4:8, :], m.ps[:, 1, :].rearrange("p (k t) -> p k t", k=4)).then_inc(xt_out[1], 1)

                    def hidden(g, s):
                        dve.wait_ge(sl_done, b * NE + g * UNROLL + s + 1)
                        dve.wait_ge(y_done, b * NE + g * UNROLL + s + 1)
                        dve.tensor_tensor(hf[:, s % 2, :], sl[:, s % 2, :], m.ps[:, 2 + s % 2, 2 * P:4 * P], ALU.mult).then_inc(hf_done, 1)

                    def y_copy(g, s):
                        dve.wait_ge(y_done, b * NE + g * UNROLL + s + 3)
                        if not (g_is_first(g) and s < 2):
                            dve.wait_ge(scattered[s % 2], (b * (NE // 2) + g * 2 + s // 2) * 16)
                        dve.tensor_copy(y[:, s % 2, 512:1024], m.ps[:, 5 + 2 * (s % 2), :]).then_inc(y_out[1], 1)

                    dve.wait_ge(pass_done, b + 1)
                    xt_copy(0, 0)
                    hidden(0, 0)
                    xt_copy(0, 1)

                    def group(g):
                        for s in range(UNROLL):
                            hidden(g + (s + 1) // UNROLL, (s + 1) % UNROLL)
                            xt_copy(g + (s + 2) // UNROLL, (s + 2) % UNROLL)
                            y_copy(g, s)

                    group(0)
                    with dve.Fori(1, GI - 1) as i:
                        group(i)
                    for s in range(UNROLL):
                        if s + 1 < UNROLL:
                            hidden(GI - 1, s + 1)
                        if s + 2 < UNROLL:
                            xt_copy(GI - 1, s + 2)
                        y_copy(GI - 1, s)

            @block.scalar
            def _(act):
                for f in range(2):
                    act.wait_ge(sh_g, f + 1)
                    if f:
                        act.wait_ge(sh_h, f)
                    act.activation(shs[:, 0:HT], m.ps[:, 0, 0:HT], ACT.Silu).then_inc(sh_s, 1)
                npass = act.value_load(r.passes[0:1, 0:1], min_val=1, max_val=4)
                with act.Fori(0, npass) as b:
                    def xt_copy(g, s):
                        act.wait_ge(xt_done, b * NE + g * UNROLL + s + 1)
                        act.wait_ge(gu_done, b * NE + g * UNROLL + s + 1)
                        act.activation(xT[:, s % 2, 0:4, :], m.ps[:, 0, :].rearrange("p (k t) -> p k t", k=4), ACT.Copy).then_inc(xt_out[0], 1)

                    def gate(g, s):
                        act.wait_ge(gu_done, b * NE + g * UNROLL + s + 3)
                        act.wait_ge(hf_done, b * NE + g * UNROLL + s + 1)
                        act.activation(sl[:, s % 2, :], m.ps[:, 2 + s % 2, 0:2 * P], ACT.Silu).then_inc(sl_done, 1)

                    def y_copy(g, s):
                        act.wait_ge(y_done, b * NE + g * UNROLL + s + 3)
                        if not (g_is_first(g) and s < 2):
                            act.wait_ge(scattered[s % 2], (b * (NE // 2) + g * 2 + s // 2) * 16)
                        act.activation(y[:, s % 2, 0:512], m.ps[:, 4 + 2 * (s % 2), :], ACT.Copy).then_inc(y_out[0], 1)

                    act.wait_ge(pass_done, b + 1)
                    xt_copy(0, 0)
                    gate(0, 0)
                    xt_copy(0, 1)

                    def group(g):
                        for s in range(UNROLL):
                            gate(g + (s + 1) // UNROLL, (s + 1) % UNROLL)
                            xt_copy(g + (s + 2) // UNROLL, (s + 2) % UNROLL)
                            y_copy(g, s)

                    group(0)
                    with act.Fori(1, GI - 1) as i:
                        group(i)
                    for s in range(UNROLL):
                        if s + 1 < UNROLL:
                            gate(GI - 1, s + 1)
                        if s + 2 < UNROLL:
                            xt_copy(GI - 1, s + 2)
                        y_copy(GI - 1, s)

            @block.gpsimd
            def _(pool):
                pool.memset(xg[:], 0.0).then_inc(cleared, 1)
                pool.wait_ge(cleared, 1)
                npass = pool.value_load(r.passes[0:1, 0:1], min_val=1, max_val=4)
                with pool.Fori(0, npass) as b:
                    pool.wait_ge(id_ready, b * 2 + 2)

                    def gather(g, s):
                        if not g_is_first(g):
                            for half in xt_out:
                                pool.wait_ge(half, b * NE + g * UNROLL + s + 2 - UNROLL)
                        pool.sem_inc(pool_steps, 1)
                        pool.tensor_copy(ig[:, s:s + 1], idg[:, bass.ds(g * UNROLL + s, 1)]).then_inc(ig_done, 1)
                        pool.wait_ge(ig_done, b * NE + g * UNROLL + s + 1)
                        pool.sem_inc(pool_steps, 1)
                        pool.indirect_dma_start(out=xg[:, s, :], out_offset=None, in_=m.H2, in_offset=bass.IndirectOffsetOnAxis(ap=ig[:, s:s + 1], axis=0),
                                                bounds_check=ROWS - 1, oob_is_err=False, compute_op=ALU.bypass).then_inc(gathered[s], 16)

                    def scatter(g, s):
                        for half in y_out:
                            pool.wait_ge(half, b * NE + g * UNROLL + s + 3)
                        pool.sem_inc(pool_steps, 1)
                        pool.tensor_copy(isc[:, s:s + 1], ids[:, bass.ds(g * UNROLL + s, 1)]).then_inc(is_done, 1)
                        pool.wait_ge(is_done, b * NE + g * UNROLL + s + 1)
                        pool.sem_inc(pool_steps, 1)
                        pool.indirect_dma_start(out=m.Y6, out_offset=bass.IndirectOffsetOnAxis(ap=isc[:, s:s + 1], axis=0), in_=y[:, s % 2, :], in_offset=None,
                                                bounds_check=TOPK * ROWS - 1, oob_is_err=False, compute_op=ALU.bypass).then_inc(scattered[s % 2], 16)

                    for s in range(UNROLL):
                        gather(0, s)
                    scatter(0, 0)
                    with pool.Fori(1, GI) as i:
                        for s in range(UNROLL):
                            gather(i, s)
                            if s < UNROLL - 1:
                                scatter(i - 1, s + 1)
                            else:
                                scatter(i, 0)
                    for s in range(1, UNROLL):
                        scatter(GI - 1, s)
                    for i in range(2):
                        pool.wait_ge(scattered[i], (b * (NE // 2) + NE // 2) * 16)
                    pool.sem_inc(pass_done, 1)


def combine(nc, m, io, r):
    nt, L = r.nt, r.L
    last_layer = r.layer == 1
    with ExitStack() as ctx:
        def sb(name, shape, dt=F32):
            return ctx.enter_context(nc.sbuf_tensor(f"{L}c_{name}", shape, dt))

        rows = m.W[:].rearrange("p a b -> p (a b)")[:, 0:2 * TOPK * D].rearrange("p (i k d) -> p i k d", i=2, k=TOPK)
        G = sb("G", [P, 2, D])
        junk = sb("junk", [P, D])
        ssq, std, rstd = (sb(n, [P, nt]) for n in ("ssq", "std", "rstd"))
        q = m.sem
        gate_in = q(f"{L}c_gate_in")
        rows_in = [q(f"{L}c_rows_in{i}") for i in range(2)]
        added, summed, squared, std_done, rec_done, scaled, x_done, stored = (
            q(f"{L}c_{n}") for n in ("added", "summed", "squared", "std_done", "rec_done", "scaled", "x_done", "stored"))
        shared = m.hT[:].rearrange("p a b -> p (a b)")
        streams = 2 if nt > 2 else 1

        with nc.Block() as block:
            @block.sync
            def _(sp):
                for s in range(streams):
                    sp.dma_start(G[:, s, :], m.MOD[r.layer, 5, s, :].partition_broadcast(P)).then_inc(gate_in, 16)
                for t in range(nt):
                    if t >= 2:
                        sp.wait_ge(summed, t - 1)
                    sp.dma_start(rows[:, t % 2], m.Y6.rearrange("(k t) d -> t k d", k=TOPK)[t * P:(t + 1) * P]).then_inc(rows_in[t % 2], 16)
                if last_layer:
                    for t in range(nt):
                        sp.wait_ge(x_done, t + 1)
                        sp.dma_start(io["out"][0, t * P:(t + 1) * P, :], m.X[:, t, :]).then_inc(stored, 16)
                    sp.wait_ge(stored, 16 * nt)

            @block.vector
            def _(dve):
                n = 0
                for t in range(nt):
                    acc = shared[:, t * D:(t + 1) * D]
                    dve.wait_ge(rows_in[t % 2], 16 * (t // 2 + 1))
                    for k in range(TOPK):
                        last = dve.scalar_tensor_tensor(acc, rows[:, t % 2, k, :], r.gk[:, t, k:k + 1], acc, ALU.mult, ALU.add)
                        if k < TOPK - 1:
                            last.then_inc(added, 1)
                            n += 1
                            dve.wait_ge(added, n)
                        else:
                            last.then_inc(summed, 1)
                dve.wait_ge(gate_in, 16 * streams)
                for t in range(nt):
                    acc = shared[:, t * D:(t + 1) * D]
                    dve.wait_ge(std_done, t + 1)
                    dve.reciprocal(rstd[:, t:t + 1], std[:, t:t + 1]).then_inc(rec_done, 1)
                    dve.wait_ge(rec_done, t + 1)
                    dve.scalar_tensor_tensor(acc, acc, rstd[:, t:t + 1], G[:, t // 2, :], ALU.mult, ALU.mult).then_inc(scaled, 1)
                    dve.wait_ge(scaled, t + 1)
                    dve.tensor_tensor(m.X[:, t, :], m.X[:, t, :], acc, ALU.add).then_inc(x_done, 1)

            @block.scalar
            def _(act):
                for t in range(nt):
                    act.wait_ge(summed, t + 1)
                    if t:
                        act.wait_ge(squared, t)
                    act.activation(junk[:], shared[:, t * D:(t + 1) * D], ACT.Square, accum_out=ssq[:, t:t + 1]).then_inc(squared, 1)
                    act.wait_ge(squared, t + 1)
                    act.activation(std[:, t:t + 1], ssq[:, t:t + 1], ACT.Sqrt, bias=m.eps[:], scale=1.0 / D).then_inc(std_done, 1)


def build(nc, io, stop=99):
    m = Memory()
    with ExitStack() as ctx:
        start(nc, ctx, m)
        steps = [
            lambda: conditioning(nc, m, io),
            lambda: modulate(nc, m, io, "m00", 0, 0, range(4), False),
            lambda: mixer(nc, m, io),
            lambda: modulate(nc, m, io, "m01", 0, 1, range(4), True),
            lambda: moe(nc, m, io, 0, 4),
            lambda: modulate(nc, m, io, "m10", 1, 0, range(4), False),
            lambda: attention(nc, m, io),
            lambda: modulate(nc, m, io, "m11", 1, 1, range(2), True),
            lambda: moe(nc, m, io, 1, 2),
        ]
        for n, step in enumerate(steps[:stop]):
            step()
            if n == 4:
                nc.clear_and_free_semaphores(m.used)
                m.used.clear()
                nc.all_engine_barrier()


def _constants():
    f = np.float32
    k = {}
    k["k_ident"] = np.eye(P, dtype=f)

    def dft(n):
        a = 2 * np.pi * (np.outer(np.arange(n), np.arange(n)) % n) / n
        return np.cos(a) / np.sqrt(n), np.sin(a) / np.sqrt(n)

    c, s = dft(P)
    k["k_fch"] = np.concatenate([c, s], 1).astype(f)
    c, s = dft(SEQ)
    k["k_fseq"] = np.concatenate([c, -s], 1).reshape(2, P, 2 * SEQ).transpose(1, 0, 2).astype(f)
    k["k_gmean"] = (np.kron(np.eye(P // CONV_GROUP), np.ones((CONV_GROUP, CONV_GROUP))) / CONV_GROUP).astype(f)
    grid = 64
    tok = np.arange(SEQ)
    n_freq = QK // 4
    inv = np.power(f(10000.0), -np.arange(n_freq, dtype=f) / f(n_freq)).astype(f)
    ang = np.concatenate([(tok // grid).astype(f)[:, None] * inv, (tok % grid).astype(f)[:, None] * inv], -1)
    ang = np.concatenate([ang, ang, ang, ang], -1).T
    k["k_cos"], k["k_sin"] = np.cos(ang).astype(f), np.sin(ang).astype(f)
    r = np.zeros((QK, QK), f)
    h = QK // 2
    for i in range(h):
        r[i + h, i] = -1.0
        r[i, i + h] = 1.0
    k["k_rot"] = np.kron(np.eye(2, dtype=f), r).astype(f)
    k["k_tri"] = np.triu(np.ones((P, P), f), 1)
    k["k_low"] = np.tril(np.ones((GROUPS, GROUPS), f), -1)
    k["k_pid"] = np.arange(P, dtype=f)[:, None]
    k["k_iota"] = np.arange(P, dtype=f)
    return k


_INS = ["x", "c", "ctx", "c_ctx", "ada_w", "ada_b", "norm_g", "cf_w_in", "cf_conv_w", "cf_conv_b", "cf_ln_g", "cf_ln_b", "cf_w_out",
        "da_w_qkv", "da_lambda", "da_subln_g", "da_w_out", "moe_router_w", "moe_router_b", "moe_w_gate", "moe_w_up", "moe_w_down",
        "moe_sh_gate", "moe_sh_up", "moe_sh_down"]


def kernel(**inputs):
    import concourse.bacc as _bacc
    from concourse.bass_utils import run_bass_kernel_spmd as _run

    nc = _bacc.Bacc("TRN2", target_bir_lowering=False, num_devices=1)
    arrays, io = {}, {}
    data = {n: np.ascontiguousarray(inputs[n]) for n in _INS} | _constants()
    for name, a in data.items():
        a = np.ascontiguousarray(a)
        arrays[f"in_{name}"] = a
        io[name] = nc.dram_tensor(f"in_{name}", a.shape, mybir.dt.from_np(a.dtype), kind="ExternalInput").ap()
    io["out"] = nc.dram_tensor("out_x", (1, SEQ, D), F32, kind="ExternalOutput").ap()
    build(nc, io)
    r = _run(nc, [arrays], core_ids=[0])
    return r.results[0]["out_x"]
```

```python
import math
from contextlib import ExitStack

import concourse.bass as bass
import numpy as np
from concourse import mybir

F32 = mybir.dt.float32
BF16 = mybir.dt.bfloat16
I32 = mybir.dt.int32
ALU = mybir.AluOpType
ACT = mybir.ActivationFunctionType
AX = mybir.AxisListType

P = 128
D = 1024
KC = D // P
SEQ = 256
TT = 2 * SEQ // P
EPS = 1e-6
CONV_CH, CONV_W, CONV_GROUP = 512, 31, 64
PAD = CONV_W // 2
CJ = CONV_CH // P
MIX_IN = 1536
HEADS, QK = 8, 64
NE, GROUPS, TOPG, TOPK, FF = 64, 8, 4, 6, 256
RSCALE = 2.5
ROWS = 2 * SEQ
EMPTY = 4096
BIG = 1e30
UNROLL = 4
SMALL = 64

BATCHES = ((0, 0, 2), (0, 2, 4), (1, 0, 6))
PART = 256


class Memory:
    pass


def start(nc, ctx, m):

    def sb(name, shape, dt=F32):
        return ctx.enter_context(nc.sbuf_tensor(name, shape, dt))

    m.X = sb("X", [P, TT, D])
    m.hT = sb("hT", [P, KC, 2 * SEQ])
    m.W = sb("W", [P, UNROLL, 3 * 2048])
    m.ident = sb("ident", [P, P])
    m.eps = sb("eps", [P, 1])
    m.ps = ctx.enter_context(nc.psum_tensor("ps", [P, 8, 512], F32))
    m.used = []

    def sem(name):
        m.used.append(nc.alloc_semaphore(name))
        return m.used[-1]

    m.sem = sem
    m.RAW = nc.dram_tensor("raw_scratch", [2, 2, 6 * D], F32).ap()
    m.MOD = nc.dram_tensor("mod_scratch", [2, 6, 2, D], F32).ap()
    m.H2 = nc.dram_tensor("h2_scratch", [ROWS, D], F32).ap()
    m.TAB = nc.dram_tensor("table_scratch", [ROWS * NE, 2], I32).ap()
    m.Y6 = nc.dram_tensor("y6_scratch", [TOPK * ROWS, D], F32).ap()


def modulation_buffers(nc, ctx, m):
    def sb(name, shape):
        return ctx.enter_context(nc.sbuf_tensor(name, shape, F32))

    m.cS = sb("cS", [P, 2, KC])
    m.one = sb("ada_one", [P, len(BATCHES)])
    m.brow = sb("ada_brow", [P, len(BATCHES), P])
    m.grow = sb("ada_grow", [P, len(BATCHES), P])
    m.raw = sb("ada_raw", [2, 4, PART])
    m.trow = sb("ada_trow", [P, P])
    m.mrow = sb("ada_mrow", [P, P])
    m.orow = sb("ada_orow", [P, len(BATCHES), P])


def bank2(m, b):
    return m.ps[:, b:b + 2, :].rearrange("p a n -> p (a n)")


def ada_load(sp, io, b, h, slot, done):
    layer, v0, _ = BATCHES[b]
    c0 = v0 * D + h * PART
    sp.dma_start(slot, io["ada_w"][layer].rearrange("(p k) n -> p k n", p=P)[:, :, c0:c0 + PART]).then_inc(done, 16)


def ada_product(pe, m, slot, bank):
    for k in range(KC):
        mm = pe.matmul(m.ps[0:2, bank, 0:PART], m.cS[:, :, k], slot[:, k, :], start=(k == 0), stop=(k == KC - 1))
    return mm


def ada_store(sp, m, b, h, i, done):
    layer, v0, _ = BATCHES[b]
    c0 = v0 * D + h * PART
    sp.dma_start(m.RAW[layer, :, c0:c0 + PART], m.raw[:, i % 4, :]).then_inc(done, 16)


def ada_reload(eng, m, b, done):
    layer, v0, nv = BATCHES[b]
    for s in range(2):
        eng.dma_start(m.trow[s * 8 * nv:(s + 1) * 8 * nv, :], m.RAW[layer, s, v0 * D:(v0 + nv) * D].rearrange("(j n) -> j n", n=P)).then_inc(done, 16)


def ada_rows(dve, m, b, biased, row_done, n):
    rows = 16 * BATCHES[b][2]
    dve.scalar_tensor_tensor(m.mrow[0:rows, :], m.trow[0:rows, :], m.one[0:rows, b:b + 1], m.brow[0:rows, b, :], ALU.add, ALU.add).then_inc(biased, 1)
    dve.wait_ge(biased, n)
    dve.tensor_tensor(m.orow[0:rows, b, :], m.mrow[0:rows, :], m.grow[0:rows, b, :], ALU.mult).then_inc(row_done, 1)


def ada_publish(eng, m, b, done):
    layer, v0, nv = BATCHES[b]
    for s in range(2):
        eng.dma_start(m.MOD[layer, v0:v0 + nv, s, :].rearrange("v (j n) -> v j n", n=P),
                      m.orow[s * 8 * nv:(s + 1) * 8 * nv, b, :]).then_inc(done, 16)


def conditioning(nc, m, io):
    with ExitStack() as ctx:
        SLOTS = 6
        cT = ctx.enter_context(nc.sbuf_tensor("cT", [P, 2, KC], F32))
        ring = m.W[:, 0:2, :].rearrange("p a b -> p (a b)").rearrange("p (s k n) -> p s k n", s=SLOTS, k=KC)
        PARTS = BATCHES[0][2] * D // PART
        c_in, params_in, ones_done = m.sem("ada_c_in"), m.sem("ada_params_in"), m.sem("ada_ones_done")
        part_in = [m.sem(f"ada_part_in{s}") for s in range(SLOTS)]
        part_used, silu_done, raw_out = m.sem("ada_part_used"), m.sem("ada_silu_done"), m.sem("ada_raw_out")
        raw_stored = [m.sem(f"ada_raw_stored{s}") for s in range(4)]
        reloaded, biased, row_done, stored = m.sem("ada_reloaded"), m.sem("ada_biased"), m.sem("ada_row_done"), m.sem("ada_stored")
        m.x_in, m.ident_in = m.sem("x_in"), m.sem("ident_in")
        eps_done = m.sem("eps_done")

        with nc.Block() as block:
            @block.sync
            def _(sp):
                sp.dma_start(cT[:, 0, :], io["c"].rearrange("o (p k) -> p (o k)", p=P)).then_inc(c_in, 16)
                sp.dma_start(cT[:, 1, :], io["c_ctx"].rearrange("(p k) -> p k", p=P)).then_inc(c_in, 16)
                for h in range(PARTS):
                    if h >= SLOTS:
                        sp.wait_ge(part_used, h - SLOTS + 1)
                    ada_load(sp, io, 0, h, ring[:, h % SLOTS], part_in[h % SLOTS])
                sp.dma_start(m.ident[:], io["k_ident"]).then_inc(m.ident_in, 16)
                sp.dma_start(m.X[:, 0:2, :], io["x"].rearrange("b (t p) d -> p (b t) d", p=P)).then_inc(m.x_in, 16)
                sp.dma_start(m.X[:, 2:4, :], io["ctx"].rearrange("b (t p) d -> p (b t) d", p=P)).then_inc(m.x_in, 16)
                for h in range(PARTS):
                    sp.wait_ge(raw_out, h + 1)
                    ada_store(sp, m, 0, h, h, raw_stored[h % 4])
                for i in range(4):
                    sp.wait_ge(raw_stored[i], 16 * (PARTS // 4))
                ada_reload(sp, m, 0, reloaded)
                sp.wait_ge(row_done, 1)
                ada_publish(sp, m, 0, stored)
                sp.wait_ge(m.x_in, 32)
                sp.wait_ge(m.ident_in, 16)
                sp.wait_ge(stored, 32)

            @block.gpsimd
            def _(pool):
                pool.memset(m.eps[:], EPS).then_inc(eps_done, 1)
                pool.memset(m.grow[:], 1.0).then_inc(ones_done, 1)
                pool.wait_ge(eps_done, 1)

            @block.scalar
            def _(act):
                act.wait_ge(c_in, 32)
                act.activation(m.cS[:], cT[:], ACT.Silu).then_inc(silu_done, 1)
                act.wait_ge(ones_done, 1)
                for b, (layer, v0, nv) in enumerate(BATCHES):
                    for s in range(2):
                        r0 = s * 8 * nv
                        act.dma_start(m.brow[r0:r0 + 8 * nv, b, :], io["ada_b"][layer, v0 * D:(v0 + nv) * D].rearrange("(j n) -> j n", n=P)).then_inc(params_in, 16)
                        for v, g in ((1, 0), (2, 1), (4, 2), (5, 3)):
                            if v0 <= v < v0 + nv:
                                rv = r0 + 8 * (v - v0)
                                act.dma_start(m.grow[rv:rv + 8, b, :], io["norm_g"][layer, g].rearrange("(j n) -> j n", n=P)).then_inc(params_in, 16)
                act.dma_start(m.one[:], io["k_one"]).then_inc(params_in, 16)
                for h in range(PARTS):
                    act.wait_ge(part_used, h + 1)
                    if h >= 4:
                        act.wait_ge(raw_stored[h % 4], 16 * (h // 4))
                    act.activation(m.raw[:, h % 4, :], m.ps[0:2, 6 + h % 2, 0:PART], ACT.Copy).then_inc(raw_out, 1)

            @block.tensor
            def _(pe):
                pe.wait_ge(silu_done, 1)
                for h in range(PARTS):
                    pe.wait_ge(part_in[h % SLOTS], (h // SLOTS + 1) * 16)
                    if h >= 2:
                        pe.wait_ge(raw_out, h - 1)
                    ada_product(pe, m, ring[:, h % SLOTS], 6 + h % 2).then_inc(part_used, 1)

            @block.vector
            def _(dve):
                gains = sum(v0 <= v < v0 + nv for _, v0, nv in BATCHES for v in (1, 2, 4, 5))
                dve.wait_ge(params_in, 16 * (2 * len(BATCHES) + 2 * gains + 1))
                dve.wait_ge(reloaded, 32)
                ada_rows(dve, m, 0, biased, row_done, 1)
                dve.wait_ge(row_done, 1)


def mixer_weights(m, io):
    m.w_in_in = m.sem("w_in_in")
    w_in = m.W[:, 2:4, :].rearrange("p a b -> p (a b)").rearrange("p (k n) -> p k n", k=KC)
    return lambda sp: sp.dma_start(w_in, io["cf_w_in"][0].rearrange("(p k) n -> p k n", p=P)).then_inc(m.w_in_in, 16)


def attention_weights(m, io):
    m.qkv_in = [m.sem(f"att_w_in{c}") for c in range(6)]
    m.wc = m.W[:].rearrange("p a b -> p (a b)").rearrange("p (c k n) -> p c k n", c=6, k=KC)

    def load(sp):
        for c in (0, 2, 1, 3, 4, 5):
            sp.dma_start(m.wc[:, c], io["da_w_qkv"][0].rearrange("(p k) n -> p k n", p=P)[:, :, c * 512:c * 512 + 512]).then_inc(m.qkv_in[c], 16)

    return load


def shared_weights(m, io, layer):
    m.sh_in = m.sem(f"moe{layer}_sh_in")

    def load(sp):
        for n, w in (("gate", wg(m, 0)), ("up", wu(m, 0))):
            sp.dma_start(w, io[f"moe_sh_{n}"][layer].rearrange("(p k) n -> p k n", p=P)).then_inc(m.sh_in, 16)
        sp.dma_start(wd(m, 0), io["moe_sh_down"][layer].rearrange("(k p) n -> p k n", p=P)).then_inc(m.sh_in, 16)

    return load


def wg(m, s):
    return m.W[:, s, 0:2048].rearrange("p (k n) -> p k n", k=KC)


def wu(m, s):
    return m.W[:, s, 2048:4096].rearrange("p (k n) -> p k n", k=KC)


def wd(m, s):
    return m.W[:, s, 4096:6144].rearrange("p (k n) -> p k n", k=2)


def modulate(nc, m, io, tag, layer, half, tiles, store, early):
    nt = len(tiles)
    with ExitStack() as ctx:
        def sb(name, shape, dt=F32):
            return ctx.enter_context(nc.sbuf_tensor(f"{tag}_{name}", shape, dt))

        A = sb("A", [P, 2, D])
        B = sb("B", [P, 2, D])
        junk = sb("junk", [P, D])
        h = sb("h", [P, 2, D])
        hp = sb("hp", [P, 2, D])
        ssq = sb("ssq", [P, TT])
        std = sb("std", [P, TT])
        rstd = sb("rstd", [P, TT])
        rows_in = m.sem(f"{tag}_rows_in")
        squared = m.sem(f"{tag}_squared")
        std_done = m.sem(f"{tag}_std_done")
        rstd_done = m.sem(f"{tag}_rstd_done")
        scaled = m.sem(f"{tag}_scaled")
        h_done = m.sem(f"{tag}_h_done")
        turned = m.sem(f"{tag}_turned")
        hT_done = m.sem(f"{tag}_hT_done")
        h_stored = [m.sem(f"{tag}_h_stored{i}") for i in range(2)]
        streams = 2 if nt > 2 else 1

        with nc.Block() as block:
            @block.sync
            def _(sp):
                for s in range(streams):
                    sp.dma_start(A[:, s, :], m.MOD[layer, 3 * half + 1, s, :].partition_broadcast(P)).then_inc(rows_in, 16)
                    sp.dma_start(B[:, s, :], m.MOD[layer, 3 * half, s, :].partition_broadcast(P)).then_inc(rows_in, 16)
                early(sp)
                if store:
                    for i, t in enumerate(tiles):
                        sp.wait_ge(h_done, i + 1)
                        sp.dma_start(m.H2[t * P:(t + 1) * P, :], hp[:, i % 2, :]).then_inc(h_stored[i % 2], 16)
                    for i in range(2):
                        sp.wait_ge(h_stored[i], 16 * (nt // 2))

            @block.scalar
            def _(act):
                for i, t in enumerate(tiles):
                    if i:
                        act.wait_ge(squared, i)
                    act.activation(junk[:], m.X[:, t, :], ACT.Square, accum_out=ssq[:, i:i + 1]).then_inc(squared, 1)
                act.wait_ge(squared, nt)
                act.activation(std[:, 0:nt], ssq[:, 0:nt], ACT.Sqrt, bias=m.eps[:], scale=1.0 / D).then_inc(std_done, 1)
                for i, t in enumerate(tiles):
                    act.wait_ge(turned, i + 1)
                    act.activation(m.hT[:, :, t * P:(t + 1) * P], bank2(m, 2 * (i % 2)).rearrange("p (k t) -> p k t", k=KC), ACT.Copy).then_inc(hT_done, 1)

            @block.vector
            def _(dve):
                dve.wait_ge(std_done, 1)
                dve.reciprocal(rstd[:, 0:nt], std[:, 0:nt]).then_inc(rstd_done, 1)
                dve.wait_ge(rstd_done, 1)
                dve.wait_ge(rows_in, 32 * streams)
                for i, t in enumerate(tiles):
                    s = t // 2
                    dve.scalar_tensor_tensor(h[:, i % 2, :], m.X[:, t, :], rstd[:, i:i + 1], A[:, s, :], ALU.mult, ALU.mult).then_inc(scaled, 1)
                    dve.wait_ge(scaled, i + 1)
                    if i >= 2:
                        dve.wait_ge(turned, i - 1)
                        if store:
                            dve.wait_ge(h_stored[i % 2], 16 * (i // 2))
                    dve.tensor_tensor(hp[:, i % 2, :].rearrange("t (k p) -> t p k", k=KC), h[:, i % 2, :].rearrange("t (p k) -> t p k", k=KC),
                                      B[:, s, :].rearrange("t (p k) -> t p k", k=KC), ALU.add).then_inc(h_done, 1)

            @block.tensor
            def _(pe):
                for i in range(nt):
                    pe.wait_ge(h_done, i + 1)
                    if i >= 2:
                        pe.wait_ge(hT_done, i - 1)
                    for k in range(KC):
                        mm = pe.transpose(m.ps[:, 2 * (i % 2) + k // 4, (k % 4) * P:(k % 4 + 1) * P], hp[:, i % 2, k * P:(k + 1) * P], m.ident[:])
                    mm.then_inc(turned, 1)


def mixer(nc, m, io):
    with ExitStack() as ctx:
        def sb(name, shape, dt=F32):
            return ctx.enter_context(nc.sbuf_tensor(f"mix_{name}", shape, dt))

        w_in = m.W[:, 2:4, :].rearrange("p a b -> p (a b)").rearrange("p (k n) -> p k n", k=KC)
        w_out = m.W[:, 0:2, :].rearrange("p a b -> p (a b)")[:, 0:KC * D].rearrange("p (k n) -> p k n", k=KC)
        apad = sb("apad", [P, CJ, 2, SEQ + 2 * PAD])
        sg = sb("sg", [P, 2, 512])
        fT = sb("fT", [P, 4, 512])
        P1 = sb("P1", [P, TT, 4, 256])
        mixT = sb("mixT", [P, KC, 512])
        fch = sb("fch", [P, 256])
        fseq = sb("fseq", [P, 2, 512])
        gmean = sb("gmean", [P, P])
        prow = sb("prow", [CONV_W + 3, 512])
        pcol = sb("pcol", [P, CJ, 64])
        G = sb("G", [P, 2, D])
        ssq = sb("ssq", [P, TT])
        std4 = sb("std4", [P, TT])
        rstd4 = sb("rstd4", [P, TT])
        sq = P1[:].rearrange("p a b c -> p (a b c)")[:, 0:1024].rearrange("p (j n) -> p j n", j=2)
        sd = P1[:].rearrange("p a b c -> p (a b c)")[:, 1024:2048].rearrange("p (j n) -> p j n", j=2)
        junk = P1[:].rearrange("p a b c -> p (a b c)")[:, 2048:3072]
        tmp = P1[:].rearrange("p a b c -> p (a b c)")[:, 3072:4096]

        s = m.sem
        consts_in, gate_in, w_out_in = s("mix_consts_in"), s("mix_gate_in"), s("mix_w_out_in")
        params_turned, params_done = s("mix_params_turned"), s("mix_params_done")
        padded = s("mix_padded")
        u_done, gate_done, val_done, f_done = s("mix_u_done"), s("mix_gate_done"), s("mix_val_done"), s("mix_f_done")
        ch_done, ch_out, seq_done, seq_out = s("mix_ch_done"), s("mix_ch_out"), s("mix_seq_done"), s("mix_seq_out")
        tap, conv_done = s("mix_tap"), s("mix_conv_done")
        mean_done, centred, squared = s("mix_mean_done"), s("mix_centred"), s("mix_squared")
        var_done, std_done, rec_done, normed, a_done = s("mix_var_done"), s("mix_std_done"), s("mix_rec_done"), s("mix_normed"), s("mix_a_done")
        y_done, y_sq, y_std, y_rec, y_scaled, x_done = s("mix_y_done"), s("mix_y_sq"), s("mix_y_std"), s("mix_y_rec"), s("mix_y_scaled"), s("mix_x_done")
        part_in = [s(f"mix_part_in{i}") for i in range(2)]
        part_used, raw_out, biased, row_done = (s(f"mix_{n}") for n in ("part_used", "raw_out", "biased", "row_done"))
        raw_stored = [s(f"mix_raw_stored{i}") for i in range(4)]
        reloaded = [s(f"mix_reloaded{b}") for b in range(2)]
        stored = [s(f"mix_stored{b}") for b in range(2)]
        slots = m.W[:, 0:2, :].rearrange("p a b -> p (a b)")[:, KC * D:KC * D + 2 * KC * PART].rearrange("p (s k n) -> p s k n", s=2, k=KC)
        parts = [(b, h) for b in (1, 2) for h in range(BATCHES[b][2] * D // PART)]
        FIRST = BATCHES[1][2] * D // PART

        with nc.Block() as block:
            @block.sync
            def _(sp):
                sp.dma_start(prow[0:CONV_W, :], io["cf_conv_w"][0].rearrange("w o c -> w (o c)")).then_inc(consts_in, 16)
                for i, n in enumerate(("cf_conv_b", "cf_ln_g", "cf_ln_b")):
                    sp.dma_start(prow[CONV_W + i:CONV_W + i + 1, :], io[n]).then_inc(consts_in, 16)
                sp.dma_start(fch[:], io["k_fch"]).then_inc(consts_in, 16)
                sp.dma_start(fseq[:], io["k_fseq"]).then_inc(consts_in, 16)
                sp.dma_start(gmean[:], io["k_gmean"]).then_inc(consts_in, 16)

                def raw_store(i):
                    sp.wait_ge(raw_out, i + 1)
                    ada_store(sp, m, *parts[i], i, raw_stored[i % 4])

                for i, (b, h) in enumerate(parts):
                    if i >= 2:
                        sp.wait_ge(part_used, i - 1)
                    ada_load(sp, io, b, h, slots[:, i % 2], part_in[i % 2])
                    if i >= 2:
                        raw_store(i - 2)
                    if i == 3:
                        sp.dma_start(w_out, io["cf_w_out"][0].rearrange("(k p) n -> p k n", p=P)).then_inc(w_out_in, 16)
                raw_store(len(parts) - 2)
                raw_store(len(parts) - 1)
                sp.wait_ge(stored[1], 32)

            @block.gpsimd
            def _(pool):
                pool.memset(apad[:], 0.0).then_inc(padded, 1)
                for n, end in enumerate((FIRST, len(parts))):
                    for i in range(4):
                        pool.wait_ge(raw_stored[i], 16 * (end // 4))
                    ada_reload(pool, m, n + 1, reloaded[n])
                    pool.wait_ge(row_done, n + 1)
                    ada_publish(pool, m, n + 1, stored[n])
                    pool.wait_ge(stored[n], 32)

            @block.tensor
            def _(pe):
                part = [0]

                def ada(count):
                    for i in range(part[0], min(part[0] + count, len(parts))):
                        pe.wait_ge(part_in[i % 2], (i // 2 + 1) * 16)
                        if i >= 2:
                            pe.wait_ge(raw_out, i - 1)
                        ada_product(pe, m, slots[:, i % 2], (5, 7)[i % 2]).then_inc(part_used, 1)
                    part[0] = min(part[0] + count, len(parts))

                def mean(j):
                    if j:
                        pe.wait_ge(centred, j)
                    pe.wait_ge(conv_done, j + 1)
                    pe.matmul(m.ps[:, 4, :], gmean[:], mixT[:, j, :], start=True, stop=True).then_inc(mean_done, 1)

                def var(j):
                    if j:
                        pe.wait_ge(std_done, j)
                    pe.wait_ge(squared, j + 1)
                    pe.matmul(m.ps[:, 6, :], gmean[:], sq[:, j % 2, :], start=True, stop=True).then_inc(var_done, 1)

                pe.wait_ge(consts_in, 16 * 7)
                for j in range(CJ):
                    mm = pe.transpose(m.ps[:, 6, j * 64:j * 64 + CONV_W + 3], prow[:, j * P:(j + 1) * P], m.ident[0:CONV_W + 3, 0:CONV_W + 3])
                mm.then_inc(params_turned, 1)
                pe.wait_ge(m.w_in_in, 16)
                order = [x for j in range(CJ) for x in (CJ + j, j)] + [2 * CJ + g for g in range(4)]
                for n, mt in enumerate(order):
                    if n >= 4:
                        q = n - 4
                        if q < 8:
                            pe.wait_ge((gate_done, val_done)[q % 2], q // 2 + 1)
                        else:
                            pe.wait_ge(f_done, q - 7)
                    for k in range(KC):
                        mm = pe.matmul(m.ps[:, n % 4, :], w_in[:, k, mt * P:(mt + 1) * P], m.hT[:, k, :], start=(k == 0), stop=(k == KC - 1))
                        if k == KC - 1:
                            mm.then_inc(u_done, 1)
                        if k % 4 == 3:
                            ada(1)
                    if n >= 3:
                        if n == 3:
                            pe.wait_ge(params_done, 1)
                        if (n - 3) % 2 == 0 and n < 11:
                            mean((n - 3) // 2)
                        elif n < 11:
                            var((n - 4) // 2)
                pe.wait_ge(f_done, 4)
                pe.wait_ge(centred, CJ)
                pe.wait_ge(std_done, CJ)
                for n in range(2 * TT):
                    t, gp = n // 2, n % 2
                    if n >= 2:
                        pe.wait_ge(ch_out, n - 1)
                    for g in (2 * gp, 2 * gp + 1):
                        mm = pe.matmul(m.ps[:, 4 + 2 * (n % 2), (g % 2) * 256:(g % 2) * 256 + 256], fT[:, g, t * P:(t + 1) * P], fch[:], start=True, stop=True)
                    mm.then_inc(ch_done, 1)
                ada(2)
                pe.wait_ge(ch_out, 2 * TT)
                for g in range(4):
                    for st in range(2):
                        for n in range(4):
                            kt, cs = n // 2, n % 2
                            mm = pe.matmul(m.ps[:, g, st * 256:st * 256 + 256], P1[:, 2 * st + kt, g, cs * P:(cs + 1) * P],
                                           fseq[:, kt, cs * 256:cs * 256 + 256], start=(n == 0), stop=(n == 3))
                    mm.then_inc(seq_done, 1)
                ada(2)
                pe.wait_ge(w_out_in, 16)
                pe.wait_ge(a_done, CJ)
                pe.wait_ge(seq_out, 4)
                for t in range(TT):
                    if t >= 2:
                        pe.wait_ge(y_scaled, t - 1)
                    for n in range(2):
                        for k in range(KC):
                            mm = pe.matmul(m.ps[:, 2 * (t % 2) + n, :], mixT[:, k, t * P:(t + 1) * P], w_out[:, k, n * 512:n * 512 + 512],
                                           start=(k == 0), stop=(k == KC - 1))
                            if n == 1 and k == KC - 1:
                                mm.then_inc(y_done, 1)
                            if k % 4 == 3:
                                ada(1)

            @block.scalar
            def _(act):
                def std(j):
                    act.wait_ge(var_done, j + 1)
                    if j >= 2:
                        act.wait_ge(normed, j - 1)
                    act.activation(sd[:, j % 2, :], m.ps[:, 6, :], ACT.Sqrt, bias=m.eps[:]).then_inc(std_done, 1)

                def silu(j):
                    act.wait_ge(normed, j + 1)
                    act.activation(mixT[:, j, :], mixT[:, j, :], ACT.Silu, bias=pcol[:, j, CONV_W + 2:CONV_W + 3], scale=pcol[:, j, CONV_W + 1:CONV_W + 2]).then_inc(a_done, 1)

                def square(j):
                    act.wait_ge(centred, j + 1)
                    if j >= 2:
                        act.wait_ge(var_done, j - 1)
                    act.activation(sq[:, j % 2, :], mixT[:, j, :], ACT.Square).then_inc(squared, 1)

                part = [0]

                def raw(count):
                    for i in range(part[0], min(part[0] + count, len(parts))):
                        act.wait_ge(part_used, i + 1)
                        if i >= 4:
                            act.wait_ge(raw_stored[i % 4], 16 * (i // 4))
                        act.activation(m.raw[:, i % 4, :], m.ps[0:2, (5, 7)[i % 2], 0:PART], ACT.Copy).then_inc(raw_out, 1)
                    part[0] = min(part[0] + count, len(parts))

                def f_copy(g):
                    act.wait_ge(u_done, 9 + g)
                    act.activation(fT[:, g, :], m.ps[:, g % 4, :], ACT.Copy).then_inc(f_done, 1)

                for n in range(CJ * 3):
                    raw(1)
                    if n >= 2 * CJ:
                        f_copy(n - 2 * CJ)
                    elif n % 2 == 0:
                        j = n // 2
                        act.wait_ge(u_done, n + 1)
                        if j >= 2:
                            act.wait_ge(val_done, j - 1)
                        act.activation(sg[:, j % 2, :], m.ps[:, n % 4, :], ACT.Sigmoid).then_inc(gate_done, 1)
                    raw(1)
                    if n % 2 and n >= 3:
                        if n >= 5:
                            silu((n - 5) // 2)
                        if n < 11:
                            square((n - 3) // 2)
                    elif n >= 4:
                        std((n - 4) // 2)
                for n in range(2 * TT):
                    act.wait_ge(ch_done, n + 1)
                    act.activation(P1[:, n // 2, 2 * (n % 2):2 * (n % 2) + 2, :], m.ps[:, 4 + 2 * (n % 2), :].rearrange("p (g c) -> p g c", g=2), ACT.Copy).then_inc(ch_out, 1)
                raw(2)
                act.wait_ge(stored[0], 32)
                for i in range(2):
                    act.dma_start(G[:, i, :], m.MOD[0, 2, i, :].partition_broadcast(P)).then_inc(gate_in, 16)
                for g in range(4):
                    act.wait_ge(seq_done, g + 1)
                    act.activation(mixT[:, 4 + g, :], m.ps[:, g, :], ACT.Copy).then_inc(seq_out, 1)
                raw(2)
                for t in range(TT):
                    raw(3)
                    act.wait_ge(y_done, t + 1)
                    if t:
                        act.wait_ge(y_sq, t)
                    act.activation(junk, bank2(m, 2 * (t % 2)), ACT.Square, accum_out=ssq[:, t:t + 1]).then_inc(y_sq, 1)
                    act.wait_ge(y_sq, t + 1)
                    act.activation(std4[:, t:t + 1], ssq[:, t:t + 1], ACT.Sqrt, bias=m.eps[:], scale=1.0 / D).then_inc(y_std, 1)
                    raw(1)

            @block.vector
            def _(dve):
                dve.wait_ge(params_turned, 1)
                dve.tensor_copy(pcol[:, :, 0:CONV_W + 3], m.ps[:, 6, 0:256].rearrange("p (j w) -> p j w", j=CJ)[:, :, 0:CONV_W + 3]).then_inc(params_done, 1)
                dve.wait_ge(padded, 1)
                dve.wait_ge(params_done, 1)
                taps = [0]

                def conv(j):
                    dve.wait_ge(gate_done, j + 1)
                    dve.wait_ge(u_done, 2 * j + 2)
                    dve.tensor_tensor(apad[:, j, :, PAD:PAD + SEQ], m.ps[:, (2 * j + 1) % 4, :].rearrange("p (s n) -> p s n", s=2),
                                      sg[:, j % 2, :].rearrange("p (s n) -> p s n", s=2), ALU.mult).then_inc(val_done, 1)
                    dve.wait_ge(val_done, j + 1)
                    acc = mixT[:, j, :].rearrange("p (s n) -> p s n", s=2)
                    dve.tensor_scalar(acc, apad[:, j, :, 0:SEQ], pcol[:, j, 0:1], pcol[:, j, CONV_W:CONV_W + 1], ALU.mult, ALU.add).then_inc(tap, 1)
                    taps[0] += 1
                    for w in range(1, CONV_W):
                        dve.wait_ge(tap, taps[0])
                        last = dve.scalar_tensor_tensor(acc, apad[:, j, :, w:w + SEQ], pcol[:, j, w:w + 1], acc, ALU.mult, ALU.add)
                        if w < CONV_W - 1:
                            last.then_inc(tap, 1)
                            taps[0] += 1
                        else:
                            last.then_inc(conv_done, 1)

                def centre(j):
                    dve.wait_ge(mean_done, j + 1)
                    dve.tensor_tensor(mixT[:, j, :], mixT[:, j, :], m.ps[:, 4, :], ALU.subtract).then_inc(centred, 1)

                def norm(j):
                    dve.wait_ge(std_done, j + 1)
                    dve.reciprocal(sd[:, j % 2, :], sd[:, j % 2, :]).then_inc(rec_done, 1)
                    dve.wait_ge(rec_done, j + 1)
                    dve.wait_ge(squared, j + 1)
                    dve.tensor_tensor(mixT[:, j, :], mixT[:, j, :], sd[:, j % 2, :], ALU.mult).then_inc(normed, 1)

                for j in range(CJ):
                    conv(j)
                    if j:
                        norm(j - 1)
                    centre(j)
                norm(CJ - 1)
                dve.wait_ge(reloaded[0], 32)
                ada_rows(dve, m, 1, biased, row_done, 1)
                dve.wait_ge(gate_in, 32)
                for t in range(TT):
                    dve.wait_ge(y_std, t + 1)
                    dve.reciprocal(rstd4[:, t:t + 1], std4[:, t:t + 1]).then_inc(y_rec, 1)
                    dve.wait_ge(y_rec, t + 1)
                    if t:
                        dve.wait_ge(x_done, t)
                    dve.scalar_tensor_tensor(tmp, bank2(m, 2 * (t % 2)), rstd4[:, t:t + 1], G[:, t // 2, :], ALU.mult, ALU.mult).then_inc(y_scaled, 1)
                    dve.wait_ge(y_scaled, t + 1)
                    dve.tensor_tensor(m.X[:, t, :], m.X[:, t, :], tmp, ALU.add).then_inc(x_done, 1)
                dve.wait_ge(reloaded[1], 32)
                ada_rows(dve, m, 2, biased, row_done, 2)


def attention(nc, m, io):
    lam_init = 0.8 - 0.6 * math.exp(-0.3)
    scale = QK ** -0.5
    with ExitStack() as ctx:
        def sb(name, shape, dt=F32):
            return ctx.enter_context(nc.sbuf_tensor(f"att_{name}", shape, dt))

        wc = m.wc
        qT = sb("qT", [P, HEADS, SEQ])
        kT = sb("kT", [P, HEADS, 2 * SEQ])
        v = sb("v", [P, TT, D])
        cosT, sinT = sb("cosT", [P, SEQ]), sb("sinT", [P, SEQ])
        rot = sb("rot", [P, P])
        t1, t2 = sb("t1", [P, SEQ]), sb("t2", [P, SEQ])
        lp = sb("lp", [P, 4 * QK])
        lj = sb("lj", [P, 2 * QK])
        ls, le, nlam = sb("ls", [P, 2]), sb("le", [P, 2]), sb("nlam", [P, 1])
        mx, nm, sm, rs = (sb(n, [P, 2 * HEADS, 2]) for n in ("mx", "nm", "sm", "rs"))
        cf = sb("cf", [P, 2 * HEADS])
        p0, p1 = sb("p0", [P, 2, 512]), sb("p1", [P, 2, 512])
        pdT = sb("pdT", [P, 2, 512])
        o = sb("o", [P, 2, D])
        ss8, st8, r8 = (sb(n, [P, 2, HEADS]) for n in ("ss8", "st8", "r8"))
        sub = sb("sub", [P, 1])
        subs = sb("subs", [P, 1])
        G = sb("G", [P, D])
        tmp = sb("tmp", [P, D])
        ssq, std, rstd = (sb(n, [P, 2]) for n in ("ssq", "std", "rstd"))
        oT = m.hT[:, :, 0:SEQ]

        s = m.sem
        w_in = m.qkv_in
        consts_in, w_out_in = s("att_consts_in"), s("att_w_out_in")
        lam_step, lam_sum, lam_exp = s("att_lam_step"), s("att_lam_sum"), s("att_lam_exp")
        raw_done, raw_out, turned, t1_done, t2_done, roped = (s(f"att_{n}") for n in ("raw_done", "raw_out", "turned", "t1_done", "t2_done", "roped"))
        v_done, v_out = s("att_v_done"), s("att_v_out")
        s_done, max_done, neg_done, exp_done, rec_done, cf_done, p1_done, pd_done = (
            s(f"att_{n}") for n in ("s_done", "max_done", "neg_done", "exp_done", "rec_done", "cf_done", "p1_done", "pd_done"))
        pT_done, pT_out, o_done, o_out = (s(f"att_{n}") for n in ("pT_done", "pT_out", "o_done", "o_out"))
        o_sq, o_sum, o_std, o_rec, o_norm, oT_done, oT_out = (s(f"att_{n}") for n in ("o_sq", "o_sum", "o_std", "o_rec", "o_norm", "oT_done", "oT_out"))
        y_done, y_sq, y_std, y_rec, y_scaled, x_done = (s(f"att_y{n}") for n in ("_done", "_sq", "_std", "_rec", "_scaled", "_x"))
        UNITS = 2 * HEADS
        CONSTS = 16 * 6

        with nc.Block() as block:
            @block.sync
            def _(sp):
                sp.dma_start(cosT[:], io["k_cos"]).then_inc(consts_in, 16)
                sp.dma_start(sinT[:], io["k_sin"]).then_inc(consts_in, 16)
                sp.dma_start(rot[:], io["k_rot"]).then_inc(consts_in, 16)
                sp.dma_start(lp[:], io["da_lambda"][0].rearrange("a b -> (a b)").partition_broadcast(P)).then_inc(consts_in, 16)
                sp.dma_start(G[:], m.MOD[1, 2, 0, :].partition_broadcast(P)).then_inc(consts_in, 16)
                sp.dma_start(sub[:], io["da_subln_g"].rearrange("a p -> p a")).then_inc(consts_in, 16)
                sp.wait_ge(raw_done, UNITS)
                for n in range(2):
                    sp.dma_start(wc[:, n], io["da_w_out"][0].rearrange("(k p) n -> p k n", p=P)[:, :, n * 512:n * 512 + 512]).then_inc(w_out_in, 16)

            @block.tensor
            def _(pe):
                def rotate(u):
                    hd, is_k = u // 2, u % 2
                    pe.wait_ge(raw_out, u + 1)
                    if u >= 2:
                        pe.wait_ge(t2_done, u - 1)
                    src = kT[:, hd, 0:SEQ] if is_k else qT[:, hd, :]
                    pe.matmul(m.ps[:, 2 + u % 2, 0:SEQ], rot[:], src, start=True, stop=True).then_inc(turned, 1)

                for u in range(UNITS):
                    hd, is_k = u // 2, u % 2
                    c, n = 2 * is_k + hd // 4, SEQ * (1 + is_k)
                    pe.wait_ge(w_in[c], 16)
                    if u >= 2:
                        pe.wait_ge(raw_out, u - 1)
                    for k in range(KC):
                        mm = pe.matmul(m.ps[:, u % 2, 0:n], wc[:, c, k, (hd % 4) * P:(hd % 4 + 1) * P], m.hT[:, k, 0:n], start=(k == 0), stop=(k == KC - 1))
                    mm.then_inc(raw_done, 1)
                    if u == 0:
                        pe.wait_ge(consts_in, CONSTS)
                    else:
                        rotate(u - 1)
                for i in range(2 * TT):
                    t, n = i // 2, i % 2
                    pe.wait_ge(w_in[4 + n], 16)
                    if i >= 2:
                        pe.wait_ge(v_out, i - 1)
                    for k in range(KC):
                        mm = pe.matmul(m.ps[:, 4 + i % 2, :], m.hT[:, k, t * P:(t + 1) * P], wc[:, 4 + n, k, :], start=(k == 0), stop=(k == KC - 1))
                    mm.then_inc(v_done, 1)
                    if i == 0:
                        rotate(UNITS - 1)
                pe.wait_ge(v_out, 2 * TT)
                pe.wait_ge(roped, UNITS)

                def scores(a):
                    hd, qt = a // 2, a % 2
                    if a >= 2:
                        pe.wait_ge(exp_done, 2 * (a - 1))
                    for c in range(2):
                        mm = pe.matmul(m.ps[:, 2 * (a % 2) + c, :], qT[c * QK:(c + 1) * QK, hd, qt * P:(qt + 1) * P], kT[c * QK:(c + 1) * QK, hd, :], start=True, stop=True)
                        mm.then_inc(s_done, 1)

                def values(a):
                    hd = a // 2
                    pe.wait_ge(pd_done, a + 1)
                    if a >= 2:
                        pe.wait_ge(pT_out, a - 1)
                        pe.wait_ge(o_out, a - 1)
                    for t in range(TT):
                        mm = pe.transpose(m.ps[:, 4 + a % 2, t * P:(t + 1) * P], p0[:, a % 2, t * P:(t + 1) * P], m.ident[:])
                    mm.then_inc(pT_done, 1)
                    pe.wait_ge(pT_out, a + 1)
                    for t in range(TT):
                        mm = pe.matmul(m.ps[:, 6 + a % 2, 0:P], pdT[:, a % 2, t * P:(t + 1) * P], v[:, t, hd * P:(hd + 1) * P], start=(t == 0), stop=(t == TT - 1))
                    mm.then_inc(o_done, 1)

                for a in range(2 * HEADS):
                    scores(a)
                    if a:
                        values(a - 1)
                values(2 * HEADS - 1)
                for qt in range(2):
                    pe.wait_ge(o_norm, qt + 1)
                    for k in range(KC):
                        mm = pe.transpose(m.ps[:, 2 * qt + k // 4, (k % 4) * P:(k % 4 + 1) * P], o[:, qt, k * P:(k + 1) * P], m.ident[:])
                    mm.then_inc(oT_done, 1)
                pe.wait_ge(w_out_in, 32)
                pe.wait_ge(o_out, 2 * HEADS)
                for qt in range(2):
                    pe.wait_ge(oT_out, qt + 1)
                    for n in range(2):
                        for k in range(KC):
                            mm = pe.matmul(m.ps[:, 4 + 2 * qt + n, :], oT[:, k, qt * P:(qt + 1) * P], wc[:, n, k, :], start=(k == 0), stop=(k == KC - 1))
                    mm.then_inc(y_done, 1)

            @block.scalar
            def _(act):
                for u in range(UNITS):
                    hd, is_k = u // 2, u % 2
                    act.wait_ge(raw_done, u + 1)
                    dst = kT[:, hd, :] if is_k else qT[:, hd, :]
                    act.activation(dst, m.ps[:, u % 2, 0:SEQ * (1 + is_k)], ACT.Copy).then_inc(raw_out, 1)
                for i in range(2 * TT):
                    act.wait_ge(v_done, i + 1)
                    act.activation(v[:, i // 2, (i % 2) * 512:(i % 2) * 512 + 512], m.ps[:, 4 + i % 2, :], ACT.Copy).then_inc(v_out, 1)
                act.wait_ge(lam_sum, 2)
                act.activation(le[:], ls[:], ACT.Exp).then_inc(lam_exp, 1)

                def output(a):
                    act.wait_ge(pT_done, a + 1)
                    if a >= 2:
                        act.wait_ge(o_done, a - 1)
                    act.activation(pdT[:, a % 2, :], m.ps[:, 4 + a % 2, :], ACT.Copy).then_inc(pT_out, 1)
                    act.wait_ge(o_done, a + 1)
                    act.activation(o[:, a % 2, (a // 2) * P:(a // 2 + 1) * P], m.ps[:, 6 + a % 2, 0:P], ACT.Copy).then_inc(o_out, 1)

                for a in range(2 * HEADS):
                    act.wait_ge(neg_done, a + 1)
                    if a >= 2:
                        act.wait_ge(pT_done, a - 1)
                    for c, pc in enumerate((p0, p1)):
                        act.activation(pc[:, a % 2, :], m.ps[:, 2 * (a % 2) + c, :], ACT.Exp, bias=nm[:, a, c:c + 1], scale=scale,
                                       accum_out=sm[:, a, c:c + 1]).then_inc(exp_done, 1)
                    if a:
                        output(a - 1)
                output(2 * HEADS - 1)
                for qt in range(2):
                    act.wait_ge(o_sum, qt + 1)
                    act.activation(st8[:, qt, :], ss8[:, qt, :], ACT.Sqrt, bias=m.eps[:], scale=1.0 / P).then_inc(o_std, 1)
                for qt in range(2):
                    act.wait_ge(oT_done, qt + 1)
                    act.wait_ge(lam_step, 3)
                    act.activation(oT[:, :, qt * P:(qt + 1) * P], bank2(m, 2 * qt).rearrange("p (k t) -> p k t", k=KC), ACT.Copy, scale=subs[:]).then_inc(oT_out, 1)
                for qt in range(2):
                    act.wait_ge(y_done, qt + 1)
                    act.activation(v[:, qt, :], bank2(m, 4 + 2 * qt), ACT.Square, accum_out=ssq[:, qt:qt + 1]).then_inc(y_sq, 1)
                    act.wait_ge(y_sq, qt + 1)
                    act.activation(std[:, qt:qt + 1], ssq[:, qt:qt + 1], ACT.Sqrt, bias=m.eps[:], scale=1.0 / D).then_inc(y_std, 1)

            @block.vector
            def _(dve):
                dve.wait_ge(consts_in, CONSTS)
                dve.tensor_scalar(subs[:], sub[:], 1.0 - lam_init, None, ALU.mult).then_inc(lam_step, 1)
                for i in range(2):
                    dve.tensor_tensor(lj[:, i * QK:(i + 1) * QK], lp[:, 2 * i * QK:(2 * i + 1) * QK], lp[:, (2 * i + 1) * QK:(2 * i + 2) * QK], ALU.mult).then_inc(lam_step, 1)
                dve.wait_ge(lam_step, 3)
                for i in range(2):
                    dve.tensor_reduce(ls[:, i:i + 1], lj[:, i * QK:(i + 1) * QK], AX.X, ALU.add).then_inc(lam_sum, 1)
                for u in range(UNITS):
                    hd, is_k = u // 2, u % 2
                    dst = kT[:, hd, 0:SEQ] if is_k else qT[:, hd, :]
                    dve.wait_ge(turned, u + 1)
                    if u:
                        dve.wait_ge(roped, u)
                    dve.tensor_tensor(t1[:], dst, cosT[:], ALU.mult).then_inc(t1_done, 1)
                    dve.tensor_tensor(t2[:], m.ps[:, 2 + u % 2, 0:SEQ], sinT[:], ALU.mult).then_inc(t2_done, 1)
                    dve.wait_ge(t1_done, u + 1)
                    dve.wait_ge(t2_done, u + 1)
                    dve.tensor_tensor(dst, t1[:], t2[:], ALU.add).then_inc(roped, 1)
                dve.wait_ge(lam_exp, 1)
                dve.tensor_tensor(nlam[:], le[:, 1:2], le[:, 0:1], ALU.subtract).then_inc(lam_step, 1)
                dve.wait_ge(lam_step, 4)
                dve.tensor_scalar(nlam[:], nlam[:], -lam_init, None, ALU.add).then_inc(lam_step, 1)
                dve.wait_ge(lam_step, 5)

                def weights(a):
                    dve.wait_ge(exp_done, 2 * a + 2)
                    dve.reciprocal(rs[:, a, :], sm[:, a, :]).then_inc(rec_done, 1)
                    dve.wait_ge(rec_done, a + 1)
                    dve.tensor_tensor(cf[:, a:a + 1], rs[:, a, 1:2], nlam[:], ALU.mult).then_inc(cf_done, 1)
                    dve.wait_ge(cf_done, a + 1)
                    dve.tensor_scalar(p1[:, a % 2, :], p1[:, a % 2, :], cf[:, a:a + 1], None, ALU.mult).then_inc(p1_done, 1)
                    dve.wait_ge(p1_done, a + 1)
                    dve.scalar_tensor_tensor(p0[:, a % 2, :], p0[:, a % 2, :], rs[:, a, 0:1], p1[:, a % 2, :], ALU.mult, ALU.add).then_inc(pd_done, 1)

                for a in range(2 * HEADS):
                    dve.wait_ge(s_done, 2 * a + 2)
                    dve.tensor_reduce(mx[:, a, :], m.ps[:, 2 * (a % 2):2 * (a % 2) + 2, :], AX.X, ALU.max).then_inc(max_done, 1)
                    dve.wait_ge(max_done, a + 1)
                    dve.tensor_scalar(nm[:, a, :], mx[:, a, :], -scale, None, ALU.mult).then_inc(neg_done, 1)
                    if a:
                        weights(a - 1)
                weights(2 * HEADS - 1)
                dve.wait_ge(o_out, 2 * HEADS)
                for qt in range(2):
                    dve.tensor_tensor(v[:, qt, :], o[:, qt, :], o[:, qt, :], ALU.mult).then_inc(o_sq, 1)
                    dve.wait_ge(o_sq, qt + 1)
                    dve.tensor_reduce(ss8[:, qt, :], v[:, qt, :].rearrange("p (h d) -> p h d", h=HEADS), AX.X, ALU.add).then_inc(o_sum, 1)
                for qt in range(2):
                    dve.wait_ge(o_std, qt + 1)
                    dve.reciprocal(r8[:, qt, :], st8[:, qt, :]).then_inc(o_rec, 1)
                    dve.wait_ge(o_rec, qt + 1)
                    oh = o[:, qt, :].rearrange("p (h d) -> p h d", h=HEADS)
                    dve.tensor_tensor(oh, oh, r8[:, qt, :].unsqueeze(2).broadcast_to([P, HEADS, P]), ALU.mult).then_inc(o_norm, 1)
                for t in range(2):
                    dve.wait_ge(y_std, t + 1)
                    dve.reciprocal(rstd[:, t:t + 1], std[:, t:t + 1]).then_inc(y_rec, 1)
                    dve.wait_ge(y_rec, t + 1)
                    if t:
                        dve.wait_ge(x_done, t)
                    dve.scalar_tensor_tensor(tmp[:], bank2(m, 4 + 2 * t), rstd[:, t:t + 1], G[:], ALU.mult, ALU.mult).then_inc(y_scaled, 1)
                    dve.wait_ge(y_scaled, t + 1)
                    dve.tensor_tensor(m.X[:, t, :], m.X[:, t, :], tmp[:], ALU.add).then_inc(x_done, 1)


def moe(nc, m, io, layer, nt):
    L = f"moe{layer}"
    with ExitStack() as ctx:
        def sb(name, shape, dt=F32):
            return ctx.enter_context(nc.sbuf_tensor(f"{L}_{name}", shape, dt))

        r = Memory()
        r.L, r.layer, r.nt = L, layer, nt
        r.gk = sb("gk", [P, nt, 8])
        r.passes = sb("passes", [1, 4], I32)
        r.counts = sb("counts", [1, NE], I32)
        r.hf_done, r.y_done, r.gu_done = m.sem(f"{L}_hf_done"), m.sem(f"{L}_y_done"), m.sem(f"{L}_gu_done")
        r.xt_out, r.y_out = ([m.sem(f"{L}_{n}_out_{e}") for e in ("act", "dve")] for n in ("xt", "y"))
        r.w_in = [m.sem(f"{L}_w_in{s}") for s in range(UNROLL)]
        r.pass_done = m.sem(f"{L}_pass_done")
        route(nc, m, io, r)
        experts(nc, m, io, r)
        combine(nc, m, io, r)


def expert_load(sp, m, io, r, e, s):
    sp.dma_start(wg(m, s), io["moe_w_gate"][r.layer, e].rearrange("(p k) n -> p k n", p=P)).then_inc(r.w_in[s], 16)
    sp.dma_start(wu(m, s), io["moe_w_up"][r.layer, e].rearrange("(p k) n -> p k n", p=P)).then_inc(r.w_in[s], 16)
    sp.dma_start(wd(m, s), io["moe_w_down"][r.layer, e].rearrange("(k p) n -> p k n", p=P)).then_inc(r.w_in[s], 16)


def route(nc, m, io, r):
    nt, L = r.nt, r.L
    with ExitStack() as ctx:
        def sb(name, shape, dt=F32):
            return ctx.enter_context(nc.sbuf_tensor(f"{L}r_{name}", shape, dt))

        rw = sb("rw", [P, KC, NE])
        rb = sb("rb", [P, NE])
        tri = sb("tri", [P, P], BF16)
        ones = sb("ones", [P, P], BF16)
        trif = sb("trif", [P, P])
        low = sb("low", [P, GROUPS, GROUPS])
        ecol = sb("ecol", [P, NE])
        val = sb("val", [P, TT * TOPK, 2], I32)
        empty = sb("empty", [P, ROWS * NE * 2 // P], I32)
        Q = sb("Q", [P, nt, NE])
        pick = sb("pick", [P, TOPK, nt, NE])
        rowf = sb("rowf", [P, TOPK, nt])
        row = sb("row", [P, TOPK, nt], I32)
        shs, shu, shh = (sb(n, [P, 2, 512]) for n in ("shs", "shu", "shh"))
        sc, bi, sel, G, t1, t2 = (sb(n, [P, nt, NE]) for n in ("sc", "bi", "sel", "G", "t1", "t2"))
        selb = sb("selb", [P, nt, NE], BF16)
        m8 = sb("m8", [P, nt, GROUPS, 8])
        gs = sb("gs", [P, nt, GROUPS])
        cmp1, cmp2 = sb("cmp1", [P, nt, GROUPS, GROUPS]), sb("cmp2", [P, nt, GROUPS, GROUPS])
        beat, gm, neg = (sb(n, [P, nt, GROUPS]) for n in ("beat", "gm", "neg"))
        top = sb("top", [P, nt, 8])
        v6 = sb("v6", [P, nt])
        need = sb("need", [P, nt])
        HALF = NE // 2
        sa, sbuf = sb("sa", [P, nt, HALF + NE]), sb("sb", [P, nt, HALF + NE])
        cnt = sb("cnt", [1, NE])
        mxc = sb("mxc", [1, 1])
        ge = sb("ge", [1, 4])
        npf = sb("npf", [1, 1])

        s = m.sem
        consts_in, ones_done, logits_done, scored = (s(f"{L}_{n}") for n in ("rconsts", "rones", "logits", "scored"))
        chain, sel_done, pos_done, route_done = (s(f"{L}_{n}") for n in ("rchain", "sel", "pos", "routed"))
        filled, row_done, tabled = (s(f"{L}_{n}") for n in ("filled", "row", "tabled"))
        empty_done = s(f"{L}_empty")
        sh_g, sh_u, sh_s, sh_c, sh_h, sh_y, sh_out = (s(f"{L}_{n}") for n in ("sh_g", "sh_u", "sh_s", "sh_c", "sh_h", "sh_y", "sh_out"))
        HT = nt * P

        with nc.Block() as block:
            @block.sync
            def _(sp):
                sp.dma_start(rw[:], io["moe_router_w"][r.layer].rearrange("(p k) n -> p k n", p=P)).then_inc(consts_in, 16)
                sp.dma_start(rb[:], io["moe_router_b"][r.layer].partition_broadcast(P)).then_inc(consts_in, 16)
                sp.dma_start(trif[:], io["k_tri"]).then_inc(consts_in, 16)
                sp.dma_start(low[:], io["k_low"].partition_broadcast(P)).then_inc(consts_in, 16)
                sp.dma_start(ecol[:], io["k_ecol"].partition_broadcast(P)).then_inc(consts_in, 16)
                sp.dma_start(val[:], io["k_val"]).then_inc(consts_in, 16)
                sp.wait_ge(empty_done, 1)
                sp.dma_start(m.TAB.rearrange("(p r) c -> p (r c)", p=P), empty[:]).then_inc(filled, 16)
                for n in (1, 2, 3):
                    expert_load(sp, m, io, r, n, n)
                sp.wait_ge(sh_y, nt)
                expert_load(sp, m, io, r, 0, 0)

            @block.gpsimd
            def _(pool):
                pool.sem_inc(r.hf_done, 2)
                pool.sem_inc(r.y_done, 2)
                pool.sem_inc(r.gu_done, 2)
                for i in range(2):
                    pool.sem_inc(r.xt_out[i], 1)
                    pool.sem_inc(r.y_out[i], 2)
                pool.sem_inc(r.pass_done, 1)
                pool.memset(empty[:], EMPTY).then_inc(empty_done, 1)
                pool.memset(ones[:], 1.0).then_inc(ones_done, 1)
                pool.memset(sa[:], 0.0).then_inc(ones_done, 1)
                pool.memset(sbuf[:], 0.0).then_inc(ones_done, 1)
                for f in range(2):
                    pool.wait_ge(sh_s, f + 1)
                    pool.wait_ge(sh_c, f + 1)
                    pool.tensor_tensor(shh[:, f, 0:HT], shs[:, f, 0:HT], shu[:, f, 0:HT], ALU.mult).then_inc(sh_h, 1)
                pool.wait_ge(consts_in, 16 * 6)
                pool.wait_ge(filled, 16)
                pool.wait_ge(row_done, 1)
                for k in range(TOPK):
                    for t in range(nt):
                        pool.indirect_dma_start(out=m.TAB, out_offset=bass.IndirectOffsetOnAxis(ap=row[:, k, t:t + 1], axis=0), in_=val[:, t * TOPK + k, :], in_offset=None,
                                                bounds_check=ROWS * NE - 1, oob_is_err=False, compute_op=ALU.bypass).then_inc(tabled, 16)
                pool.wait_ge(tabled, 16 * TOPK * nt)

            @block.scalar
            def _(act):
                act.wait_ge(logits_done, 1)
                act.activation(sc[:], m.ps[:, 0, 0:nt * NE].rearrange("p (t e) -> p t e", t=nt), ACT.Sigmoid).then_inc(scored, 1)
                for f in range(2):
                    act.wait_ge(sh_g, f + 1)
                    act.activation(shs[:, f, 0:HT], m.ps[:, 3 + 2 * f, 0:HT], ACT.Silu).then_inc(sh_s, 1)
                    act.wait_ge(sh_u, f + 1)
                    act.activation(shu[:, f, 0:HT], m.ps[:, 4 + 2 * f, 0:HT], ACT.Copy).then_inc(sh_c, 1)
                for t in range(nt):
                    act.wait_ge(sh_y, t + 1)
                    act.activation(m.hT[:].rearrange("p a b -> p (a b)")[:, t * D:(t + 1) * D], bank2(m, 4 + 2 * (t % 2)), ACT.Copy).then_inc(sh_out, 1)

            @block.tensor
            def _(pe):
                pe.wait_ge(consts_in, 16 * 6)
                for t in range(nt):
                    for k in range(KC):
                        mm = pe.matmul(m.ps[:, 0, t * NE:(t + 1) * NE], m.hT[:, k, t * P:(t + 1) * P], rw[:, k, :], start=(k == 0), stop=(k == KC - 1))
                mm.then_inc(logits_done, 1)
                pe.wait_ge(m.sh_in, 48)
                for f in range(2):
                    for w, b, done in ((wg(m, 0), 3, sh_g), (wu(m, 0), 4, sh_u)):
                        for k in range(KC):
                            mm = pe.matmul(m.ps[:, b + 2 * f, 0:HT], w[:, k, f * P:(f + 1) * P], m.hT[:, k, 0:HT], start=(k == 0), stop=(k == KC - 1))
                        mm.then_inc(done, 1)
                pe.wait_ge(sel_done, 1)
                pe.wait_ge(ones_done, 3)
                for t in range(nt):
                    for q in range(t):
                        pe.matmul(m.ps[:, 1, t * NE:(t + 1) * NE], ones[:], selb[:, q, :], start=(q == 0), stop=False)
                    pe.matmul(m.ps[:, 1, t * NE:(t + 1) * NE], tri[:], selb[:, t, :], start=(t == 0), stop=True)
                for t in range(nt):
                    mm = pe.matmul(m.ps[:, 2, 0:NE], ones[:], selb[:, t, :], start=(t == 0), stop=(t == nt - 1))
                mm.then_inc(pos_done, 1)
                pe.wait_ge(sh_h, 2)
                for t in range(nt):
                    if t >= 2:
                        pe.wait_ge(sh_out, t - 1)
                    for n in range(2):
                        for f in range(2):
                            mm = pe.matmul(m.ps[:, 4 + 2 * (t % 2) + n, :], shh[:, f, t * P:(t + 1) * P], wd(m, 0)[:, f, n * 512:n * 512 + 512], start=(f == 0), stop=(f == 1))
                    mm.then_inc(sh_y, 1)
                pe.wait_ge(sh_out, nt)

            @block.vector
            def _(dve):
                done = [0]

                def link(ins):
                    done[0] += 1
                    ins.then_inc(chain, 1)
                    dve.wait_ge(chain, done[0])

                def scan(src, out):
                    link(dve.tensor_copy(sa[:, :, HALF:], src))
                    a, b, d = sa, sbuf, 1
                    while d <= HALF:
                        link(dve.tensor_tensor(b[:, :, HALF:] if d < HALF else out, a[:, :, HALF:], a[:, :, HALF - d:HALF + NE - d], ALU.add))
                        a, b, d = b, a, 2 * d

                dve.wait_ge(consts_in, 16 * 6)
                dve.wait_ge(ones_done, 3)
                link(dve.tensor_copy(tri[:], trif[:]))
                dve.wait_ge(scored, 1)
                for t in range(nt):
                    last = dve.tensor_tensor(bi[:, t, :], sc[:, t, :], rb[:], ALU.add)
                link(last)
                for t in range(nt):
                    for g in range(GROUPS):
                        last = dve.max(m8[:, t, g, :], bi[:, t, g * 8:(g + 1) * 8])
                link(last)
                link(dve.tensor_tensor(gs[:], m8[:, :, :, 0], m8[:, :, :, 1], ALU.add))
                for t in range(nt):
                    other = gs[:, t, :].unsqueeze(1).broadcast_to([P, GROUPS, GROUPS])
                    own = gs[:, t, :].unsqueeze(2).broadcast_to([P, GROUPS, GROUPS])
                    dve.tensor_tensor(cmp1[:, t], other, own, ALU.is_gt)
                    link(dve.tensor_tensor(cmp2[:, t], other, own, ALU.is_equal))
                    link(dve.tensor_tensor(cmp2[:, t], cmp2[:, t], low[:], ALU.mult))
                link(dve.tensor_tensor(cmp1[:], cmp1[:], cmp2[:], ALU.add))
                link(dve.tensor_reduce(beat[:], cmp1[:], AX.X, ALU.add))
                link(dve.tensor_scalar(gm[:], beat[:], float(TOPG), None, ALU.is_lt))
                link(dve.tensor_scalar(neg[:], gm[:], -1.0, BIG, ALU.add, ALU.mult))
                for t in range(nt):
                    bit = bi[:, t, :].rearrange("p (g e) -> p g e", g=GROUPS)
                    link(dve.tensor_tensor(bit, bit, gm[:, t, :].unsqueeze(2).broadcast_to([P, GROUPS, 8]), ALU.mult))
                    link(dve.tensor_tensor(bit, bit, neg[:, t, :].unsqueeze(2).broadcast_to([P, GROUPS, 8]), ALU.add))
                for t in range(nt):
                    last = dve.max(top[:, t, :], bi[:, t, :])
                link(last)
                for t in range(nt):
                    dve.tensor_scalar(t1[:, t, :], bi[:, t, :], top[:, t, TOPK - 1:TOPK], None, ALU.is_gt)
                    link(dve.tensor_scalar(t2[:, t, :], bi[:, t, :], top[:, t, TOPK - 1:TOPK], None, ALU.is_equal))
                link(dve.tensor_reduce(need[:], t1[:], AX.X, ALU.add))
                link(dve.tensor_scalar(need[:], need[:], -1.0, float(TOPK), ALU.mult, ALU.add))
                scan(t2[:], G[:])
                for t in range(nt):
                    link(dve.tensor_scalar(G[:, t, :], G[:, t, :], need[:, t:t + 1], None, ALU.is_le))
                link(dve.tensor_tensor(t2[:], t2[:], G[:], ALU.mult))
                link(dve.tensor_tensor(sel[:], t1[:], t2[:], ALU.add))
                dve.tensor_copy(selb[:], sel[:]).then_inc(sel_done, 1)
                scan(sel[:], t1[:])
                link(dve.tensor_tensor(t1[:], t1[:], sel[:], ALU.mult))
                dve.wait_ge(pos_done, 1)
                for t in range(nt):
                    last = dve.scalar_tensor_tensor(Q[:, t, :], m.ps[:, 1, t * NE:(t + 1) * NE], float(NE), ecol[:], ALU.mult, ALU.add)
                link(last)
                for k in range(TOPK):
                    last = dve.scalar_tensor_tensor(pick[:, k], t1[:], float(k + 1), Q[:], ALU.is_equal, ALU.mult)
                link(last)
                link(dve.tensor_reduce(rowf[:], pick[:], AX.X, ALU.add))
                link(dve.tensor_copy(row[:], rowf[:]))
                dve.sem_inc(row_done, 1)
                link(dve.tensor_tensor(G[:], sc[:], sel[:], ALU.mult))
                link(dve.tensor_reduce(v6[:], G[:], AX.X, ALU.add))
                link(dve.reciprocal(need[:], v6[:]))
                for t in range(nt):
                    last = dve.tensor_scalar(G[:, t, :], G[:, t, :], need[:, t:t + 1], RSCALE, ALU.mult, ALU.mult)
                link(last)
                for k in range(TOPK):
                    last = dve.scalar_tensor_tensor(pick[:, k], t1[:], float(k + 1), G[:], ALU.is_equal, ALU.mult)
                link(last)
                link(dve.tensor_reduce(r.gk[:, :, 0:TOPK].rearrange("p t k -> p k t"), pick[:], AX.X, ALU.add))
                link(dve.tensor_copy(cnt[:], m.ps[0:1, 2, 0:NE]))
                link(dve.tensor_copy(r.counts[:], cnt[:]))
                link(dve.tensor_reduce(mxc[:], cnt[:], AX.X, ALU.max))
                for i in range(4):
                    link(dve.tensor_scalar(ge[:, i:i + 1], mxc[:], float(P * i) if i else -1.0, None, ALU.is_gt))
                link(dve.tensor_reduce(npf[:], ge[:], AX.X, ALU.add))
                dve.tensor_copy(r.passes[:, 0:1], npf[:]).then_inc(route_done, 1)
                dve.wait_ge(route_done, 1)


def experts(nc, m, io, r):
    nt, L, layer = r.nt, r.L, r.layer
    with ExitStack() as ctx:
        def sb(name, shape, dt=F32):
            return ctx.enter_context(nc.sbuf_tensor(f"{L}e_{name}", shape, dt))

        table = sb("table", [P, NE, 2], I32)
        ig, isc = sb("ig", [P, UNROLL], I32), sb("isc", [P, UNROLL], I32)
        xg = sb("xg", [P, UNROLL, D])
        xT = sb("xT", [P, 2, KC, P])
        sl = sb("sl", [P, 2, 2 * P])
        hf = sb("hf", [P, 2, 2 * P])
        y = sb("y", [P, 2, D])

        q = m.sem
        w_in = r.w_in
        hf_done, y_done, gu_done, xt_out, y_out, pass_done = r.hf_done, r.y_done, r.gu_done, r.xt_out, r.y_out, r.pass_done
        scattered = [q(f"{L}e_scattered{i}") for i in range(2)]
        pool_steps = q(f"{L}e_pool_steps")
        pe_steps = q(f"{L}e_pe_steps")
        cleared, ig_done, is_done = (q(f"{L}e_{n}") for n in ("cleared", "ig_done", "is_done"))
        gathered = [q(f"{L}e_gathered{s}") for s in range(UNROLL)]
        xt_done, sl_done = q(f"{L}e_xt_done"), q(f"{L}e_sl_done")

        table_in = q(f"{L}e_table_in")
        GI = NE // UNROLL

        def g_is_first(g):
            return isinstance(g, int) and g == 0

        with nc.Block() as block:
            @block.sync
            def _(sp):
                npass = sp.value_load(r.passes[0:1, 0:1], min_val=1, max_val=4)
                with sp.Fori(1, npass * GI) as g:
                    for s in range(UNROLL):
                        sp.wait_ge(y_done, g * UNROLL + s - 1)
                        expert_load(sp, m, io, r, (g % GI) * UNROLL + s, s)

            @block.tensor
            def _(pe):
                npass = pe.value_load(r.passes[0:1, 0:1], min_val=1, max_val=4)
                with pe.Fori(0, npass) as b:
                    def turn_rows(s, rows):
                        for k in range(KC):
                            mm = pe.transpose(m.ps[:, k // 4, (k % 4) * P:(k % 4) * P + rows], xg[0:rows, s, k * P:(k + 1) * P], m.ident[0:rows, 0:rows])
                        mm.then_inc(xt_done, 1)

                    def up_rows(s, rows):
                        for c in range(4):
                            w = wg(m, s) if c < 2 else wu(m, s)
                            for k in range(KC):
                                mm = pe.matmul(m.ps[:, 2 + s % 2, c * P:c * P + rows], w[:, k, (c % 2) * P:(c % 2 + 1) * P], xT[:, s % 2, k, 0:rows],
                                               start=(k == 0), stop=(k == KC - 1))
                        mm.then_inc(gu_done, 1)

                    def by_size(n, work, s):
                        pe.sem_inc(pe_steps, 1)
                        count = pe.value_load(r.counts[0:1, bass.ds(at(n), 1)], min_val=0, max_val=ROWS)
                        with pe.If(count <= SMALL):
                            work(s, SMALL)
                        with pe.Else():
                            work(s, P)

                    def turn(n, s):
                        pe.wait_ge(gathered[s], (b * GI + n // UNROLL + 1) * 16 if isinstance(n, int) else (b * GI + n[0] + 1) * 16)
                        for half in xt_out:
                            pe.wait_ge(half, b * NE + at(n) + 1)
                        by_size(n, turn_rows, s)

                    def at(n):
                        return n if isinstance(n, int) else n[0] * UNROLL + n[1]

                    def up(n, s):
                        g = n // UNROLL if isinstance(n, int) else n[0]
                        pe.wait_ge(w_in[s], (b * GI + g + 1) * 48)
                        for half in xt_out:
                            pe.wait_ge(half, b * NE + at(n) + 2)
                        pe.wait_ge(hf_done, b * NE + at(n) + 1)
                        by_size(n, up_rows, s)

                    def down(n, s):
                        pe.wait_ge(hf_done, b * NE + at(n) + 3)
                        for half in y_out:
                            pe.wait_ge(half, b * NE + at(n) + 1)
                        for c in range(2):
                            for k in range(2):
                                mm = pe.matmul(m.ps[:, 4 + 2 * (s % 2) + c, :], hf[:, s % 2, k * P:(k + 1) * P], wd(m, s)[:, k, c * 512:c * 512 + 512], start=(k == 0), stop=(k == 1))
                        mm.then_inc(y_done, 1)

                    turn(0, 0)
                    up(0, 0)
                    turn(1, 1)
                    with pe.Fori(0, GI - 1) as i:
                        for s in range(UNROLL):
                            up((i + (s + 1) // UNROLL, (s + 1) % UNROLL), (s + 1) % UNROLL)
                            turn((i + (s + 2) // UNROLL, (s + 2) % UNROLL), (s + 2) % UNROLL)
                            down((i, s), s)
                    for n in range(NE - UNROLL, NE):
                        if n + 1 < NE:
                            up(n + 1, (n + 1) % UNROLL)
                        if n + 2 < NE:
                            turn(n + 2, (n + 2) % UNROLL)
                        down(n, n % UNROLL)

            @block.vector
            def _(dve):
                npass = dve.value_load(r.passes[0:1, 0:1], min_val=1, max_val=4)
                with dve.Fori(0, npass) as b:
                    dve.wait_ge(pass_done, b + 1)

                    def xt_copy(g, s):
                        dve.wait_ge(xt_done, b * NE + g * UNROLL + s + 1)
                        dve.wait_ge(gu_done, b * NE + g * UNROLL + s + 1)
                        dve.tensor_copy(xT[:, s % 2, 4:8, :], m.ps[:, 1, :].rearrange("p (k t) -> p k t", k=4)).then_inc(xt_out[1], 1)

                    def hidden(g, s):
                        dve.wait_ge(sl_done, b * NE + g * UNROLL + s + 1)
                        dve.wait_ge(y_done, b * NE + g * UNROLL + s + 1)
                        dve.tensor_tensor(hf[:, s % 2, :], sl[:, s % 2, :], m.ps[:, 2 + s % 2, 2 * P:4 * P], ALU.mult).then_inc(hf_done, 1)

                    def y_copy(g, s):
                        dve.wait_ge(y_done, b * NE + g * UNROLL + s + 3)
                        if not (g_is_first(g) and s < 2):
                            dve.wait_ge(scattered[s % 2], (b * (NE // 2) + g * 2 + s // 2) * 16)
                        dve.tensor_copy(y[:, s % 2, 512:1024], m.ps[:, 5 + 2 * (s % 2), :]).then_inc(y_out[1], 1)

                    xt_copy(0, 0)
                    hidden(0, 0)
                    xt_copy(0, 1)

                    def group(g):
                        for s in range(UNROLL):
                            hidden(g + (s + 1) // UNROLL, (s + 1) % UNROLL)
                            xt_copy(g + (s + 2) // UNROLL, (s + 2) % UNROLL)
                            y_copy(g, s)

                    group(0)
                    with dve.Fori(1, GI - 1) as i:
                        group(i)
                    for s in range(UNROLL):
                        if s + 1 < UNROLL:
                            hidden(GI - 1, s + 1)
                        if s + 2 < UNROLL:
                            xt_copy(GI - 1, s + 2)
                        y_copy(GI - 1, s)

            @block.scalar
            def _(act):
                npass = act.value_load(r.passes[0:1, 0:1], min_val=1, max_val=4)
                with act.Fori(0, npass) as b:
                    def xt_copy(g, s):
                        act.wait_ge(xt_done, b * NE + g * UNROLL + s + 1)
                        act.wait_ge(gu_done, b * NE + g * UNROLL + s + 1)
                        act.activation(xT[:, s % 2, 0:4, :], m.ps[:, 0, :].rearrange("p (k t) -> p k t", k=4), ACT.Copy).then_inc(xt_out[0], 1)

                    def gate(g, s):
                        act.wait_ge(gu_done, b * NE + g * UNROLL + s + 3)
                        act.wait_ge(hf_done, b * NE + g * UNROLL + s + 1)
                        act.activation(sl[:, s % 2, :], m.ps[:, 2 + s % 2, 0:2 * P], ACT.Silu).then_inc(sl_done, 1)

                    def y_copy(g, s):
                        act.wait_ge(y_done, b * NE + g * UNROLL + s + 3)
                        if not (g_is_first(g) and s < 2):
                            act.wait_ge(scattered[s % 2], (b * (NE // 2) + g * 2 + s // 2) * 16)
                        act.activation(y[:, s % 2, 0:512], m.ps[:, 4 + 2 * (s % 2), :], ACT.Copy).then_inc(y_out[0], 1)

                    act.wait_ge(pass_done, b + 1)
                    act.dma_start(table[:], m.TAB.rearrange("(b p e) c -> b p e c", p=P, e=NE)[b]).then_inc(table_in, 16)
                    xt_copy(0, 0)
                    gate(0, 0)
                    xt_copy(0, 1)

                    def group(g):
                        for s in range(UNROLL):
                            gate(g + (s + 1) // UNROLL, (s + 1) % UNROLL)
                            xt_copy(g + (s + 2) // UNROLL, (s + 2) % UNROLL)
                            y_copy(g, s)

                    group(0)
                    with act.Fori(1, GI - 1) as i:
                        group(i)
                    for s in range(UNROLL):
                        if s + 1 < UNROLL:
                            gate(GI - 1, s + 1)
                        if s + 2 < UNROLL:
                            xt_copy(GI - 1, s + 2)
                        y_copy(GI - 1, s)

            @block.gpsimd
            def _(pool):
                pool.memset(xg[:], 0.0).then_inc(cleared, 1)
                pool.wait_ge(cleared, 1)
                npass = pool.value_load(r.passes[0:1, 0:1], min_val=1, max_val=4)
                with pool.Fori(0, npass) as b:
                    pool.wait_ge(table_in, b * 16 + 16)

                    def gather_rows(s, rows):
                        pool.indirect_dma_start(out=xg[0:rows, s, :], out_offset=None, in_=m.H2, in_offset=bass.IndirectOffsetOnAxis(ap=ig[0:rows, s:s + 1], axis=0),
                                                bounds_check=ROWS - 1, oob_is_err=False, compute_op=ALU.bypass).then_inc(gathered[s], 16)

                    def scatter_rows(s, rows):
                        pool.indirect_dma_start(out=m.Y6, out_offset=bass.IndirectOffsetOnAxis(ap=isc[0:rows, s:s + 1], axis=0), in_=y[0:rows, s % 2, :], in_offset=None,
                                                bounds_check=TOPK * ROWS - 1, oob_is_err=False, compute_op=ALU.bypass).then_inc(scattered[s % 2], 16)

                    def by_size(g, s, work):
                        count = pool.value_load(r.counts[0:1, bass.ds(g * UNROLL + s, 1)], min_val=0, max_val=ROWS)
                        with pool.If(count <= SMALL):
                            work(s, SMALL)
                        with pool.Else():
                            work(s, P)

                    def gather(g, s):
                        if not g_is_first(g):
                            for half in xt_out:
                                pool.wait_ge(half, b * NE + g * UNROLL + s + 2 - UNROLL)
                        pool.sem_inc(pool_steps, 1)
                        pool.tensor_copy(ig[:, s:s + 1], table[:, bass.ds(g * UNROLL + s, 1), 0]).then_inc(ig_done, 1)
                        pool.wait_ge(ig_done, b * NE + g * UNROLL + s + 1)
                        pool.sem_inc(pool_steps, 1)
                        by_size(g, s, gather_rows)

                    def scatter(g, s):
                        for half in y_out:
                            pool.wait_ge(half, b * NE + g * UNROLL + s + 3)
                        pool.sem_inc(pool_steps, 1)
                        pool.tensor_copy(isc[:, s:s + 1], table[:, bass.ds(g * UNROLL + s, 1), 1]).then_inc(is_done, 1)
                        pool.wait_ge(is_done, b * NE + g * UNROLL + s + 1)
                        pool.sem_inc(pool_steps, 1)
                        by_size(g, s, scatter_rows)

                    for s in range(UNROLL):
                        gather(0, s)
                    scatter(0, 0)
                    with pool.Fori(1, GI) as i:
                        for s in range(UNROLL):
                            gather(i, s)
                            if s < UNROLL - 1:
                                scatter(i - 1, s + 1)
                            else:
                                scatter(i, 0)
                    for s in range(1, UNROLL):
                        scatter(GI - 1, s)
                    for i in range(2):
                        pool.wait_ge(scattered[i], (b * (NE // 2) + NE // 2) * 16)
                    pool.sem_inc(pass_done, 1)


def combine(nc, m, io, r):
    nt, L = r.nt, r.L
    last_layer = r.layer == 1
    with ExitStack() as ctx:
        def sb(name, shape, dt=F32):
            return ctx.enter_context(nc.sbuf_tensor(f"{L}c_{name}", shape, dt))

        rows = m.W[:].rearrange("p a b -> p (a b)")[:, 0:2 * TOPK * D].rearrange("p (i k d) -> p i k d", i=2, k=TOPK)
        G = sb("G", [P, 2, D])
        junk = sb("junk", [P, D])
        ssq, std, rstd = (sb(n, [P, nt]) for n in ("ssq", "std", "rstd"))
        q = m.sem
        gate_in = q(f"{L}c_gate_in")
        rows_in = [q(f"{L}c_rows_in{i}") for i in range(2)]
        added, summed, squared, std_done, rec_done, scaled, x_done, stored = (
            q(f"{L}c_{n}") for n in ("added", "summed", "squared", "std_done", "rec_done", "scaled", "x_done", "stored"))
        shared = m.hT[:].rearrange("p a b -> p (a b)")
        streams = 2 if nt > 2 else 1

        with nc.Block() as block:
            @block.sync
            def _(sp):
                for s in range(streams):
                    sp.dma_start(G[:, s, :], m.MOD[r.layer, 5, s, :].partition_broadcast(P)).then_inc(gate_in, 16)
                for t in range(nt):
                    if t >= 2:
                        sp.wait_ge(summed, t - 1)
                    sp.dma_start(rows[:, t % 2], m.Y6.rearrange("(k t) d -> t k d", k=TOPK)[t * P:(t + 1) * P]).then_inc(rows_in[t % 2], 16)
                if last_layer:
                    for t in range(nt):
                        sp.wait_ge(x_done, t + 1)
                        sp.dma_start(io["out"][0, t * P:(t + 1) * P, :], m.X[:, t, :]).then_inc(stored, 16)
                    sp.wait_ge(stored, 16 * nt)

            @block.vector
            def _(dve):
                n = 0
                for t in range(nt):
                    acc = shared[:, t * D:(t + 1) * D]
                    dve.wait_ge(rows_in[t % 2], 16 * (t // 2 + 1))
                    for k in range(TOPK):
                        last = dve.scalar_tensor_tensor(acc, rows[:, t % 2, k, :], r.gk[:, t, k:k + 1], acc, ALU.mult, ALU.add)
                        if k < TOPK - 1:
                            last.then_inc(added, 1)
                            n += 1
                            dve.wait_ge(added, n)
                        else:
                            last.then_inc(summed, 1)
                dve.wait_ge(gate_in, 16 * streams)
                for t in range(nt):
                    acc = shared[:, t * D:(t + 1) * D]
                    dve.wait_ge(std_done, t + 1)
                    dve.reciprocal(rstd[:, t:t + 1], std[:, t:t + 1]).then_inc(rec_done, 1)
                    dve.wait_ge(rec_done, t + 1)
                    dve.scalar_tensor_tensor(acc, acc, rstd[:, t:t + 1], G[:, t // 2, :], ALU.mult, ALU.mult).then_inc(scaled, 1)
                    dve.wait_ge(scaled, t + 1)
                    dve.tensor_tensor(m.X[:, t, :], m.X[:, t, :], acc, ALU.add).then_inc(x_done, 1)

            @block.scalar
            def _(act):
                for t in range(nt):
                    act.wait_ge(summed, t + 1)
                    if t:
                        act.wait_ge(squared, t)
                    act.activation(junk[:], shared[:, t * D:(t + 1) * D], ACT.Square, accum_out=ssq[:, t:t + 1]).then_inc(squared, 1)
                    act.wait_ge(squared, t + 1)
                    act.activation(std[:, t:t + 1], ssq[:, t:t + 1], ACT.Sqrt, bias=m.eps[:], scale=1.0 / D).then_inc(std_done, 1)


def build(nc, io, stop=99):
    m = Memory()
    with ExitStack() as ctx:
        start(nc, ctx, m)
        first = ctx.enter_context(ExitStack())
        modulation_buffers(nc, first, m)
        steps = [
            lambda: conditioning(nc, m, io),
            lambda: modulate(nc, m, io, "m00", 0, 0, range(4), False, mixer_weights(m, io)),
            lambda: mixer(nc, m, io),
            lambda: modulate(nc, m, io, "m01", 0, 1, range(4), True, shared_weights(m, io, 0)),
            lambda: moe(nc, m, io, 0, 4),
            lambda: modulate(nc, m, io, "m10", 1, 0, range(4), False, attention_weights(m, io)),
            lambda: attention(nc, m, io),
            lambda: modulate(nc, m, io, "m11", 1, 1, range(2), True, shared_weights(m, io, 1)),
            lambda: moe(nc, m, io, 1, 2),
        ]
        for n, step in enumerate(steps[:stop]):
            step()
            if n == 2:
                first.close()
            if n == 4:
                nc.clear_and_free_semaphores(m.used)
                m.used.clear()
                nc.all_engine_barrier()


def _constants():
    f = np.float32
    k = {}
    k["k_ident"] = np.eye(P, dtype=f)
    k["k_one"] = np.zeros((P, len(BATCHES)), f)
    for b, (_, v0, nv) in enumerate(BATCHES):
        for s in range(2):
            for v in range(nv):
                k["k_one"][(s * nv + v) * 8:(s * nv + v + 1) * 8, b] = 1.0 if v0 + v in (1, 4) else 0.0

    def dft(n):
        a = 2 * np.pi * (np.outer(np.arange(n), np.arange(n)) % n) / n
        return np.cos(a) / np.sqrt(n), np.sin(a) / np.sqrt(n)

    c, s = dft(P)
    k["k_fch"] = np.concatenate([c, s], 1).astype(f)
    c, s = dft(SEQ)
    k["k_fseq"] = np.concatenate([c, -s], 1).reshape(2, P, 2 * SEQ).transpose(1, 0, 2).astype(f)
    k["k_gmean"] = (np.kron(np.eye(P // CONV_GROUP), np.ones((CONV_GROUP, CONV_GROUP))) / CONV_GROUP).astype(f)
    grid = 64
    tok = np.arange(SEQ)
    n_freq = QK // 4
    inv = np.power(f(10000.0), -np.arange(n_freq, dtype=f) / f(n_freq)).astype(f)
    ang = np.concatenate([(tok // grid).astype(f)[:, None] * inv, (tok % grid).astype(f)[:, None] * inv], -1)
    ang = np.concatenate([ang, ang, ang, ang], -1).T
    k["k_cos"], k["k_sin"] = np.cos(ang).astype(f), np.sin(ang).astype(f)
    r = np.zeros((QK, QK), f)
    h = QK // 2
    for i in range(h):
        r[i + h, i] = -1.0
        r[i, i + h] = 1.0
    k["k_rot"] = np.kron(np.eye(2, dtype=f), r).astype(f)
    k["k_tri"] = np.triu(np.ones((P, P), f), 1)
    k["k_low"] = np.tril(np.ones((GROUPS, GROUPS), f), -1)
    k["k_ecol"] = np.arange(NE, dtype=f)
    token = np.arange(P)[:, None, None] + P * np.arange(TT)[None, :, None]
    rank = np.arange(TOPK)[None, None, :]
    k["k_val"] = np.stack([token + 0 * rank, token + ROWS * rank], -1).reshape(P, TT * TOPK, 2).astype(np.int32)
    return k


_INS = ["x", "c", "ctx", "c_ctx", "ada_w", "ada_b", "norm_g", "cf_w_in", "cf_conv_w", "cf_conv_b", "cf_ln_g", "cf_ln_b", "cf_w_out",
        "da_w_qkv", "da_lambda", "da_subln_g", "da_w_out", "moe_router_w", "moe_router_b", "moe_w_gate", "moe_w_up", "moe_w_down",
        "moe_sh_gate", "moe_sh_up", "moe_sh_down"]


def kernel(**inputs):
    import concourse.bacc as _bacc
    from concourse.bass_utils import run_bass_kernel_spmd as _run

    nc = _bacc.Bacc("TRN2", target_bir_lowering=False, num_devices=1)
    arrays, io = {}, {}
    data = {n: np.ascontiguousarray(inputs[n]) for n in _INS} | _constants()
    for name, a in data.items():
        a = np.ascontiguousarray(a)
        arrays[f"in_{name}"] = a
        io[name] = nc.dram_tensor(f"in_{name}", a.shape, mybir.dt.from_np(a.dtype), kind="ExternalInput").ap()
    io["out"] = nc.dram_tensor("out_x", (1, SEQ, D), F32, kind="ExternalOutput").ap()
    build(nc, io)
    r = _run(nc, [arrays], core_ids=[0])
    return r.results[0]["out_x"]
```

```python
import math
from contextlib import ExitStack

import concourse.bass as bass
import numpy as np
from concourse import mybir

F32 = mybir.dt.float32
BF16 = mybir.dt.bfloat16
I32 = mybir.dt.int32
ALU = mybir.AluOpType
ACT = mybir.ActivationFunctionType
AX = mybir.AxisListType

P = 128
D = 1024
KC = D // P
SEQ = 256
TT = 2 * SEQ // P
EPS = 1e-6
CONV_CH, CONV_W, CONV_GROUP = 512, 31, 64
PAD = CONV_W // 2
CJ = CONV_CH // P
MIX_IN = 1536
HEADS, QK = 8, 64
NE, GROUPS, TOPG, TOPK, FF = 64, 8, 4, 6, 256
RSCALE = 2.5
ROWS = 2 * SEQ
EMPTY = 4096
BIG = 1e30
UNROLL = 4
SHARED = UNROLL - 1
SMALL = 64

BATCHES = ((0, 0, 2), (0, 2, 4), (1, 0, 6))
PART = 256
AHEAD = 4
LATE = TT


class Memory:
    pass


def start(nc, ctx, m):

    def sb(name, shape, dt=F32):
        return ctx.enter_context(nc.sbuf_tensor(name, shape, dt))

    m.X = sb("X", [P, TT, D])
    m.hT = sb("hT", [P, KC, 2 * SEQ])
    m.W = sb("W", [P, UNROLL, 3 * 2048])
    m.ident = sb("ident", [P, P])
    m.eps = sb("eps", [P, 1])
    m.ssq = sb("ssq", [P, TT])
    m.ps = ctx.enter_context(nc.psum_tensor("ps", [P, 8, 512], F32))
    m.used = []

    def sem(name):
        m.used.append(nc.alloc_semaphore(name))
        return m.used[-1]

    m.sem = sem
    m.RAW = nc.dram_tensor("raw_scratch", [2, 2, 6 * D], F32).ap()
    m.MOD = nc.dram_tensor("mod_scratch", [2, 6, 2, D], F32).ap()
    m.H2 = nc.dram_tensor("h2_scratch", [ROWS, D], F32).ap()
    m.TAB = nc.dram_tensor("table_scratch", [ROWS * NE, 2], I32).ap()
    m.Y6 = nc.dram_tensor("y6_scratch", [TOPK * ROWS, D], F32).ap()


def modulation_buffers(nc, ctx, m):
    def sb(name, shape):
        return ctx.enter_context(nc.sbuf_tensor(name, shape, F32))

    m.cS = sb("cS", [P, 2, KC])
    m.one = sb("ada_one", [P, len(BATCHES)])
    m.brow = sb("ada_brow", [P, len(BATCHES), P])
    m.grow = sb("ada_grow", [P, len(BATCHES), P])
    m.raw = sb("ada_raw", [2, 4, PART])
    m.trow = sb("ada_trow", [P, P])
    m.mrow = sb("ada_mrow", [P, P])
    m.orow = sb("ada_orow", [P, len(BATCHES), P])


def bank2(m, b):
    return m.ps[:, b:b + 2, :].rearrange("p a n -> p (a n)")


def ada_load(sp, io, b, h, slot, done):
    layer, v0, _ = BATCHES[b]
    c0 = v0 * D + h * PART
    sp.dma_start(slot, io["ada_w"][layer].rearrange("(p k) n -> p k n", p=P)[:, :, c0:c0 + PART]).then_inc(done, 16)


def ada_product(pe, m, slot, bank):
    for k in range(KC):
        mm = pe.matmul(m.ps[0:2, bank, 0:PART], m.cS[:, :, k], slot[:, k, :], start=(k == 0), stop=(k == KC - 1))
    return mm


def ada_store(sp, m, b, h, raw, i, done):
    layer, v0, _ = BATCHES[b]
    c0 = v0 * D + h * PART
    sp.dma_start(m.RAW[layer, :, c0:c0 + PART], raw[:, i, :]).then_inc(done, 16)


def ada_reload(eng, m, b, done):
    layer, v0, nv = BATCHES[b]
    for s in range(2):
        eng.dma_start(m.trow[s * 8 * nv:(s + 1) * 8 * nv, :], m.RAW[layer, s, v0 * D:(v0 + nv) * D].rearrange("(j n) -> j n", n=P)).then_inc(done, 16)


def ada_rows(dve, m, b, biased, row_done, n):
    rows = 16 * BATCHES[b][2]
    dve.scalar_tensor_tensor(m.mrow[0:rows, :], m.trow[0:rows, :], m.one[0:rows, b:b + 1], m.brow[0:rows, b, :], ALU.add, ALU.add).then_inc(biased, 1)
    dve.wait_ge(biased, n)
    dve.tensor_tensor(m.orow[0:rows, b, :], m.mrow[0:rows, :], m.grow[0:rows, b, :], ALU.mult).then_inc(row_done, 1)


def ada_publish(eng, m, b, done):
    layer, v0, nv = BATCHES[b]
    for s in range(2):
        eng.dma_start(m.MOD[layer, v0:v0 + nv, s, :].rearrange("v (j n) -> v j n", n=P),
                      m.orow[s * 8 * nv:(s + 1) * 8 * nv, b, :]).then_inc(done, 16)


def conditioning(nc, m, io):
    with ExitStack() as ctx:
        SLOTS = 6
        cT = ctx.enter_context(nc.sbuf_tensor("cT", [P, 2, KC], F32))
        ring = m.W[:, 0:2, :].rearrange("p a b -> p (a b)").rearrange("p (s k n) -> p s k n", s=SLOTS, k=KC)
        PARTS = BATCHES[0][2] * D // PART
        parts = [(0, h) for h in range(PARTS)] + [(1, h) for h in range(AHEAD)]
        c_in, params_in, ones_done = m.sem("ada_c_in"), m.sem("ada_params_in"), m.sem("ada_ones_done")
        part_in = [m.sem(f"ada_part_in{s}") for s in range(SLOTS)]
        part_used, silu_done, raw_out = m.sem("ada_part_used"), m.sem("ada_silu_done"), m.sem("ada_raw_out")
        raw_stored = m.sem("ada_raw_stored")
        ahead_stored = m.sem("ada_ahead_stored")
        raw = ctx.enter_context(nc.sbuf_tensor("ada_raw0", [2, PARTS + AHEAD, PART], F32))
        reloaded, biased, row_done, stored = m.sem("ada_reloaded"), m.sem("ada_biased"), m.sem("ada_row_done"), m.sem("ada_stored")
        m.x_in, m.ident_in = m.sem("x_in"), m.sem("ident_in")
        m.w_in_in = [m.sem(f"w_in_in{c}") for c in range(3)]
        eps_done, x_sq = m.sem("eps_done"), m.sem("ada_x_sq")
        junk = ctx.enter_context(nc.sbuf_tensor("ada_junk", [P, D], F32))

        with nc.Block() as block:
            @block.sync
            def _(sp):
                sp.dma_start(cT[:, 0, :], io["c"].rearrange("o (p k) -> p (o k)", p=P)).then_inc(c_in, 16)
                sp.dma_start(cT[:, 1, :], io["c_ctx"].rearrange("(p k) -> p k", p=P)).then_inc(c_in, 16)

                def load(i):
                    if i >= SLOTS:
                        sp.wait_ge(part_used, i - SLOTS + 1)
                    ada_load(sp, io, *parts[i], ring[:, i % SLOTS], part_in[i % SLOTS])

                for i in range(PARTS):
                    load(i)
                sp.dma_start(m.ident[:], io["k_ident"]).then_inc(m.ident_in, 16)
                sp.dma_start(m.X[:, 0:2, :], io["x"].rearrange("b (t p) d -> p (b t) d", p=P)).then_inc(m.x_in, 16)
                sp.dma_start(m.X[:, 2:4, :], io["ctx"].rearrange("b (t p) d -> p (b t) d", p=P)).then_inc(m.x_in, 16)
                load(PARTS)
                load(PARTS + 1)
                for i in range(PARTS):
                    sp.wait_ge(raw_out, i + 1)
                    ada_store(sp, m, *parts[i], raw, i, raw_stored)
                sp.wait_ge(raw_stored, 16 * PARTS)
                ada_reload(sp, m, 0, reloaded)
                load(PARTS + 2)
                sp.wait_ge(row_done, 1)
                ada_publish(sp, m, 0, stored)
                load(PARTS + 3)
                for i in range(PARTS, PARTS + AHEAD):
                    sp.wait_ge(raw_out, i + 1)
                    ada_store(sp, m, *parts[i], raw, i, ahead_stored)
                sp.wait_ge(ahead_stored, 16 * AHEAD)
                sp.wait_ge(m.x_in, 32)
                sp.wait_ge(m.ident_in, 16)
                sp.wait_ge(stored, 32)

            @block.gpsimd
            def _(pool):
                pool.memset(m.eps[:], EPS).then_inc(eps_done, 1)
                pool.memset(m.grow[:], 1.0).then_inc(ones_done, 1)
                pool.wait_ge(eps_done, 1)

            @block.scalar
            def _(act):
                act.wait_ge(c_in, 32)
                act.activation(m.cS[:], cT[:], ACT.Silu).then_inc(silu_done, 1)
                act.wait_ge(ones_done, 1)
                for b, (layer, v0, nv) in enumerate(BATCHES):
                    for s in range(2):
                        r0 = s * 8 * nv
                        act.dma_start(m.brow[r0:r0 + 8 * nv, b, :], io["ada_b"][layer, v0 * D:(v0 + nv) * D].rearrange("(j n) -> j n", n=P)).then_inc(params_in, 16)
                        for v, g in ((1, 0), (2, 1), (4, 2), (5, 3)):
                            if v0 <= v < v0 + nv:
                                rv = r0 + 8 * (v - v0)
                                act.dma_start(m.grow[rv:rv + 8, b, :], io["norm_g"][layer, g].rearrange("(j n) -> j n", n=P)).then_inc(params_in, 16)
                act.dma_start(m.one[:], io["k_one"]).then_inc(params_in, 16)

                def raw_copy(i):
                    act.wait_ge(part_used, i + 1)
                    act.activation(raw[:, i, :], m.ps[0:2, 6 + i % 2, 0:PART], ACT.Copy).then_inc(raw_out, 1)

                for i in range(PARTS):
                    raw_copy(i)
                act.wait_ge(m.x_in, 32)
                for t in range(TT):
                    if t:
                        act.wait_ge(x_sq, t)
                    act.activation(junk[:], m.X[:, t, :], ACT.Square, accum_out=m.ssq[:, t:t + 1]).then_inc(x_sq, 1)
                    if t < AHEAD:
                        raw_copy(PARTS + t)
            @block.tensor
            def _(pe):
                pe.wait_ge(silu_done, 1)
                for h in range(PARTS + AHEAD):
                    pe.wait_ge(part_in[h % SLOTS], (h // SLOTS + 1) * 16)
                    if h >= 2:
                        pe.wait_ge(raw_out, h - 1)
                    ada_product(pe, m, ring[:, h % SLOTS], 6 + h % 2).then_inc(part_used, 1)

            @block.vector
            def _(dve):
                gains = sum(v0 <= v < v0 + nv for _, v0, nv in BATCHES for v in (1, 2, 4, 5))
                dve.wait_ge(params_in, 16 * (2 * len(BATCHES) + 2 * gains + 1))
                dve.wait_ge(reloaded, 32)
                ada_rows(dve, m, 0, biased, row_done, 1)
                dve.wait_ge(row_done, 1)


def mixer_weights(sp, m, io, c):
    w_in = m.W[:, 2:4, :].rearrange("p a b -> p (a b)").rearrange("p (k n) -> p k n", k=KC)
    sp.dma_start(w_in[:, :, c * 512:c * 512 + 512], io["cf_w_in"][0].rearrange("(p k) n -> p k n", p=P)[:, :, c * 512:c * 512 + 512]).then_inc(m.w_in_in[c], 16)


def mixer_parts(m):
    parts = [(b, h) for b in (1, 2) for h in range(BATCHES[b][2] * D // PART)][AHEAD:-LATE]
    slots = m.W[:, 0:2, :].rearrange("p a b -> p (a b)")[:, KC * D:KC * D + 2 * KC * PART].rearrange("p (s k n) -> p s k n", s=2, k=KC)
    return parts, slots


class LateParts:

    def __init__(self, m):
        last, _, nv = BATCHES[-1]
        n = nv * D // PART
        self.parts = [(len(BATCHES) - 1, h) for h in range(n - LATE, n)]
        _, slots = mixer_parts(m)
        more = m.W[:, 3, 0:2 * KC * PART].rearrange("p (s k n) -> p s k n", s=2, k=KC)
        self.slots = [slots[:, 0], slots[:, 1], more[:, 0], more[:, 1]]
        self.loaded = [m.sem(f"late_loaded{i}") for i in range(LATE)]
        self.used, self.raw_out, self.stored = m.sem("late_used"), m.sem("late_raw_out"), m.sem("late_stored")
        self.reloaded, self.biased, self.row_done, self.published = (m.sem(f"late_{n}") for n in ("reloaded", "biased", "row_done", "published"))

    def load(self, sp, io, i):
        ada_load(sp, io, *self.parts[i], self.slots[i], self.loaded[i])

    def product(self, pe, m, i):
        pe.wait_ge(self.loaded[i], 16)
        ada_product(pe, m, self.slots[i], 4 + i).then_inc(self.used, 1)

    def copy(self, act, m, i):
        act.wait_ge(self.used, i + 1)
        act.activation(m.raw[:, i, :], m.ps[0:2, 4 + i, 0:PART], ACT.Copy).then_inc(self.raw_out, 1)

    def store(self, sp, m, i):
        sp.wait_ge(self.raw_out, i + 1)
        ada_store(sp, m, *self.parts[i], m.raw, i, self.stored)


def mixer_first(m, io):
    m.mix_part_in = [m.sem(f"mix_part_in{i}") for i in range(2)]
    parts, slots = mixer_parts(m)

    def load(sp):
        for i, c in enumerate((1, 0)):
            mixer_weights(sp, m, io, c)
            ada_load(sp, io, *parts[i], slots[:, i], m.mix_part_in[i])

    return load, None


def attention_weights(m, io):
    m.qkv_in = [m.sem(f"att_w_in{c}") for c in range(6)]
    m.wc = m.W[:].rearrange("p a b -> p (a b)").rearrange("p (c k n) -> p c k n", c=6, k=KC)
    return lambda sp: [attention_load(sp, m, io, c) for c in (0, 2)], None


def attention_load(sp, m, io, c):
    sp.dma_start(m.wc[:, c], io["da_w_qkv"][0].rearrange("(p k) n -> p k n", p=P)[:, :, c * 512:c * 512 + 512]).then_inc(m.qkv_in[c], 16)


def route_buffers(nc, ctx, m):
    def sb(name, shape, dt=F32):
        return ctx.enter_context(nc.sbuf_tensor(name, shape, dt))

    m.rb = sb("rb", [P, NE])
    m.tri = sb("trif", [P, P])
    m.low = sb("low", [P, GROUPS, GROUPS])
    m.ecol = sb("ecol", [P, NE])
    m.val = sb("val", [P, TT * TOPK, 2], I32)


def shared_weights(m, io, layer):
    m.sh_in = m.sem(f"moe{layer}_sh_in")
    m.router_in = m.sem(f"moe{layer}_router_in")
    m.rw = m.W[:, 2, 4 * D:4 * D + KC * NE].rearrange("p (k e) -> p k e", k=KC)

    def router(sp):
        sp.dma_start(m.rw, io["moe_router_w"][layer].rearrange("(p k) n -> p k n", p=P)).then_inc(m.router_in, 16)
        sp.dma_start(m.rb[:], io["moe_router_b"][layer].partition_broadcast(P)).then_inc(m.router_in, 16)
        if layer == 0:
            sp.dma_start(m.low[:], io["k_low"].partition_broadcast(P)).then_inc(m.router_in, 16)
            sp.dma_start(m.tri[:], io["k_tri"]).then_inc(m.router_in, 16)
            sp.dma_start(m.ecol[:], io["k_ecol"].partition_broadcast(P)).then_inc(m.router_in, 16)
            sp.dma_start(m.val[:], io["k_val"]).then_inc(m.router_in, 16)

    def shared(sp):
        for n, w in (("gate", wg(m, SHARED)), ("up", wu(m, SHARED))):
            sp.dma_start(w, io[f"moe_sh_{n}"][layer].rearrange("(p k) n -> p k n", p=P)).then_inc(m.sh_in, 16)
        sp.dma_start(wd(m, SHARED), io["moe_sh_down"][layer].rearrange("(k p) n -> p k n", p=P)).then_inc(m.sh_in, 16)

    return router, shared


def wg(m, s):
    return m.W[:, s, 0:2048].rearrange("p (k n) -> p k n", k=KC)


def wu(m, s):
    return m.W[:, s, 2048:4096].rearrange("p (k n) -> p k n", k=KC)


def wd(m, s):
    return m.W[:, s, 4096:6144].rearrange("p (k n) -> p k n", k=2)


def norm_rows(m):
    ab = m.W[:, 2, 0:4 * D].rearrange("p (i s d) -> p i s d", i=2, s=2)
    return ab[:, 0], ab[:, 1]


def norm_rows_load(eng, m, layer, half, streams, done):
    A, B = norm_rows(m)
    for s in range(streams):
        eng.dma_start(A[:, s, :], m.MOD[layer, 3 * half + 1, s, :].partition_broadcast(P)).then_inc(done, 16)
        eng.dma_start(B[:, s, :], m.MOD[layer, 3 * half, s, :].partition_broadcast(P)).then_inc(done, 16)


def modulate(nc, m, io, tag, layer, half, tiles, store, early, late=False):
    nt = len(tiles)
    with ExitStack() as ctx:
        def sb(name, shape, dt=F32):
            return ctx.enter_context(nc.sbuf_tensor(f"{tag}_{name}", shape, dt))

        first = layer == 0 and half == 0
        if first:
            A, B = sb("A", [P, 2, D]), sb("B", [P, 2, D])
            m.rows_in = m.sem(f"{tag}_rows_in")
        else:
            A, B = norm_rows(m)
        h = sb("h", [P, 2, D])
        hp = sb("hp", [P, 2, D])
        std = sb("std", [P, TT])
        rstd = sb("rstd", [P, TT])
        rows_in = m.rows_in
        std_done = m.sem(f"{tag}_std_done")
        rstd_done = m.sem(f"{tag}_rstd_done")
        scaled = m.sem(f"{tag}_scaled")
        h_done = m.sem(f"{tag}_h_done")
        turned = m.sem(f"{tag}_turned")
        hT_done = m.sem(f"{tag}_hT_done")
        h_stored = [m.sem(f"{tag}_h_stored{i}") for i in range(2)]
        streams = 2 if nt > 2 else 1

        with nc.Block() as block:
            @block.sync
            def _(sp):
                for s in range(streams if first else 0):
                    sp.dma_start(A[:, s, :], m.MOD[layer, 1, s, :].partition_broadcast(P)).then_inc(rows_in, 16)
                    sp.dma_start(B[:, s, :], m.MOD[layer, 0, s, :].partition_broadcast(P)).then_inc(rows_in, 16)
                early[0](sp)
                if store:
                    for i, t in enumerate(tiles):
                        sp.wait_ge(h_done, i + 1)
                        sp.dma_start(m.H2[t * P:(t + 1) * P, :], hp[:, i % 2, :]).then_inc(h_stored[i % 2], 16)
                        if late:
                            m.late.store(sp, m, i)
                    early[1](sp)
                    for i in range(2):
                        sp.wait_ge(h_stored[i], 16 * (nt // 2))

            @block.scalar
            def _(act):
                act.activation(std[:, 0:nt], m.ssq[:, 0:nt], ACT.Sqrt, bias=m.eps[:], scale=1.0 / D).then_inc(std_done, 1)
                for i, t in enumerate(tiles):
                    if late:
                        m.late.copy(act, m, i)
                    act.wait_ge(turned, i + 1)
                    act.activation(m.hT[:, :, t * P:(t + 1) * P], bank2(m, 2 * (i % 2)).rearrange("p (k t) -> p k t", k=KC), ACT.Copy).then_inc(hT_done, 1)

            @block.vector
            def _(dve):
                dve.wait_ge(std_done, 1)
                dve.reciprocal(rstd[:, 0:nt], std[:, 0:nt]).then_inc(rstd_done, 1)
                dve.wait_ge(rstd_done, 1)
                dve.wait_ge(rows_in, 32 * streams)
                for i, t in enumerate(tiles):
                    s = t // 2
                    dve.scalar_tensor_tensor(h[:, i % 2, :], m.X[:, t, :], rstd[:, i:i + 1], A[:, s, :], ALU.mult, ALU.mult).then_inc(scaled, 1)
                    dve.wait_ge(scaled, i + 1)
                    if i >= 2:
                        dve.wait_ge(turned, i - 1)
                        if store:
                            dve.wait_ge(h_stored[i % 2], 16 * (i // 2))
                    dve.tensor_tensor(hp[:, i % 2, :].rearrange("t (k p) -> t p k", k=KC), h[:, i % 2, :].rearrange("t (p k) -> t p k", k=KC),
                                      B[:, s, :].rearrange("t (p k) -> t p k", k=KC), ALU.add).then_inc(h_done, 1)

            @block.tensor
            def _(pe):
                for i in range(nt):
                    if late:
                        m.late.product(pe, m, i)
                    pe.wait_ge(h_done, i + 1)
                    if i >= 2:
                        pe.wait_ge(hT_done, i - 1)
                    for k in range(KC):
                        mm = pe.transpose(m.ps[:, 2 * (i % 2) + k // 4, (k % 4) * P:(k % 4 + 1) * P], hp[:, i % 2, k * P:(k + 1) * P], m.ident[:])
                    mm.then_inc(turned, 1)


def mixer(nc, m, io):
    with ExitStack() as ctx:
        def sb(name, shape, dt=F32):
            return ctx.enter_context(nc.sbuf_tensor(f"mix_{name}", shape, dt))

        w_in = m.W[:, 2:4, :].rearrange("p a b -> p (a b)").rearrange("p (k n) -> p k n", k=KC)
        w_out = m.W[:, 0:2, :].rearrange("p a b -> p (a b)")[:, 0:KC * D].rearrange("p (k n) -> p k n", k=KC)
        apad = sb("apad", [P, CJ, 2, SEQ + 2 * PAD])
        sg = sb("sg", [P, 2, 512])
        fT = sb("fT", [P, 4, 512])
        P1 = sb("P1", [P, TT, 4, 256])
        mixT = sb("mixT", [P, KC, 512])
        fch = sb("fch", [P, 256])
        fseq = sb("fseq", [P, 2, 512])
        gmean = sb("gmean", [P, P])
        prow = sb("prow", [CONV_W + 3, 512])
        pcol = sb("pcol", [P, CJ, 64])
        G = m.W[:, 3, 4 * D:6 * D].rearrange("p (s d) -> p s d", s=2)
        ssq = sb("ssq", [P, TT])
        std4 = sb("std4", [P, TT])
        rstd4 = sb("rstd4", [P, TT])
        sq = P1[:].rearrange("p a b c -> p (a b c)")[:, 0:1024].rearrange("p (j n) -> p j n", j=2)
        sd = P1[:].rearrange("p a b c -> p (a b c)")[:, 1024:2048].rearrange("p (j n) -> p j n", j=2)
        junk = P1[:].rearrange("p a b c -> p (a b c)")[:, 2048:3072]
        tmp = P1[:].rearrange("p a b c -> p (a b c)")[:, 3072:4096]
        xjunk = P1[:].rearrange("p a b c -> p (a b c)")[:, 0:1024]

        s = m.sem
        consts_in, gate_in, w_out_in = s("mix_consts_in"), s("mix_gate_in"), s("mix_w_out_in")
        params_turned, params_done = s("mix_params_turned"), s("mix_params_done")
        padded = s("mix_padded")
        u_done, gate_done, val_done, f_done = s("mix_u_done"), s("mix_gate_done"), s("mix_val_done"), s("mix_f_done")
        ch_done, ch_out, seq_done, seq_out = s("mix_ch_done"), s("mix_ch_out"), s("mix_seq_done"), s("mix_seq_out")
        tap, conv_done = s("mix_tap"), s("mix_conv_done")
        mean_done, centred, squared = s("mix_mean_done"), s("mix_centred"), s("mix_squared")
        var_done, std_done, rec_done, normed, a_done = s("mix_var_done"), s("mix_std_done"), s("mix_rec_done"), s("mix_normed"), s("mix_a_done")
        y_done, y_sq, y_std, y_rec, y_scaled, x_done = s("mix_y_done"), s("mix_y_sq"), s("mix_y_std"), s("mix_y_rec"), s("mix_y_scaled"), s("mix_x_done")
        x_sq = s("mix_x_sq")
        m.rows_in = s("m01_rows_in")
        part_in = m.mix_part_in
        part_used, raw_out, biased, row_done = (s(f"mix_{n}") for n in ("part_used", "raw_out", "biased", "row_done"))
        raw_stored = [s(f"mix_raw_stored{i}") for i in range(4)]
        reloaded = s("mix_reloaded")
        stored = s("mix_stored")
        m.late = LateParts(m)
        parts, slots = mixer_parts(m)
        FIRST = BATCHES[1][2] * D // PART - AHEAD

        with nc.Block() as block:
            @block.sync
            def _(sp):
                sp.dma_start(prow[0:CONV_W, :], io["cf_conv_w"][0].rearrange("w o c -> w (o c)")).then_inc(consts_in, 16)
                for i, n in enumerate(("cf_conv_b", "cf_ln_g", "cf_ln_b")):
                    sp.dma_start(prow[CONV_W + i:CONV_W + i + 1, :], io[n]).then_inc(consts_in, 16)
                sp.dma_start(fch[:], io["k_fch"]).then_inc(consts_in, 16)
                sp.dma_start(fseq[:], io["k_fseq"]).then_inc(consts_in, 16)
                sp.dma_start(gmean[:], io["k_gmean"]).then_inc(consts_in, 16)

                def raw_store(i):
                    sp.wait_ge(raw_out, i + 1)
                    ada_store(sp, m, *parts[i], m.raw, i % 4, raw_stored[i % 4])

                for i, (b, h) in enumerate(parts):
                    if i >= 2:
                        sp.wait_ge(part_used, i - 1)
                        ada_load(sp, io, b, h, slots[:, i % 2], part_in[i % 2])
                        raw_store(i - 2)
                    if i == 3:
                        mixer_weights(sp, m, io, 2)
                    if i == 7:
                        sp.dma_start(w_out, io["cf_w_out"][0].rearrange("(k p) n -> p k n", p=P)).then_inc(w_out_in, 16)
                sp.wait_ge(u_done, 3 * CJ)
                for i in (2, 3):
                    m.late.load(sp, io, i)
                for i in range(2):
                    sp.wait_ge(part_used, len(parts) - 1 + i)
                    m.late.load(sp, io, i)
                    raw_store(len(parts) - 2 + i)
                for i in range(4):
                    sp.wait_ge(raw_stored[i], 16 * (len(parts) // 4))

            @block.gpsimd
            def _(pool):
                pool.memset(apad[:], 0.0).then_inc(padded, 1)
                for i in range(4):
                    pool.wait_ge(raw_stored[i], 16 * (FIRST // 4))
                ada_reload(pool, m, 1, reloaded)
                pool.wait_ge(row_done, 1)
                ada_publish(pool, m, 1, stored)
                pool.wait_ge(stored, 32)

            @block.tensor
            def _(pe):
                part = [0]

                def ada(count):
                    for i in range(part[0], min(part[0] + count, len(parts))):
                        pe.wait_ge(part_in[i % 2], (i // 2 + 1) * 16)
                        if i >= 2:
                            pe.wait_ge(raw_out, i - 1)
                        ada_product(pe, m, slots[:, i % 2], (5, 7)[i % 2]).then_inc(part_used, 1)
                    part[0] = min(part[0] + count, len(parts))

                def mean(j):
                    if j:
                        pe.wait_ge(centred, j)
                    pe.wait_ge(conv_done, j + 1)
                    pe.matmul(m.ps[:, 4, :], gmean[:], mixT[:, j, :], start=True, stop=True).then_inc(mean_done, 1)

                def var(j):
                    if j:
                        pe.wait_ge(std_done, j)
                    pe.wait_ge(squared, j + 1)
                    pe.matmul(m.ps[:, 6, :], gmean[:], sq[:, j % 2, :], start=True, stop=True).then_inc(var_done, 1)

                order = [x for j in range(CJ) for x in (CJ + j, j)] + [2 * CJ + g for g in range(4)]
                for n, mt in enumerate(order):
                    if n in (0, 1, 8):
                        pe.wait_ge(m.w_in_in[mt // CJ], 16)
                    if n >= 4:
                        q = n - 4
                        if q < 8:
                            pe.wait_ge((gate_done, val_done)[q % 2], q // 2 + 1)
                        else:
                            pe.wait_ge(f_done, q - 7)
                    for k in range(KC):
                        mm = pe.matmul(m.ps[:, n % 4, :], w_in[:, k, mt * P:(mt + 1) * P], m.hT[:, k, :], start=(k == 0), stop=(k == KC - 1))
                        if k == KC - 1:
                            mm.then_inc(u_done, 1)
                        if k % 4 == 3:
                            ada(1)
                    if n == 0:
                        pe.wait_ge(consts_in, 16 * 7)
                        for j in range(CJ):
                            mm = pe.transpose(m.ps[:, 6, j * 64:j * 64 + CONV_W + 3], prow[:, j * P:(j + 1) * P], m.ident[0:CONV_W + 3, 0:CONV_W + 3])
                        mm.then_inc(params_turned, 1)
                    if n >= 3:
                        if n == 3:
                            pe.wait_ge(params_done, 1)
                        if (n - 3) % 2 == 0 and n < 11:
                            mean((n - 3) // 2)
                        elif n < 11:
                            var((n - 4) // 2)
                pe.wait_ge(f_done, 4)
                pe.wait_ge(centred, CJ)
                pe.wait_ge(std_done, CJ)
                for n in range(2 * TT):
                    t, gp = n // 2, n % 2
                    if n >= 2:
                        pe.wait_ge(ch_out, n - 1)
                    for g in (2 * gp, 2 * gp + 1):
                        mm = pe.matmul(m.ps[:, 4 + 2 * (n % 2), (g % 2) * 256:(g % 2) * 256 + 256], fT[:, g, t * P:(t + 1) * P], fch[:], start=True, stop=True)
                    mm.then_inc(ch_done, 1)
                    if n % 4 == 3:
                        ada(1)
                pe.wait_ge(ch_out, 2 * TT)
                for g in range(4):
                    for st in range(2):
                        for n in range(4):
                            kt, cs = n // 2, n % 2
                            mm = pe.matmul(m.ps[:, g, st * 256:st * 256 + 256], P1[:, 2 * st + kt, g, cs * P:(cs + 1) * P],
                                           fseq[:, kt, cs * 256:cs * 256 + 256], start=(n == 0), stop=(n == 3))
                    mm.then_inc(seq_done, 1)
                    ada(1)
                pe.wait_ge(w_out_in, 16)
                pe.wait_ge(a_done, CJ)
                pe.wait_ge(seq_out, 4)
                for t in range(TT):
                    if t >= 2:
                        pe.wait_ge(y_scaled, t - 1)
                    for n in range(2):
                        for k in range(KC):
                            mm = pe.matmul(m.ps[:, 2 * (t % 2) + n, :], mixT[:, k, t * P:(t + 1) * P], w_out[:, k, n * 512:n * 512 + 512],
                                           start=(k == 0), stop=(k == KC - 1))
                            if n == 1 and k == KC - 1:
                                mm.then_inc(y_done, 1)
                            if k % 4 == 3:
                                ada(1)

            @block.scalar
            def _(act):
                def std(j):
                    act.wait_ge(var_done, j + 1)
                    if j >= 2:
                        act.wait_ge(normed, j - 1)
                    act.activation(sd[:, j % 2, :], m.ps[:, 6, :], ACT.Sqrt, bias=m.eps[:]).then_inc(std_done, 1)

                def silu(j):
                    act.wait_ge(normed, j + 1)
                    act.activation(mixT[:, j, :], mixT[:, j, :], ACT.Silu, bias=pcol[:, j, CONV_W + 2:CONV_W + 3], scale=pcol[:, j, CONV_W + 1:CONV_W + 2]).then_inc(a_done, 1)

                def square(j):
                    act.wait_ge(centred, j + 1)
                    if j >= 2:
                        act.wait_ge(var_done, j - 1)
                    act.activation(sq[:, j % 2, :], mixT[:, j, :], ACT.Square).then_inc(squared, 1)

                def x_square(t):
                    act.wait_ge(x_done, t + 1)
                    if t:
                        act.wait_ge(x_sq, t)
                    act.activation(xjunk, m.X[:, t, :], ACT.Square, accum_out=m.ssq[:, t:t + 1]).then_inc(x_sq, 1)

                part = [0]

                def raw(count):
                    for i in range(part[0], min(part[0] + count, len(parts))):
                        act.wait_ge(part_used, i + 1)
                        if i >= 4:
                            act.wait_ge(raw_stored[i % 4], 16 * (i // 4))
                        act.activation(m.raw[:, i % 4, :], m.ps[0:2, (5, 7)[i % 2], 0:PART], ACT.Copy).then_inc(raw_out, 1)
                    part[0] = min(part[0] + count, len(parts))

                def f_copy(g):
                    act.wait_ge(u_done, 9 + g)
                    act.activation(fT[:, g, :], m.ps[:, g % 4, :], ACT.Copy).then_inc(f_done, 1)

                for n in range(CJ * 3):
                    raw(1)
                    if n >= 2 * CJ:
                        f_copy(n - 2 * CJ)
                    elif n % 2 == 0:
                        j = n // 2
                        act.wait_ge(u_done, n + 1)
                        if j >= 2:
                            act.wait_ge(val_done, j - 1)
                        act.activation(sg[:, j % 2, :], m.ps[:, n % 4, :], ACT.Sigmoid).then_inc(gate_done, 1)
                    raw(1)
                    if n % 2 and n >= 3:
                        if n >= 5:
                            silu((n - 5) // 2)
                        if n < 11:
                            square((n - 3) // 2)
                    elif n >= 4:
                        std((n - 4) // 2)
                for n in range(2 * TT):
                    act.wait_ge(ch_done, n + 1)
                    act.activation(P1[:, n // 2, 2 * (n % 2):2 * (n % 2) + 2, :], m.ps[:, 4 + 2 * (n % 2), :].rearrange("p (g c) -> p g c", g=2), ACT.Copy).then_inc(ch_out, 1)
                    if n % 4 == 3:
                        raw(1)
                act.wait_ge(stored, 32)
                for i in range(2):
                    act.dma_start(G[:, i, :], m.MOD[0, 2, i, :].partition_broadcast(P)).then_inc(gate_in, 16)
                for g in range(4):
                    act.wait_ge(seq_done, g + 1)
                    act.activation(mixT[:, 4 + g, :], m.ps[:, g, :], ACT.Copy).then_inc(seq_out, 1)
                    raw(1)
                norm_rows_load(act, m, 0, 1, 2, m.rows_in)
                for t in range(TT):
                    raw(3)
                    act.wait_ge(y_done, t + 1)
                    if t:
                        act.wait_ge(y_sq, t)
                    act.activation(junk, bank2(m, 2 * (t % 2)), ACT.Square, accum_out=ssq[:, t:t + 1]).then_inc(y_sq, 1)
                    act.wait_ge(y_sq, t + 1)
                    act.activation(std4[:, t:t + 1], ssq[:, t:t + 1], ACT.Sqrt, bias=m.eps[:], scale=1.0 / D).then_inc(y_std, 1)
                    raw(1)
                    if t:
                        x_square(t - 1)
                x_square(TT - 1)

            @block.vector
            def _(dve):
                dve.wait_ge(params_turned, 1)
                dve.tensor_copy(pcol[:, :, 0:CONV_W + 3], m.ps[:, 6, 0:256].rearrange("p (j w) -> p j w", j=CJ)[:, :, 0:CONV_W + 3]).then_inc(params_done, 1)
                dve.wait_ge(padded, 1)
                dve.wait_ge(params_done, 1)
                taps = [0]

                def conv(j):
                    dve.wait_ge(gate_done, j + 1)
                    dve.wait_ge(u_done, 2 * j + 2)
                    dve.tensor_tensor(apad[:, j, :, PAD:PAD + SEQ], m.ps[:, (2 * j + 1) % 4, :].rearrange("p (s n) -> p s n", s=2),
                                      sg[:, j % 2, :].rearrange("p (s n) -> p s n", s=2), ALU.mult).then_inc(val_done, 1)
                    dve.wait_ge(val_done, j + 1)
                    acc = mixT[:, j, :].rearrange("p (s n) -> p s n", s=2)
                    dve.tensor_scalar(acc, apad[:, j, :, 0:SEQ], pcol[:, j, 0:1], pcol[:, j, CONV_W:CONV_W + 1], ALU.mult, ALU.add).then_inc(tap, 1)
                    taps[0] += 1
                    for w in range(1, CONV_W):
                        dve.wait_ge(tap, taps[0])
                        last = dve.scalar_tensor_tensor(acc, apad[:, j, :, w:w + SEQ], pcol[:, j, w:w + 1], acc, ALU.mult, ALU.add)
                        if w < CONV_W - 1:
                            last.then_inc(tap, 1)
                            taps[0] += 1
                        else:
                            last.then_inc(conv_done, 1)

                def centre(j):
                    dve.wait_ge(mean_done, j + 1)
                    dve.tensor_tensor(mixT[:, j, :], mixT[:, j, :], m.ps[:, 4, :], ALU.subtract).then_inc(centred, 1)

                def norm(j):
                    dve.wait_ge(std_done, j + 1)
                    dve.reciprocal(sd[:, j % 2, :], sd[:, j % 2, :]).then_inc(rec_done, 1)
                    dve.wait_ge(rec_done, j + 1)
                    dve.wait_ge(squared, j + 1)
                    dve.tensor_tensor(mixT[:, j, :], mixT[:, j, :], sd[:, j % 2, :], ALU.mult).then_inc(normed, 1)

                for j in range(CJ):
                    conv(j)
                    if j:
                        norm(j - 1)
                    centre(j)
                norm(CJ - 1)
                dve.wait_ge(reloaded, 32)
                ada_rows(dve, m, 1, biased, row_done, 1)
                dve.wait_ge(gate_in, 32)
                for t in range(TT):
                    dve.wait_ge(y_std, t + 1)
                    dve.reciprocal(rstd4[:, t:t + 1], std4[:, t:t + 1]).then_inc(y_rec, 1)
                    dve.wait_ge(y_rec, t + 1)
                    if t:
                        dve.wait_ge(x_done, t)
                    dve.scalar_tensor_tensor(tmp, bank2(m, 2 * (t % 2)), rstd4[:, t:t + 1], G[:, t // 2, :], ALU.mult, ALU.mult).then_inc(y_scaled, 1)
                    dve.wait_ge(y_scaled, t + 1)
                    dve.tensor_tensor(m.X[:, t, :], m.X[:, t, :], tmp, ALU.add).then_inc(x_done, 1)


def attention(nc, m, io):
    lam_init = 0.8 - 0.6 * math.exp(-0.3)
    scale = QK ** -0.5
    with ExitStack() as ctx:
        def sb(name, shape, dt=F32):
            return ctx.enter_context(nc.sbuf_tensor(f"att_{name}", shape, dt))

        wc = m.wc
        qT = sb("qT", [P, HEADS, SEQ])
        kT = sb("kT", [P, HEADS, 2 * SEQ])
        v = sb("v", [P, TT, D])
        cosT, sinT = sb("cosT", [P, SEQ]), sb("sinT", [P, SEQ])
        rot = sb("rot", [P, P])
        t1, t2 = sb("t1", [P, SEQ]), sb("t2", [P, SEQ])
        lp = sb("lp", [P, 4 * QK])
        lj = sb("lj", [P, 2 * QK])
        ls, le, nlam = sb("ls", [P, 2]), sb("le", [P, 2]), sb("nlam", [P, 1])
        mx, nm, sm, rs = (sb(n, [P, 2 * HEADS, 2]) for n in ("mx", "nm", "sm", "rs"))
        cf = sb("cf", [P, 2 * HEADS])
        p0, p1 = sb("p0", [P, 2, 512]), sb("p1", [P, 2, 512])
        pdT = sb("pdT", [P, 2, 512])
        o = sb("o", [P, 2, D])
        osq = sb("osq", [P, P])
        ss8, st8, r8 = (sb(n, [P, 2, HEADS]) for n in ("ss8", "st8", "r8"))
        sub = sb("sub", [P, 1])
        subs = sb("subs", [P, 1])
        G = sb("G", [P, D])
        tmp = sb("tmp", [P, D])
        ssq, std, rstd = (sb(n, [P, 2]) for n in ("ssq", "std", "rstd"))
        oT = m.hT[:, :, 0:SEQ]

        s = m.sem
        w_in = m.qkv_in
        consts_in, w_out_in = s("att_consts_in"), s("att_w_out_in")
        lam_step, lam_sum, lam_exp = s("att_lam_step"), s("att_lam_sum"), s("att_lam_exp")
        raw_done, raw_out, turned, t1_done, t2_done, roped = (s(f"att_{n}") for n in ("raw_done", "raw_out", "turned", "t1_done", "t2_done", "roped"))
        v_done, v_out = s("att_v_done"), s("att_v_out")
        s_done, max_done, neg_done, exp_done, rec_done, cf_done, p1_done, pd_done = (
            s(f"att_{n}") for n in ("s_done", "max_done", "neg_done", "exp_done", "rec_done", "cf_done", "p1_done", "pd_done"))
        pT_done, pT_out, o_done, o_out = (s(f"att_{n}") for n in ("pT_done", "pT_out", "o_done", "o_out"))
        o_sq, o_std, o_rec, o_norm, oT_done, oT_out = (s(f"att_{n}") for n in ("o_sq", "o_std", "o_rec", "o_norm", "oT_done", "oT_out"))
        y_done, y_sq, y_std, y_rec, y_scaled, x_done = (s(f"att_y{n}") for n in ("_done", "_sq", "_std", "_rec", "_scaled", "_x"))
        x_sq = s("att_x_sq")
        m.rows_in = s("m11_rows_in")
        UNITS = 2 * HEADS
        CONSTS = 16 * 6

        with nc.Block() as block:
            @block.sync
            def _(sp):
                sp.dma_start(cosT[:], io["k_cos"]).then_inc(consts_in, 16)
                sp.dma_start(sinT[:], io["k_sin"]).then_inc(consts_in, 16)
                sp.dma_start(rot[:], io["k_rot"]).then_inc(consts_in, 16)
                sp.dma_start(lp[:], io["da_lambda"][0].rearrange("a b -> (a b)").partition_broadcast(P)).then_inc(consts_in, 16)
                sp.dma_start(G[:], m.MOD[1, 2, 0, :].partition_broadcast(P)).then_inc(consts_in, 16)
                sp.dma_start(sub[:], io["da_subln_g"].rearrange("a p -> p a")).then_inc(consts_in, 16)
                for c in (1, 3, 4, 5):
                    attention_load(sp, m, io, c)
                sp.wait_ge(raw_done, UNITS)
                for n in range(2):
                    sp.dma_start(wc[:, n], io["da_w_out"][0].rearrange("(k p) n -> p k n", p=P)[:, :, n * 512:n * 512 + 512]).then_inc(w_out_in, 16)
                norm_rows_load(sp, m, 1, 1, 1, m.rows_in)

            @block.tensor
            def _(pe):
                def rotate(u):
                    hd, is_k = u // 2, u % 2
                    pe.wait_ge(raw_out, u + 1)
                    if u >= 2:
                        pe.wait_ge(t2_done, u - 1)
                    src = kT[:, hd, 0:SEQ] if is_k else qT[:, hd, :]
                    pe.matmul(m.ps[:, 2 + u % 2, 0:SEQ], rot[:], src, start=True, stop=True).then_inc(turned, 1)

                for u in range(UNITS):
                    hd, is_k = u // 2, u % 2
                    c, n = 2 * is_k + hd // 4, SEQ * (1 + is_k)
                    pe.wait_ge(w_in[c], 16)
                    if u >= 2:
                        pe.wait_ge(raw_out, u - 1)
                    for k in range(KC):
                        mm = pe.matmul(m.ps[:, u % 2, 0:n], wc[:, c, k, (hd % 4) * P:(hd % 4 + 1) * P], m.hT[:, k, 0:n], start=(k == 0), stop=(k == KC - 1))
                    mm.then_inc(raw_done, 1)
                    if u == 0:
                        pe.wait_ge(consts_in, CONSTS)
                    else:
                        rotate(u - 1)
                for i in range(2 * TT):
                    t, n = i // 2, i % 2
                    pe.wait_ge(w_in[4 + n], 16)
                    if i >= 2:
                        pe.wait_ge(v_out, i - 1)
                    for k in range(KC):
                        mm = pe.matmul(m.ps[:, 4 + i % 2, :], m.hT[:, k, t * P:(t + 1) * P], wc[:, 4 + n, k, :], start=(k == 0), stop=(k == KC - 1))
                    mm.then_inc(v_done, 1)
                    if i == 0:
                        rotate(UNITS - 1)
                pe.wait_ge(v_out, 2 * TT)
                pe.wait_ge(roped, UNITS)

                def scores(a):
                    hd, qt = a // 2, a % 2
                    if a >= 3:
                        pe.wait_ge(exp_done, 2 * (a - 2))
                    for c in range(2):
                        mm = pe.matmul(m.ps[:, 2 * (a % 3) + c, :], qT[c * QK:(c + 1) * QK, hd, qt * P:(qt + 1) * P], kT[c * QK:(c + 1) * QK, hd, :], start=True, stop=True)
                        mm.then_inc(s_done, 1)

                def turn_weights(a):
                    pe.wait_ge(pd_done, a + 1)
                    if a:
                        pe.wait_ge(pT_out, a)
                    for t in range(TT):
                        mm = pe.transpose(m.ps[:, 6, t * P:(t + 1) * P], p0[:, a % 2, t * P:(t + 1) * P], m.ident[:])
                    mm.then_inc(pT_done, 1)

                def values(a):
                    hd = a // 2
                    pe.wait_ge(pT_out, a + 1)
                    if a:
                        pe.wait_ge(o_out, a)
                    for t in range(TT):
                        mm = pe.matmul(m.ps[:, 7, 0:P], pdT[:, a % 2, t * P:(t + 1) * P], v[:, t, hd * P:(hd + 1) * P], start=(t == 0), stop=(t == TT - 1))
                    mm.then_inc(o_done, 1)

                for a in range(2 * HEADS + 3):
                    if a < 2 * HEADS:
                        scores(a)
                    if 0 <= a - 2 < 2 * HEADS:
                        turn_weights(a - 2)
                    if a >= 3:
                        values(a - 3)
                for qt in range(2):
                    pe.wait_ge(o_norm, qt + 1)
                    for k in range(KC):
                        mm = pe.transpose(m.ps[:, 2 * qt + k // 4, (k % 4) * P:(k % 4 + 1) * P], o[:, qt, k * P:(k + 1) * P], m.ident[:])
                    mm.then_inc(oT_done, 1)
                pe.wait_ge(w_out_in, 32)
                pe.wait_ge(o_out, 2 * HEADS)
                for qt in range(2):
                    pe.wait_ge(oT_out, qt + 1)
                    for n in range(2):
                        for k in range(KC):
                            mm = pe.matmul(m.ps[:, 4 + 2 * qt + n, :], oT[:, k, qt * P:(qt + 1) * P], wc[:, n, k, :], start=(k == 0), stop=(k == KC - 1))
                    mm.then_inc(y_done, 1)

            @block.scalar
            def _(act):
                for u in range(UNITS):
                    hd, is_k = u // 2, u % 2
                    act.wait_ge(raw_done, u + 1)
                    dst = kT[:, hd, :] if is_k else qT[:, hd, :]
                    act.activation(dst, m.ps[:, u % 2, 0:SEQ * (1 + is_k)], ACT.Copy).then_inc(raw_out, 1)
                for i in range(2 * TT):
                    act.wait_ge(v_done, i + 1)
                    act.activation(v[:, i // 2, (i % 2) * 512:(i % 2) * 512 + 512], m.ps[:, 4 + i % 2, :], ACT.Copy).then_inc(v_out, 1)
                act.wait_ge(lam_sum, 2)
                act.activation(le[:], ls[:], ACT.Exp).then_inc(lam_exp, 1)

                def exps(a):
                    act.wait_ge(neg_done, a + 1)
                    if a >= 2:
                        act.wait_ge(pT_done, a - 1)
                    for c, pc in enumerate((p0, p1)):
                        act.activation(pc[:, a % 2, :], m.ps[:, 2 * (a % 3) + c, :], ACT.Exp, bias=nm[:, a, c:c + 1], scale=scale,
                                       accum_out=sm[:, a, c:c + 1]).then_inc(exp_done, 1)

                def weights_copy(a):
                    act.wait_ge(pT_done, a + 1)
                    if a >= 2:
                        act.wait_ge(o_done, a - 1)
                    act.activation(pdT[:, a % 2, :], m.ps[:, 6, :], ACT.Copy).then_inc(pT_out, 1)

                def output_copy(a):
                    act.wait_ge(o_done, a + 1)
                    if a:
                        act.wait_ge(o_sq, a)
                    act.activation(osq[:], m.ps[:, 7, 0:P], ACT.Square, accum_out=ss8[:, a % 2, a // 2:a // 2 + 1]).then_inc(o_sq, 1)
                    act.activation(o[:, a % 2, (a // 2) * P:(a // 2 + 1) * P], m.ps[:, 7, 0:P], ACT.Copy).then_inc(o_out, 1)

                for a in range(2 * HEADS + 3):
                    if 0 <= a - 2 < 2 * HEADS:
                        weights_copy(a - 2)
                    if a < 2 * HEADS:
                        exps(a)
                    if a >= 3:
                        output_copy(a - 3)
                for qt in range(2):
                    act.wait_ge(o_sq, 2 * HEADS)
                    act.activation(st8[:, qt, :], ss8[:, qt, :], ACT.Sqrt, bias=m.eps[:], scale=1.0 / P).then_inc(o_std, 1)
                for qt in range(2):
                    act.wait_ge(oT_done, qt + 1)
                    act.wait_ge(lam_step, 3)
                    act.activation(oT[:, :, qt * P:(qt + 1) * P], bank2(m, 2 * qt).rearrange("p (k t) -> p k t", k=KC), ACT.Copy, scale=subs[:]).then_inc(oT_out, 1)
                for qt in range(2):
                    act.wait_ge(y_done, qt + 1)
                    act.activation(v[:, qt, :], bank2(m, 4 + 2 * qt), ACT.Square, accum_out=ssq[:, qt:qt + 1]).then_inc(y_sq, 1)
                    act.wait_ge(y_sq, qt + 1)
                    act.activation(std[:, qt:qt + 1], ssq[:, qt:qt + 1], ACT.Sqrt, bias=m.eps[:], scale=1.0 / D).then_inc(y_std, 1)
                for t in range(2):
                    act.wait_ge(x_done, t + 1)
                    act.activation(v[:, 2 + t, :], m.X[:, t, :], ACT.Square, accum_out=m.ssq[:, t:t + 1]).then_inc(x_sq, 1)

            @block.vector
            def _(dve):
                dve.wait_ge(consts_in, CONSTS)
                dve.tensor_scalar(subs[:], sub[:], 1.0 - lam_init, None, ALU.mult).then_inc(lam_step, 1)
                for i in range(2):
                    dve.tensor_tensor(lj[:, i * QK:(i + 1) * QK], lp[:, 2 * i * QK:(2 * i + 1) * QK], lp[:, (2 * i + 1) * QK:(2 * i + 2) * QK], ALU.mult).then_inc(lam_step, 1)
                dve.wait_ge(lam_step, 3)
                for i in range(2):
                    dve.tensor_reduce(ls[:, i:i + 1], lj[:, i * QK:(i + 1) * QK], AX.X, ALU.add).then_inc(lam_sum, 1)
                for u in range(UNITS):
                    hd, is_k = u // 2, u % 2
                    dst = kT[:, hd, 0:SEQ] if is_k else qT[:, hd, :]
                    dve.wait_ge(turned, u + 1)
                    if u:
                        dve.wait_ge(roped, u)
                    dve.tensor_tensor(t1[:], dst, cosT[:], ALU.mult).then_inc(t1_done, 1)
                    dve.tensor_tensor(t2[:], m.ps[:, 2 + u % 2, 0:SEQ], sinT[:], ALU.mult).then_inc(t2_done, 1)
                    dve.wait_ge(t1_done, u + 1)
                    dve.wait_ge(t2_done, u + 1)
                    dve.tensor_tensor(dst, t1[:], t2[:], ALU.add).then_inc(roped, 1)
                dve.wait_ge(lam_exp, 1)
                dve.tensor_tensor(nlam[:], le[:, 1:2], le[:, 0:1], ALU.subtract).then_inc(lam_step, 1)
                dve.wait_ge(lam_step, 4)
                dve.tensor_scalar(nlam[:], nlam[:], -lam_init, None, ALU.add).then_inc(lam_step, 1)
                dve.wait_ge(lam_step, 5)

                def weights(a):
                    dve.wait_ge(exp_done, 2 * a + 2)
                    dve.reciprocal(rs[:, a, :], sm[:, a, :]).then_inc(rec_done, 1)
                    dve.wait_ge(rec_done, a + 1)
                    dve.tensor_tensor(cf[:, a:a + 1], rs[:, a, 1:2], nlam[:], ALU.mult).then_inc(cf_done, 1)
                    dve.wait_ge(cf_done, a + 1)
                    dve.tensor_scalar(p1[:, a % 2, :], p1[:, a % 2, :], cf[:, a:a + 1], None, ALU.mult).then_inc(p1_done, 1)
                    dve.wait_ge(p1_done, a + 1)
                    dve.scalar_tensor_tensor(p0[:, a % 2, :], p0[:, a % 2, :], rs[:, a, 0:1], p1[:, a % 2, :], ALU.mult, ALU.add).then_inc(pd_done, 1)

                for a in range(2 * HEADS):
                    dve.wait_ge(s_done, 2 * a + 2)
                    dve.tensor_reduce(mx[:, a, :], m.ps[:, 2 * (a % 3):2 * (a % 3) + 2, :], AX.X, ALU.max).then_inc(max_done, 1)
                    dve.wait_ge(max_done, a + 1)
                    dve.tensor_scalar(nm[:, a, :], mx[:, a, :], -scale, None, ALU.mult).then_inc(neg_done, 1)
                    if a:
                        weights(a - 1)
                weights(2 * HEADS - 1)
                dve.wait_ge(o_out, 2 * HEADS)
                for qt in range(2):
                    dve.wait_ge(o_std, qt + 1)
                    dve.reciprocal(r8[:, qt, :], st8[:, qt, :]).then_inc(o_rec, 1)
                    dve.wait_ge(o_rec, qt + 1)
                    oh = o[:, qt, :].rearrange("p (h d) -> p h d", h=HEADS)
                    dve.tensor_tensor(oh, oh, r8[:, qt, :].unsqueeze(2).broadcast_to([P, HEADS, P]), ALU.mult).then_inc(o_norm, 1)
                for t in range(2):
                    dve.wait_ge(y_std, t + 1)
                    dve.reciprocal(rstd[:, t:t + 1], std[:, t:t + 1]).then_inc(y_rec, 1)
                    dve.wait_ge(y_rec, t + 1)
                    if t:
                        dve.wait_ge(x_done, t)
                    dve.scalar_tensor_tensor(tmp[:], bank2(m, 4 + 2 * t), rstd[:, t:t + 1], G[:], ALU.mult, ALU.mult).then_inc(y_scaled, 1)
                    dve.wait_ge(y_scaled, t + 1)
                    dve.tensor_tensor(m.X[:, t, :], m.X[:, t, :], tmp[:], ALU.add).then_inc(x_done, 1)


def moe(nc, m, io, layer, nt):
    L = f"moe{layer}"
    with ExitStack() as ctx:
        def sb(name, shape, dt=F32):
            return ctx.enter_context(nc.sbuf_tensor(f"{L}_{name}", shape, dt))

        r = Memory()
        r.L, r.layer, r.nt = L, layer, nt
        r.gk = sb("gk", [P, nt, 8])
        r.passes = sb("passes", [1, 4], I32)
        r.counts = sb("counts", [1, NE], I32)
        r.xg = sb("xg", [P, UNROLL, D])
        r.hf_done, r.y_done, r.gu_done = m.sem(f"{L}_hf_done"), m.sem(f"{L}_y_done"), m.sem(f"{L}_gu_done")
        r.x_turned = m.sem(f"{L}_x_turned")
        r.y_out = [m.sem(f"{L}_y_out_{e}") for e in ("act", "dve")]
        r.w_in = [m.sem(f"{L}_w_in{s}") for s in range(UNROLL)]
        r.pass_done = m.sem(f"{L}_pass_done")
        route(nc, m, io, r)
        experts(nc, m, io, r)
        if layer == 0:
            nc.clear_and_free_semaphores(m.used)
            m.used.clear()
            nc.all_engine_barrier()
        combine(nc, m, io, r)


def expert_load(sp, m, io, r, e, s, parts=(0, 1, 2)):
    for part in parts:
        if part < 2:
            name, w = (("gate", wg(m, s)), ("up", wu(m, s)))[part]
            sp.dma_start(w, io[f"moe_w_{name}"][r.layer, e].rearrange("(p k) n -> p k n", p=P)).then_inc(r.w_in[s], 16)
        else:
            sp.dma_start(wd(m, s), io["moe_w_down"][r.layer, e].rearrange("(k p) n -> p k n", p=P)).then_inc(r.w_in[s], 16)


def route(nc, m, io, r):
    nt, L = r.nt, r.L
    with ExitStack() as ctx:
        def sb(name, shape, dt=F32):
            return ctx.enter_context(nc.sbuf_tensor(f"{L}r_{name}", shape, dt))

        lt = sb("lt", [NE, nt * P])
        tri = sb("tri", [P, P], BF16)
        ones = sb("ones", [P, P], BF16)
        empty = sb("empty", [P, ROWS * NE * 2 // P], I32)
        Q = sb("Q", [P, nt, NE])
        pick = sb("pick", [P, TOPK, nt, NE])
        rowf = sb("rowf", [P, TOPK, nt])
        row = sb("row", [P, TOPK, nt], I32)
        shs, shu, shh = (sb(n, [P, 2, 512]) for n in ("shs", "shu", "shh"))
        sc, bi, sel, G, t1, t2 = (sb(n, [P, nt, NE]) for n in ("sc", "bi", "sel", "G", "t1", "t2"))
        selb = sb("selb", [P, nt, NE], BF16)
        m8 = sb("m8", [P, nt, GROUPS, 8])
        gs = sb("gs", [P, nt, GROUPS])
        cmp1, cmp2 = sb("cmp1", [P, nt, GROUPS, GROUPS]), sb("cmp2", [P, nt, GROUPS, GROUPS])
        beat, gm, neg = (sb(n, [P, nt, GROUPS]) for n in ("beat", "gm", "neg"))
        top = sb("top", [P, nt, 8])
        v6 = sb("v6", [P, nt])
        need = sb("need", [P, nt])
        keep = sb("keep", [P, nt, NE])
        cnt = sb("cnt", [1, NE])
        mxc = sb("mxc", [1, 1])
        ge = sb("ge", [1, 4])
        npf = sb("npf", [1, 1])

        s = m.sem
        ones_done, logits_done, scored = (s(f"{L}_{n}") for n in ("rones", "logits", "scored"))
        chain, sel_done, pos_done, route_done = (s(f"{L}_{n}") for n in ("rchain", "sel", "pos", "routed"))
        filled, row_done, tabled = (s(f"{L}_{n}") for n in ("filled", "row", "tabled"))
        keep_step = s(f"{L}_keep_step")
        empty_done, cleared = s(f"{L}_empty"), s(f"{L}_cleared")
        lt_out, lt_turned = s(f"{L}_lt_out"), s(f"{L}_lt_turned")
        sh_g, sh_u, sh_s, sh_c, sh_h, sh_y, sh_out = (s(f"{L}_{n}") for n in ("sh_g", "sh_u", "sh_s", "sh_c", "sh_h", "sh_y", "sh_out"))
        HT = nt * P
        CONSTS = 16 * (6 if r.layer == 0 else 2)

        with nc.Block() as block:
            @block.sync
            def _(sp):
                sp.wait_ge(empty_done, 1)
                sp.dma_start(m.TAB.rearrange("(p r) c -> p (r c)", p=P), empty[:]).then_inc(filled, 16)
                for n in range(SHARED):
                    if n == 2:
                        sp.wait_ge(logits_done, 1)
                    expert_load(sp, m, io, r, n, n)
                for part in range(3 if nt > 2 else 0):
                    sp.wait_ge((sh_g, sh_u, sh_y)[part], (2, 2, nt)[part])
                    expert_load(sp, m, io, r, SHARED, SHARED, (part,))

            @block.gpsimd
            def _(pool):
                pool.sem_inc(r.hf_done, 2)
                pool.sem_inc(r.y_done, 2)
                pool.sem_inc(r.gu_done, 2)
                for half in r.y_out:
                    pool.sem_inc(half, 2)
                pool.sem_inc(r.pass_done, 1)
                pool.memset(empty[:], EMPTY).then_inc(empty_done, 1)
                pool.memset(ones[:], 1.0).then_inc(ones_done, 1)
                pool.memset(keep[:], 1.0).then_inc(keep_step, 1)
                pool.wait_ge(keep_step, 1)
                pool.memset(keep[:, :, 0:1], 0.0).then_inc(ones_done, 1)
                pool.memset(r.xg[:], 0.0).then_inc(cleared, 1)
                pool.wait_ge(m.router_in, CONSTS)
                pool.wait_ge(filled, 16)
                pool.wait_ge(row_done, 1)
                for k in range(TOPK):
                    for t in range(nt):
                        pool.indirect_dma_start(out=m.TAB, out_offset=bass.IndirectOffsetOnAxis(ap=row[:, k, t:t + 1], axis=0), in_=m.val[:, t * TOPK + k, :], in_offset=None,
                                                bounds_check=ROWS * NE - 1, oob_is_err=False, compute_op=ALU.bypass).then_inc(tabled, 16)
                pool.wait_ge(cleared, 1)
                pool.wait_ge(tabled, 16 * TOPK * nt)

            @block.scalar
            def _(act):
                if r.layer == 0:
                    act.wait_ge(m.late.stored, 16 * LATE)
                    ada_reload(act, m, len(BATCHES) - 1, m.late.reloaded)
                act.wait_ge(logits_done, 1)
                act.activation(lt[:], m.ps[0:NE, 0, 0:HT], ACT.Copy).then_inc(lt_out, 1)
                act.wait_ge(lt_turned, 1)
                act.activation(sc[:], m.ps[:, 7, 0:nt * NE].rearrange("p (t e) -> p t e", t=nt), ACT.Sigmoid).then_inc(scored, 1)
                for f in range(2):
                    act.wait_ge(sh_g, f + 1)
                    act.activation(shs[:, f, 0:HT], m.ps[:, 3 + 2 * f, 0:HT], ACT.Silu).then_inc(sh_s, 1)
                    act.wait_ge(sh_u, f + 1)
                    act.activation(shu[:, f, 0:HT], m.ps[:, 4 + 2 * f, 0:HT], ACT.Copy).then_inc(sh_c, 1)
                for t in range(nt):
                    act.wait_ge(sh_y, t + 1)
                    act.activation(m.hT[:].rearrange("p a b -> p (a b)")[:, t * D:(t + 1) * D], bank2(m, 4 + 2 * (t % 2)), ACT.Copy).then_inc(sh_out, 1)
                    if r.layer == 0 and t == 2:
                        act.wait_ge(m.late.row_done, 1)
                        ada_publish(act, m, len(BATCHES) - 1, m.late.published)
                if r.layer == 0:
                    act.wait_ge(m.late.published, 32)

            @block.tensor
            def _(pe):
                pe.wait_ge(m.router_in, CONSTS)
                for k in range(KC):
                    mm = pe.matmul(m.ps[0:NE, 0, 0:HT], m.rw[:, k, :], m.hT[:, k, 0:HT], start=(k == 0), stop=(k == KC - 1))
                mm.then_inc(logits_done, 1)
                pe.wait_ge(lt_out, 1)
                for t in range(nt):
                    mm = pe.transpose(m.ps[:, 7, t * NE:(t + 1) * NE], lt[:, t * P:(t + 1) * P], m.ident[0:NE, 0:NE])
                mm.then_inc(lt_turned, 1)

                def places():
                    pe.wait_ge(sel_done, 1)
                    pe.wait_ge(ones_done, 2)
                    for t in range(nt):
                        for q in range(t):
                            pe.matmul(m.ps[:, 1, t * NE:(t + 1) * NE], ones[:], selb[:, q, :], start=(q == 0), stop=False)
                        pe.matmul(m.ps[:, 1, t * NE:(t + 1) * NE], tri[:], selb[:, t, :], start=(t == 0), stop=True)
                    for t in range(nt):
                        mm = pe.matmul(m.ps[:, 2, 0:NE], ones[:], selb[:, t, :], start=(t == 0), stop=(t == nt - 1))
                    mm.then_inc(pos_done, 1)

                pe.wait_ge(m.sh_in, 48)
                for f in range(2):
                    for w, b, done in ((wg(m, SHARED), 3, sh_g), (wu(m, SHARED), 4, sh_u)):
                        for k in range(KC):
                            mm = pe.matmul(m.ps[:, b + 2 * f, 0:HT], w[:, k, f * P:(f + 1) * P], m.hT[:, k, 0:HT], start=(k == 0), stop=(k == KC - 1))
                        mm.then_inc(done, 1)
                        if f == 0 and done is sh_u:
                            places()

                pe.wait_ge(sh_h, 2)
                for t in range(nt):
                    if t >= 2:
                        pe.wait_ge(sh_out, t - 1)
                    for n in range(2):
                        for f in range(2):
                            mm = pe.matmul(m.ps[:, 4 + 2 * (t % 2) + n, :], shh[:, f, t * P:(t + 1) * P], wd(m, SHARED)[:, f, n * 512:n * 512 + 512], start=(f == 0), stop=(f == 1))
                    mm.then_inc(sh_y, 1)
                pe.wait_ge(sh_out, nt)

            @block.vector
            def _(dve):
                done = [0]

                def link(ins):
                    done[0] += 1
                    ins.then_inc(chain, 1)
                    dve.wait_ge(chain, done[0])

                def scan(src, out):
                    link(dve.tensor_tensor_scan(out.rearrange("p t e -> p (t e)"), keep[:].rearrange("p t e -> p (t e)"), src.rearrange("p t e -> p (t e)"),
                                                0.0, ALU.mult, ALU.add))

                dve.wait_ge(m.router_in, CONSTS)
                dve.wait_ge(ones_done, 2)
                link(dve.tensor_copy(tri[:], m.tri[:]))
                dve.wait_ge(scored, 1)
                link(dve.tensor_tensor(bi[:], sc[:], m.rb[:].unsqueeze(1).broadcast_to([P, nt, NE]), ALU.add))
                for t in range(nt):
                    for g in range(GROUPS):
                        last = dve.max(m8[:, t, g, :], bi[:, t, g * 8:(g + 1) * 8])
                link(last)
                link(dve.tensor_tensor(gs[:], m8[:, :, :, 0], m8[:, :, :, 1], ALU.add))
                other = gs[:].unsqueeze(2).broadcast_to([P, nt, GROUPS, GROUPS])
                own = gs[:].unsqueeze(3).broadcast_to([P, nt, GROUPS, GROUPS])
                dve.tensor_tensor(cmp1[:], other, own, ALU.is_gt)
                link(dve.tensor_tensor(cmp2[:], other, own, ALU.is_equal))
                link(dve.tensor_tensor(cmp2[:], cmp2[:], m.low[:].unsqueeze(1).broadcast_to([P, nt, GROUPS, GROUPS]), ALU.mult))
                link(dve.tensor_tensor(cmp1[:], cmp1[:], cmp2[:], ALU.add))
                link(dve.tensor_reduce(beat[:], cmp1[:], AX.X, ALU.add))
                link(dve.tensor_scalar(gm[:], beat[:], float(TOPG), None, ALU.is_lt))
                link(dve.tensor_scalar(neg[:], gm[:], -1.0, BIG, ALU.add, ALU.mult))
                bit = bi[:].rearrange("p t (g e) -> p (t g) e", g=GROUPS)
                for mask, op in ((gm, ALU.mult), (neg, ALU.add)):
                    link(dve.tensor_tensor(bit, bit, mask[:].rearrange("p t g -> p (t g)").unsqueeze(2).broadcast_to([P, nt * GROUPS, 8]), op))
                for t in range(nt):
                    last = dve.max(top[:, t, :], bi[:, t, :])
                link(last)
                sixth = top[:, :, TOPK - 1:TOPK].broadcast_to([P, nt, NE])
                dve.tensor_tensor(t1[:], bi[:], sixth, ALU.is_gt)
                link(dve.tensor_tensor(t2[:], bi[:], sixth, ALU.is_equal))
                link(dve.tensor_reduce(need[:], t1[:], AX.X, ALU.add))
                link(dve.tensor_scalar(need[:], need[:], -1.0, float(TOPK), ALU.mult, ALU.add))
                scan(t2[:], G[:])
                link(dve.tensor_tensor(G[:], G[:], need[:].unsqueeze(2).broadcast_to([P, nt, NE]), ALU.is_le))
                link(dve.tensor_tensor(t2[:], t2[:], G[:], ALU.mult))
                link(dve.tensor_tensor(sel[:], t1[:], t2[:], ALU.add))
                dve.tensor_copy(selb[:], sel[:]).then_inc(sel_done, 1)
                scan(sel[:], t1[:])
                link(dve.tensor_tensor(t1[:], t1[:], sel[:], ALU.mult))
                dve.wait_ge(pos_done, 1)
                link(dve.scalar_tensor_tensor(Q[:], m.ps[:, 1, 0:nt * NE].rearrange("p (t e) -> p t e", t=nt), float(NE),
                                              m.ecol[:].unsqueeze(1).broadcast_to([P, nt, NE]), ALU.mult, ALU.add))
                for k in range(TOPK):
                    last = dve.scalar_tensor_tensor(pick[:, k], t1[:], float(k + 1), Q[:], ALU.is_equal, ALU.mult)
                link(last)
                link(dve.tensor_reduce(rowf[:], pick[:], AX.X, ALU.add))
                link(dve.tensor_copy(row[:], rowf[:]))
                dve.sem_inc(row_done, 1)
                for f in range(2):
                    dve.wait_ge(sh_s, f + 1)
                    dve.wait_ge(sh_c, f + 1)
                    dve.tensor_tensor(shh[:, f, 0:HT], shs[:, f, 0:HT], shu[:, f, 0:HT], ALU.mult).then_inc(sh_h, 1)
                link(dve.tensor_tensor(G[:], sc[:], sel[:], ALU.mult))
                link(dve.tensor_reduce(v6[:], G[:], AX.X, ALU.add))
                link(dve.reciprocal(need[:], v6[:]))
                for t in range(nt):
                    last = dve.tensor_scalar(G[:, t, :], G[:, t, :], need[:, t:t + 1], RSCALE, ALU.mult, ALU.mult)
                link(last)
                for k in range(TOPK):
                    last = dve.scalar_tensor_tensor(pick[:, k], t1[:], float(k + 1), G[:], ALU.is_equal, ALU.mult)
                link(last)
                link(dve.tensor_reduce(r.gk[:, :, 0:TOPK].rearrange("p t k -> p k t"), pick[:], AX.X, ALU.add))
                link(dve.tensor_copy(cnt[:], m.ps[0:1, 2, 0:NE]))
                link(dve.tensor_copy(r.counts[:], cnt[:]))
                link(dve.tensor_reduce(mxc[:], cnt[:], AX.X, ALU.max))
                for i in range(4):
                    link(dve.tensor_scalar(ge[:, i:i + 1], mxc[:], float(P * i) if i else -1.0, None, ALU.is_gt))
                link(dve.tensor_reduce(npf[:], ge[:], AX.X, ALU.add))
                dve.tensor_copy(r.passes[:, 0:1], npf[:]).then_inc(route_done, 1)
                dve.wait_ge(route_done, 1)
                if r.layer == 0:
                    dve.wait_ge(m.late.reloaded, 32)
                    ada_rows(dve, m, len(BATCHES) - 1, m.late.biased, m.late.row_done, 1)


def experts(nc, m, io, r):
    nt, L, layer = r.nt, r.L, r.layer
    with ExitStack() as ctx:
        def sb(name, shape, dt=F32):
            return ctx.enter_context(nc.sbuf_tensor(f"{L}e_{name}", shape, dt))

        table = sb("table", [P, NE, 2], I32)
        ig, isc = sb("ig", [P, UNROLL], I32), sb("isc", [P, UNROLL], I32)
        xg = r.xg
        xT = sb("xT", [P, 2, KC, P])
        BLK = 32
        sl = sb("sl", [P, 2, 2 * P])
        hf = sb("hf", [P, 2, 2 * P])
        y = sb("y", [P, 2, D])

        q = m.sem
        w_in = r.w_in
        hf_done, y_done, gu_done, x_turned, y_out, pass_done = r.hf_done, r.y_done, r.gu_done, r.x_turned, r.y_out, r.pass_done
        scattered = [q(f"{L}e_scattered{i}") for i in range(2)]
        pool_steps = q(f"{L}e_pool_steps")
        pe_steps = q(f"{L}e_pe_steps")
        ig_done, is_done = q(f"{L}e_ig_done"), q(f"{L}e_is_done")
        gathered = [q(f"{L}e_gathered{s}") for s in range(UNROLL)]
        sl_done = q(f"{L}e_sl_done")
        dve_steps = q(f"{L}e_dve_steps")

        table_in = q(f"{L}e_table_in")
        GI = NE // UNROLL

        def g_is_first(g):
            return isinstance(g, int) and g == 0

        with nc.Block() as block:
            @block.sync
            def _(sp):
                if nt <= 2:
                    sp.wait_ge(gathered[0], 16)
                    expert_load(sp, m, io, r, SHARED, SHARED)
                npass = sp.value_load(r.passes[0:1, 0:1], min_val=1, max_val=4)
                with sp.Fori(1, npass * GI) as g:
                    for s in range(UNROLL):
                        sp.wait_ge(y_done, g * UNROLL + s - 1)
                        expert_load(sp, m, io, r, (g % GI) * UNROLL + s, s)

            @block.tensor
            def _(pe):
                npass = pe.value_load(r.passes[0:1, 0:1], min_val=1, max_val=4)
                with pe.Fori(0, npass) as b:
                    def up_rows(s, rows):
                        for c in range(4):
                            w = wg(m, s) if c < 2 else wu(m, s)
                            for k in range(KC):
                                mm = pe.matmul(m.ps[:, 2 + s % 2, c * P:c * P + rows], w[:, k, (c % 2) * P:(c % 2 + 1) * P], xT[:, s % 2, k, 0:rows],
                                               start=(k == 0), stop=(k == KC - 1))
                        mm.then_inc(gu_done, 1)

                    def by_size(n, work, s):
                        pe.sem_inc(pe_steps, 1)
                        count = pe.value_load(r.counts[0:1, bass.ds(at(n), 1)], min_val=0, max_val=ROWS)
                        with pe.If(count <= SMALL):
                            work(s, SMALL)
                        with pe.Else():
                            work(s, P)

                    def at(n):
                        return n if isinstance(n, int) else n[0] * UNROLL + n[1]

                    def up(n, s):
                        g = n // UNROLL if isinstance(n, int) else n[0]
                        pe.wait_ge(w_in[s], (b * GI + g + 1) * 48)
                        pe.wait_ge(x_turned, b * NE + at(n) + 1)
                        pe.wait_ge(hf_done, b * NE + at(n) + 1)
                        by_size(n, up_rows, s)

                    def down(n, s):
                        pe.wait_ge(hf_done, b * NE + at(n) + 3)
                        for half in y_out:
                            pe.wait_ge(half, b * NE + at(n) + 1)
                        for c in range(2):
                            for k in range(2):
                                mm = pe.matmul(m.ps[:, 4 + 2 * (s % 2) + c, :], hf[:, s % 2, k * P:(k + 1) * P], wd(m, s)[:, k, c * 512:c * 512 + 512], start=(k == 0), stop=(k == 1))
                        mm.then_inc(y_done, 1)

                    up(0, 0)
                    with pe.Fori(0, GI - 1) as i:
                        for s in range(UNROLL):
                            up((i + (s + 1) // UNROLL, (s + 1) % UNROLL), (s + 1) % UNROLL)
                            down((i, s), s)
                    for n in range(NE - UNROLL, NE):
                        if n + 1 < NE:
                            up(n + 1, (n + 1) % UNROLL)
                        down(n, n % UNROLL)

            @block.vector
            def _(dve):
                npass = dve.value_load(r.passes[0:1, 0:1], min_val=1, max_val=4)
                with dve.Fori(0, npass) as b:
                    dve.wait_ge(pass_done, b + 1)

                    def turn_rows(s, rows):
                        for t in range(rows // BLK):
                            for p in range(P // BLK):
                                last = dve.transpose(xT[p * BLK:(p + 1) * BLK, s % 2, :, t * BLK:(t + 1) * BLK],
                                                     xg[t * BLK:(t + 1) * BLK, s, :].rearrange("t (k p) -> t k p", p=P)[:, :, p * BLK:(p + 1) * BLK])
                        last.then_inc(x_turned, 1)

                    def turn(g, s):
                        dve.wait_ge(gathered[s], (b * GI + g + 1) * 16)
                        dve.wait_ge(gu_done, b * NE + g * UNROLL + s + 1)
                        dve.sem_inc(dve_steps, 1)
                        count = dve.value_load(r.counts[0:1, bass.ds(g * UNROLL + s, 1)], min_val=0, max_val=ROWS)
                        with dve.If(count <= SMALL):
                            turn_rows(s, SMALL)
                        with dve.Else():
                            turn_rows(s, P)

                    def hidden(g, s):
                        dve.wait_ge(sl_done, b * NE + g * UNROLL + s + 1)
                        dve.wait_ge(y_done, b * NE + g * UNROLL + s + 1)
                        dve.tensor_tensor(hf[:, s % 2, :], sl[:, s % 2, :], m.ps[:, 2 + s % 2, 2 * P:4 * P], ALU.mult).then_inc(hf_done, 1)

                    def y_copy(g, s):
                        dve.wait_ge(y_done, b * NE + g * UNROLL + s + 3)
                        if not (g_is_first(g) and s < 2):
                            dve.wait_ge(scattered[s % 2], (b * (NE // 2) + g * 2 + s // 2) * 16)
                        dve.tensor_copy(y[:, s % 2, 512:1024], m.ps[:, 5 + 2 * (s % 2), :]).then_inc(y_out[1], 1)

                    turn(0, 0)
                    turn(0, 1)
                    hidden(0, 0)

                    def group(g):
                        for s in range(UNROLL):
                            turn(g + (s + 2) // UNROLL, (s + 2) % UNROLL)
                            hidden(g + (s + 1) // UNROLL, (s + 1) % UNROLL)
                            y_copy(g, s)

                    group(0)
                    with dve.Fori(1, GI - 1) as i:
                        group(i)
                    for s in range(UNROLL):
                        if s + 2 < UNROLL:
                            turn(GI - 1, s + 2)
                        if s + 1 < UNROLL:
                            hidden(GI - 1, s + 1)
                        y_copy(GI - 1, s)

            @block.scalar
            def _(act):
                npass = act.value_load(r.passes[0:1, 0:1], min_val=1, max_val=4)
                with act.Fori(0, npass) as b:
                    def gate(g, s):
                        act.wait_ge(gu_done, b * NE + g * UNROLL + s + 3)
                        act.wait_ge(hf_done, b * NE + g * UNROLL + s + 1)
                        act.activation(sl[:, s % 2, :], m.ps[:, 2 + s % 2, 0:2 * P], ACT.Silu).then_inc(sl_done, 1)

                    def y_copy(g, s):
                        act.wait_ge(y_done, b * NE + g * UNROLL + s + 3)
                        if not (g_is_first(g) and s < 2):
                            act.wait_ge(scattered[s % 2], (b * (NE // 2) + g * 2 + s // 2) * 16)
                        act.activation(y[:, s % 2, 0:512], m.ps[:, 4 + 2 * (s % 2), :], ACT.Copy).then_inc(y_out[0], 1)

                    act.wait_ge(pass_done, b + 1)
                    act.dma_start(table[:], m.TAB.rearrange("(b p e) c -> b p e c", p=P, e=NE)[b]).then_inc(table_in, 16)
                    gate(0, 0)

                    def group(g):
                        for s in range(UNROLL):
                            gate(g + (s + 1) // UNROLL, (s + 1) % UNROLL)
                            y_copy(g, s)

                    group(0)
                    with act.Fori(1, GI - 1) as i:
                        group(i)
                    for s in range(UNROLL):
                        if s + 1 < UNROLL:
                            gate(GI - 1, s + 1)
                        y_copy(GI - 1, s)

            @block.gpsimd
            def _(pool):
                npass = pool.value_load(r.passes[0:1, 0:1], min_val=1, max_val=4)
                with pool.Fori(0, npass) as b:
                    pool.wait_ge(table_in, b * 16 + 16)

                    def gather_rows(s, rows):
                        pool.indirect_dma_start(out=xg[0:rows, s, :], out_offset=None, in_=m.H2, in_offset=bass.IndirectOffsetOnAxis(ap=ig[0:rows, s:s + 1], axis=0),
                                                bounds_check=ROWS - 1, oob_is_err=False, compute_op=ALU.bypass).then_inc(gathered[s], 16)

                    def scatter_rows(s, rows):
                        pool.indirect_dma_start(out=m.Y6, out_offset=bass.IndirectOffsetOnAxis(ap=isc[0:rows, s:s + 1], axis=0), in_=y[0:rows, s % 2, :], in_offset=None,
                                                bounds_check=TOPK * ROWS - 1, oob_is_err=False, compute_op=ALU.bypass).then_inc(scattered[s % 2], 16)

                    def by_size(g, s, work):
                        count = pool.value_load(r.counts[0:1, bass.ds(g * UNROLL + s, 1)], min_val=0, max_val=ROWS)
                        with pool.If(count <= SMALL // 2):
                            work(s, SMALL // 2)
                        with pool.Else():
                            with pool.If(count <= SMALL):
                                work(s, SMALL)
                            with pool.Else():
                                with pool.If(count <= SMALL + SMALL // 2):
                                    work(s, SMALL + SMALL // 2)
                                with pool.Else():
                                    work(s, P)

                    def gather(g, s):
                        if not g_is_first(g):
                            pool.wait_ge(x_turned, b * NE + g * UNROLL + s + 1 - UNROLL)
                        pool.sem_inc(pool_steps, 1)
                        pool.tensor_copy(ig[:, s:s + 1], table[:, bass.ds(g * UNROLL + s, 1), 0]).then_inc(ig_done, 1)
                        pool.wait_ge(ig_done, b * NE + g * UNROLL + s + 1)
                        pool.sem_inc(pool_steps, 1)
                        by_size(g, s, gather_rows)

                    def scatter(g, s):
                        for half in y_out:
                            pool.wait_ge(half, b * NE + g * UNROLL + s + 3)
                        pool.sem_inc(pool_steps, 1)
                        pool.tensor_copy(isc[:, s:s + 1], table[:, bass.ds(g * UNROLL + s, 1), 1]).then_inc(is_done, 1)
                        pool.wait_ge(is_done, b * NE + g * UNROLL + s + 1)
                        pool.sem_inc(pool_steps, 1)
                        by_size(g, s, scatter_rows)

                    for s in range(UNROLL):
                        gather(0, s)
                    scatter(0, 0)
                    with pool.Fori(1, GI) as i:
                        for s in range(UNROLL):
                            gather(i, s)
                            if s < UNROLL - 1:
                                scatter(i - 1, s + 1)
                            else:
                                scatter(i, 0)
                    for s in range(1, UNROLL):
                        scatter(GI - 1, s)
                    for i in range(2):
                        pool.wait_ge(scattered[i], (b * (NE // 2) + NE // 2) * 16)
                    pool.sem_inc(pass_done, 1)


def combine(nc, m, io, r):
    nt, L = r.nt, r.L
    last_layer = r.layer == 1
    with ExitStack() as ctx:
        def sb(name, shape, dt=F32):
            return ctx.enter_context(nc.sbuf_tensor(f"{L}c_{name}", shape, dt))

        SLOTS = 3
        rows = [m.W[:, i, :].rearrange("p (k d) -> p k d", k=TOPK) for i in (0, 1, 3)]
        G = sb("G", [P, 2, D])
        junk = sb("junk", [P, D])
        xjunk = sb("xjunk", [P, D])
        ssq, std, rstd = (sb(n, [P, nt]) for n in ("ssq", "std", "rstd"))
        q = m.sem
        gate_in = q(f"{L}c_gate_in")
        rows_in = [[q(f"{L}c_rows_in{i}_{k}") for k in range(TOPK // 2)] for i in range(SLOTS)]
        added, summed, squared, std_done, rec_done, scaled, x_done, x_sq, stored = (
            q(f"{L}c_{n}") for n in ("added", "summed", "squared", "std_done", "rec_done", "scaled", "x_done", "x_sq", "stored"))
        shared = m.hT[:].rearrange("p a b -> p (a b)")
        streams = 2 if nt > 2 else 1
        if not last_layer:
            m.rows_in = q("m10_rows_in")

        with nc.Block() as block:
            @block.sync
            def _(sp):
                for t in range(nt):
                    if t >= SLOTS:
                        sp.wait_ge(summed, t - SLOTS + 1)
                    for k in range(0, TOPK, 2):
                        sp.dma_start(rows[t % SLOTS][:, k:k + 2, :], m.Y6.rearrange("(k t) d -> t k d", k=TOPK)[t * P:(t + 1) * P, k:k + 2]).then_inc(rows_in[t % SLOTS][k // 2], 16)
                    if t == 0:
                        for s in range(streams):
                            sp.dma_start(G[:, s, :], m.MOD[r.layer, 5, s, :].partition_broadcast(P)).then_inc(gate_in, 16)
                if last_layer:
                    for t in range(nt):
                        sp.wait_ge(x_done, t + 1)
                        sp.dma_start(io["out"][0, t * P:(t + 1) * P, :], m.X[:, t, :]).then_inc(stored, 16)
                    sp.wait_ge(stored, 16 * nt)
                else:
                    norm_rows_load(sp, m, 1, 0, 2, m.rows_in)

            @block.vector
            def _(dve):
                def finish(t):
                    acc = shared[:, t * D:(t + 1) * D]
                    dve.wait_ge(std_done, t + 1)
                    dve.reciprocal(rstd[:, t:t + 1], std[:, t:t + 1]).then_inc(rec_done, 1)
                    dve.wait_ge(rec_done, t + 1)
                    dve.scalar_tensor_tensor(acc, acc, rstd[:, t:t + 1], G[:, t // 2, :], ALU.mult, ALU.mult).then_inc(scaled, 1)
                    dve.wait_ge(scaled, t + 1)
                    dve.tensor_tensor(m.X[:, t, :], m.X[:, t, :], acc, ALU.add).then_inc(x_done, 1)

                n = 0
                for t in range(nt):
                    acc = shared[:, t * D:(t + 1) * D]
                    for k in range(TOPK):
                        dve.wait_ge(rows_in[t % SLOTS][k // 2], 16 * (t // SLOTS + 1))
                        last = dve.scalar_tensor_tensor(acc, rows[t % SLOTS][:, k, :], r.gk[:, t, k:k + 1], acc, ALU.mult, ALU.add)
                        if k < TOPK - 1:
                            last.then_inc(added, 1)
                            n += 1
                            dve.wait_ge(added, n)
                        else:
                            last.then_inc(summed, 1)
                    if t == 0:
                        dve.wait_ge(gate_in, 16 * streams)
                    else:
                        finish(t - 1)
                finish(nt - 1)

            @block.scalar
            def _(act):
                def x_square(t):
                    act.wait_ge(x_done, t + 1)
                    if t:
                        act.wait_ge(x_sq, t)
                    act.activation(xjunk[:], m.X[:, t, :], ACT.Square, accum_out=m.ssq[:, t:t + 1]).then_inc(x_sq, 1)

                for t in range(nt):
                    act.wait_ge(summed, t + 1)
                    if t:
                        act.wait_ge(squared, t)
                    act.activation(junk[:], shared[:, t * D:(t + 1) * D], ACT.Square, accum_out=ssq[:, t:t + 1]).then_inc(squared, 1)
                    act.wait_ge(squared, t + 1)
                    act.activation(std[:, t:t + 1], ssq[:, t:t + 1], ACT.Sqrt, bias=m.eps[:], scale=1.0 / D).then_inc(std_done, 1)
                    if t and not last_layer:
                        x_square(t - 1)
                if not last_layer:
                    x_square(nt - 1)


def build(nc, io, stop=99):
    m = Memory()
    with ExitStack() as ctx:
        start(nc, ctx, m)
        route_buffers(nc, ctx, m)
        first = ctx.enter_context(ExitStack())
        modulation_buffers(nc, first, m)
        steps = [
            lambda: conditioning(nc, m, io),
            lambda: modulate(nc, m, io, "m00", 0, 0, range(4), False, mixer_first(m, io)),
            lambda: mixer(nc, m, io),
            lambda: modulate(nc, m, io, "m01", 0, 1, range(4), True, shared_weights(m, io, 0), late=True),
            lambda: moe(nc, m, io, 0, 4),
            lambda: modulate(nc, m, io, "m10", 1, 0, range(4), False, attention_weights(m, io)),
            lambda: attention(nc, m, io),
            lambda: modulate(nc, m, io, "m11", 1, 1, range(2), True, shared_weights(m, io, 1)),
            lambda: moe(nc, m, io, 1, 2),
        ]
        for n, step in enumerate(steps[:stop]):
            step()
            if n == 4:
                first.close()


def _constants():
    f = np.float32
    k = {}
    k["k_ident"] = np.eye(P, dtype=f)
    k["k_one"] = np.zeros((P, len(BATCHES)), f)
    for b, (_, v0, nv) in enumerate(BATCHES):
        for s in range(2):
            for v in range(nv):
                k["k_one"][(s * nv + v) * 8:(s * nv + v + 1) * 8, b] = 1.0 if v0 + v in (1, 4) else 0.0

    def dft(n):
        a = 2 * np.pi * (np.outer(np.arange(n), np.arange(n)) % n) / n
        return np.cos(a) / np.sqrt(n), np.sin(a) / np.sqrt(n)

    c, s = dft(P)
    k["k_fch"] = np.concatenate([c, s], 1).astype(f)
    c, s = dft(SEQ)
    k["k_fseq"] = np.concatenate([c, -s], 1).reshape(2, P, 2 * SEQ).transpose(1, 0, 2).astype(f)
    k["k_gmean"] = (np.kron(np.eye(P // CONV_GROUP), np.ones((CONV_GROUP, CONV_GROUP))) / CONV_GROUP).astype(f)
    grid = 64
    tok = np.arange(SEQ)
    n_freq = QK // 4
    inv = np.power(f(10000.0), -np.arange(n_freq, dtype=f) / f(n_freq)).astype(f)
    ang = np.concatenate([(tok // grid).astype(f)[:, None] * inv, (tok % grid).astype(f)[:, None] * inv], -1)
    ang = np.concatenate([ang, ang, ang, ang], -1).T
    k["k_cos"], k["k_sin"] = np.cos(ang).astype(f), np.sin(ang).astype(f)
    r = np.zeros((QK, QK), f)
    h = QK // 2
    for i in range(h):
        r[i + h, i] = -1.0
        r[i, i + h] = 1.0
    k["k_rot"] = np.kron(np.eye(2, dtype=f), r).astype(f)
    k["k_tri"] = np.triu(np.ones((P, P), f), 1)
    k["k_low"] = np.tril(np.ones((GROUPS, GROUPS), f), -1)
    k["k_ecol"] = np.arange(NE, dtype=f)
    token = np.arange(P)[:, None, None] + P * np.arange(TT)[None, :, None]
    rank = np.arange(TOPK)[None, None, :]
    k["k_val"] = np.stack([token + 0 * rank, token + ROWS * rank], -1).reshape(P, TT * TOPK, 2).astype(np.int32)
    return k


_INS = ["x", "c", "ctx", "c_ctx", "ada_w", "ada_b", "norm_g", "cf_w_in", "cf_conv_w", "cf_conv_b", "cf_ln_g", "cf_ln_b", "cf_w_out",
        "da_w_qkv", "da_lambda", "da_subln_g", "da_w_out", "moe_router_w", "moe_router_b", "moe_w_gate", "moe_w_up", "moe_w_down",
        "moe_sh_gate", "moe_sh_up", "moe_sh_down"]


def kernel(**inputs):
    import concourse.bacc as _bacc
    from concourse.bass_utils import run_bass_kernel_spmd as _run

    nc = _bacc.Bacc("TRN2", target_bir_lowering=False, num_devices=1)
    arrays, io = {}, {}
    data = {n: np.ascontiguousarray(inputs[n]) for n in _INS} | _constants()
    for name, a in data.items():
        a = np.ascontiguousarray(a)
        arrays[f"in_{name}"] = a
        io[name] = nc.dram_tensor(f"in_{name}", a.shape, mybir.dt.from_np(a.dtype), kind="ExternalInput").ap()
    io["out"] = nc.dram_tensor("out_x", (1, SEQ, D), F32, kind="ExternalOutput").ap()
    build(nc, io)
    r = _run(nc, [arrays], core_ids=[0])
    return r.results[0]["out_x"]
```
